# Optimizing a Trainium2 kernel written in Bass

```python
import jax, jax.numpy as jnp
from jax import lax
import numpy as np

D_MODEL = 1024
BATCH = 1
SEQ = 1024
DEPTH = 1
DEC_BATCH = 1
DEC_SEQ = 512
PAST_LEN = 128

ATTN_WIDTH = D_MODEL // 2
CONV_WIDTH = D_MODEL - ATTN_WIDTH
HEAD_DIM = 64
N_HEADS = ATTN_WIDTH // HEAD_DIM
N_KV_HEADS = 2
KV_GROUP = N_HEADS // N_KV_HEADS
KV_WIDTH = N_KV_HEADS * HEAD_DIM
IN_WIDTH = ATTN_WIDTH + 2 * KV_WIDTH + 2 * CONV_WIDTH
CONV_K = 31
GRID_W = 64
ROPE_THETA = 10000.0
AXIS_DIM = HEAD_DIM // 2
Q_BLOCK = 128
N_EXPERTS = 16
EXPERT_FF = 2 * D_MODEL
CAPACITY_FACTOR = 2
EPS = 1e-6

kernel_name = "hymba_attn_conformer_ec_moe_encoder"

def rms_norm(x, g):
    xf = x.astype(jnp.float32)
    y = xf * lax.rsqrt(jnp.mean(xf * xf, axis=-1, keepdims=True) + EPS)
    return (y * g.astype(jnp.float32)).astype(x.dtype)

def layer_norm(x, g, b):
    xf = x.astype(jnp.float32)
    mu = jnp.mean(xf, axis=-1, keepdims=True)
    xc = xf - mu
    y = xc * lax.rsqrt(jnp.mean(xc * xc, axis=-1, keepdims=True) + EPS)
    return (y * g.astype(jnp.float32) + b.astype(jnp.float32)).astype(x.dtype)

def axial_rope(n_tokens):
    rows = n_tokens // GRID_W
    row = jnp.repeat(jnp.arange(rows, dtype=jnp.float32), GRID_W)
    col = jnp.tile(jnp.arange(GRID_W, dtype=jnp.float32), rows)
    inv_freq = ROPE_THETA ** (-jnp.arange(0, AXIS_DIM, 2, dtype=jnp.float32) / AXIS_DIM)
    ang = jnp.concatenate([row[:, None] * inv_freq, col[:, None] * inv_freq], axis=-1)
    return jnp.cos(ang), jnp.sin(ang)

def apply_rope(x, cos, sin):
    xf = x.astype(jnp.float32).reshape(x.shape[:-1] + (HEAD_DIM // 2, 2))
    x0, x1 = xf[..., 0], xf[..., 1]
    c = cos[None, :, None, :]
    s = sin[None, :, None, :]
    out = jnp.stack([x0 * c - x1 * s, x0 * s + x1 * c], axis=-1).reshape(x.shape)
    return out.astype(x.dtype)

def blocked_attention(q, k, v):
    B, S, H, Dh = q.shape
    nb = S // Q_BLOCK
    qb = q.reshape(B, nb, Q_BLOCK, N_KV_HEADS, KV_GROUP, Dh).transpose(1, 0, 2, 3, 4, 5)
    scale = HEAD_DIM ** -0.5

    def one_block(qblk):
        s = jnp.einsum('bqkgd,bskd->bkgqs', qblk, k, preferred_element_type=jnp.float32) * scale
        p = jax.nn.softmax(s, axis=-1)
        return jnp.einsum('bkgqs,bskd->bqkgd', p.astype(v.dtype), v)

    o = lax.map(one_block, qb)
    return o.transpose(1, 0, 2, 3, 4, 5).reshape(B, S, H * Dh)

def conformer_conv(cv, cg, dw_w, dw_b, ln_g, ln_b):
    u = cv * jax.nn.sigmoid(cg)
    u = lax.conv_general_dilated(
        u, dw_w[:, None, :].astype(u.dtype), window_strides=(1,),
        padding=[(CONV_K // 2, CONV_K // 2)],
        dimension_numbers=('NWC', 'WIO', 'NWC'),
        feature_group_count=CONV_WIDTH) + dw_b.astype(u.dtype)
    u = layer_norm(u, ln_g, ln_b)
    return jax.nn.silu(u)

def expert_choice_ffn(h, w_router, w_gate, w_up, w_down):
    B, S, D = h.shape
    n = B * S
    cap = CAPACITY_FACTOR * n // N_EXPERTS
    hf = h.reshape(n, D)
    logits = jnp.einsum('nd,de->en', hf, w_router, preferred_element_type=jnp.float32)
    aff = jax.nn.softmax(logits, axis=0)
    gate, idx = lax.top_k(aff, cap)
    xg = hf[idx]
    a = jnp.einsum('ecd,edf->ecf', xg, w_gate)
    b = jnp.einsum('ecd,edf->ecf', xg, w_up)
    out = jnp.einsum('ecf,efd->ecd', jax.nn.silu(a) * b, w_down) * gate[..., None].astype(h.dtype)
    y = jnp.zeros_like(hf).at[idx.reshape(-1)].add(out.reshape(-1, D))
    return y.reshape(B, S, D)

def encoder_layer(x, cos, sin, attn_norm_g, w_in, q_norm_g, k_norm_g, conv_dw_w, conv_dw_b,
                  conv_ln_g, conv_ln_b, attn_out_g, conv_out_g, w_out, ffn_norm_g,
                  w_router, w_gate, w_up, w_down):
    B, S, _ = x.shape
    h = rms_norm(x, attn_norm_g)
    proj = h @ w_in
    q, k, v, cv, cg = jnp.split(proj, [ATTN_WIDTH, ATTN_WIDTH + KV_WIDTH, ATTN_WIDTH + 2 * KV_WIDTH,
                                       ATTN_WIDTH + 2 * KV_WIDTH + CONV_WIDTH], axis=-1)
    q = q.reshape(B, S, N_HEADS, HEAD_DIM)
    k = k.reshape(B, S, N_KV_HEADS, HEAD_DIM)
    v = v.reshape(B, S, N_KV_HEADS, HEAD_DIM)
    q = apply_rope(rms_norm(q, q_norm_g), cos, sin)
    k = apply_rope(rms_norm(k, k_norm_g), cos, sin)
    attn = blocked_attention(q, k, v)
    conv = conformer_conv(cv, cg, conv_dw_w, conv_dw_b, conv_ln_g, conv_ln_b)
    mixed = jnp.concatenate([rms_norm(attn, attn_out_g), rms_norm(conv, conv_out_g)], axis=-1)
    x = x + mixed @ w_out
    x = x + expert_choice_ffn(rms_norm(x, ffn_norm_g), w_router, w_gate, w_up, w_down)
    return x

def encoder_trunk(x, attn_norm_g, w_in, q_norm_g, k_norm_g, conv_dw_w, conv_dw_b, conv_ln_g,
                  conv_ln_b, attn_out_g, conv_out_g, w_out, ffn_norm_g, w_router, w_gate, w_up, w_down):
    cos, sin = axial_rope(x.shape[1])
    for l in range(DEPTH):
        x = encoder_layer(x, cos, sin, attn_norm_g[l], w_in[l], q_norm_g[l], k_norm_g[l],
                          conv_dw_w[l], conv_dw_b[l], conv_ln_g[l], conv_ln_b[l],
                          attn_out_g[l], conv_out_g[l], w_out[l], ffn_norm_g[l],
                          w_router[l], w_gate[l], w_up[l], w_down[l])
    return x

def setup_inputs(seed: int = 0) -> dict:
    key = jax.random.key(seed)
    ks = jax.random.split(key, 20)
    f32 = jnp.float32

    def nrm(k, shape, scale):
        return jax.random.normal(k, shape, f32) * scale

    def gain(k, shape):
        return 1.0 + 0.02 * jax.random.normal(k, shape, f32)

    return {
        "x_prompt": nrm(ks[0], (BATCH, SEQ, D_MODEL), 1.0),
        "x_sample": nrm(ks[1], (DEC_BATCH, DEC_SEQ, D_MODEL), 1.0),
        "attn_norm_g": gain(ks[2], (DEPTH, D_MODEL)),
        "w_in": nrm(ks[3], (DEPTH, D_MODEL, IN_WIDTH), D_MODEL ** -0.5),
        "q_norm_g": gain(ks[4], (DEPTH, HEAD_DIM)),
        "k_norm_g": gain(ks[5], (DEPTH, HEAD_DIM)),
        "conv_dw_w": nrm(ks[6], (DEPTH, CONV_K, CONV_WIDTH), CONV_K ** -0.5),
        "conv_dw_b": nrm(ks[7], (DEPTH, CONV_WIDTH), 0.02),
        "conv_ln_g": gain(ks[8], (DEPTH, CONV_WIDTH)),
        "conv_ln_b": nrm(ks[9], (DEPTH, CONV_WIDTH), 0.02),
        "attn_out_g": gain(ks[10], (DEPTH, ATTN_WIDTH)),
        "conv_out_g": gain(ks[11], (DEPTH, CONV_WIDTH)),
        "w_out": nrm(ks[12], (DEPTH, D_MODEL, D_MODEL), D_MODEL ** -0.5),
        "ffn_norm_g": gain(ks[13], (DEPTH, D_MODEL)),
        "w_router": nrm(ks[14], (DEPTH, D_MODEL, N_EXPERTS), D_MODEL ** -0.5),
        "w_gate": nrm(ks[15], (DEPTH, N_EXPERTS, D_MODEL, EXPERT_FF), D_MODEL ** -0.5),
        "w_up": nrm(ks[16], (DEPTH, N_EXPERTS, D_MODEL, EXPERT_FF), D_MODEL ** -0.5),
        "w_down": nrm(ks[17], (DEPTH, N_EXPERTS, EXPERT_FF, D_MODEL), EXPERT_FF ** -0.5),
    }

def reference(x_prompt, x_sample, attn_norm_g, w_in, q_norm_g, k_norm_g, conv_dw_w, conv_dw_b,
              conv_ln_g, conv_ln_b, attn_out_g, conv_out_g, w_out, ffn_norm_g, w_router,
              w_gate, w_up, w_down):
    y_prompt = encoder_trunk(x_prompt, attn_norm_g, w_in, q_norm_g, k_norm_g, conv_dw_w, conv_dw_b,
                             conv_ln_g, conv_ln_b, attn_out_g, conv_out_g, w_out, ffn_norm_g,
                             w_router, w_gate, w_up, w_down)
    y_sample = encoder_trunk(x_sample, attn_norm_g, w_in, q_norm_g, k_norm_g, conv_dw_w, conv_dw_b,
                             conv_ln_g, conv_ln_b, attn_out_g, conv_out_g, w_out, ffn_norm_g,
                             w_router, w_gate, w_up, w_down)
    return (y_prompt, y_sample)


_drawn_inputs = setup_inputs


def setup_inputs(seed=0):
    import zlib

    import numpy as np

    out = dict(_drawn_inputs(seed))
    spreads = {}
    factors = {'q_norm_g': 4.269,
     'k_norm_g': 3.853,
     'conv_ln_g': 4.043,
     'conv_ln_b': 4.695,
     'attn_out_g': 4.389,
     'conv_out_g': 4.23,
     'ffn_norm_g': 4.272}
    for name, (base, spread) in spreads.items():
        noise = np.random.default_rng([zlib.crc32(name.encode()), seed]).standard_normal(out[name].shape)
        drawn = base * np.exp(spread * noise) if base else spread * noise
        out[name] = __import__('jax').numpy.asarray(drawn.astype(out[name].dtype))
    for name, factor in factors.items():
        out[name] = (out[name] * factor).astype(out[name].dtype)
    return out
```

```python
from contextlib import ExitStack

import concourse.bass as bass
from concourse import mybir
import numpy as np

F32 = mybir.dt.float32
F32R = mybir.dt.float32r
U32 = mybir.dt.uint32
ALU = mybir.AluOpType
ACT = mybir.ActivationFunctionType
AX_X = mybir.AxisListType.X

P = 128
D = 1024
KD = D // P
N_PROMPT, N_SAMPLE = 1024, 512
TILES = (N_PROMPT + N_SAMPLE) // P
HD = 64
NH, NKV = 8, 2
AW = NH * HD
CW = D - AW
NC_CONV = CW // P
CONV_K = 31
PAD = CONV_K // 2
ROT_TILES = N_PROMPT // P
EPS = 1e-6
NE = 16
FF = 2 * D
CAP_P, CAP_S = 2 * N_PROMPT // NE, 2 * N_SAMPLE // NE
CAP = CAP_P + CAP_S

GROUPS = [(0, N_PROMPT // P, N_PROMPT, 0), (N_PROMPT // P, N_SAMPLE // P, N_SAMPLE, N_PROMPT + 2 * PAD)]
SLOT = N_PROMPT + N_SAMPLE + 4 * PAD
CHUNKS = 7
CCOLS = 256
SEL_ROWS = 48
SAMPLE_ROW = 32

COL_NORM, COL_TAP, COL_BIAS = 0, KD, KD + NC_CONV * CONV_K
COLS = COL_BIAS + NC_CONV
ROW_Q, ROW_K, ROW_LNG, ROW_LNB, ROW_MIX, ROW_FFN = 0, 2 * HD, 4 * HD, 4 * HD + CW, 4 * HD + 2 * CW, 4 * HD + 2 * CW + D
ROWS = ROW_FFN + D

EC = 24
CH = 2048
RAW_SLOTS, SPLIT_SLOTS = 4, 3
PAIRS = 8
TURN = 8


def encoder_layer_kernel(nc, x_prompt, x_sample, w_in, w_out, w_router, w_gate, w_up, w_down,
                         cols, rows, rotary, ident_in, y_prompt, y_sample):
    h_rows = nc.dram_tensor("h_rows", [N_PROMPT + N_SAMPLE, D], F32).ap()
    wi = w_in.rearrange("l (k p) n -> p (l k) n", p=P)
    wo = w_out.rearrange("l (k p) n -> p (l k) n", p=P)
    wr = w_router.rearrange("l (k p) n -> p (l k) n", p=P)
    gate_cols = w_gate.rearrange("l e (k p) f -> (l e) p k f", p=P)
    up_cols = w_up.rearrange("l e (k p) f -> (l e) p k f", p=P)
    down_rows = w_down.rearrange("l e (j k p) d -> (l e) j p k d", p=P, k=2)

    def x_rows(t):
        src, i = (x_prompt, t) if t < ROT_TILES else (x_sample, t - ROT_TILES)
        return src[0, i * P:(i + 1) * P, :]

    def y_rows(t):
        dst, i = (y_prompt, t) if t < ROT_TILES else (y_sample, t - ROT_TILES)
        return dst[0, i * P:(i + 1) * P, :]

    with ExitStack() as ctx:
        def sem(name):
            return ctx.enter_context(nc.semaphore(name))

        def in_region(stack, name, shape, dt):
            return stack.enter_context(nc.sbuf_tensor(name, shape, dt))

        psum = ctx.enter_context(nc.psum_tensor("psum", [P, 8, 512], F32))

        ident = in_region(ctx, "ident", [P, P], F32)
        colp = in_region(ctx, "colp", [P, COLS], F32)
        conv = in_region(ctx, "conv", [P, NC_CONV + 1, SLOT], F32)
        tok = in_region(ctx, "tok", [P, TILES, AW], F32)
        stat = in_region(ctx, "stat", [P, TILES, 16], F32)
        aff = in_region(ctx, "aff", [SEL_ROWS, N_PROMPT], F32)
        top = in_region(ctx, "top", [SEL_ROWS, CAP_P], F32)
        topi = in_region(ctx, "topi", [SEL_ROWS, CAP_P], U32)
        topf = in_region(ctx, "topf", [SEL_ROWS, CAP_P], F32)
        gates = in_region(ctx, "gates", [P, SEL_ROWS], F32)
        rows_p = in_region(ctx, "rows_p", [P, NE], U32)
        rows_s = in_region(ctx, "rows_s", [CAP_S, NE], U32)
        rows_sg = in_region(ctx, "rows_sg", [CAP_S, NE], U32)

        with ExitStack() as region:
            k_tok = in_region(region, "k_tok", [P, TILES, NKV * HD], F32)
            val = in_region(region, "val", [P, TILES, NKV, 2 * HD], F32R)
            with ExitStack() as ra:
                hT_hi = in_region(ra, "hT_hi", [P, KD, N_PROMPT], F32R)
                hT_lo = in_region(ra, "hT_lo", [P, KD, N_PROMPT], F32R)
                wi_raw = in_region(ra, "wi_raw", [P, 2, KD // 2, CCOLS], F32)
                wi_hi = in_region(ra, "wi_hi", [P, 2, KD, CCOLS], F32R)
                wi_lo = in_region(ra, "wi_lo", [P, 2, KD, CCOLS], F32R)
                xin = in_region(ra, "xin", [P, 2, D], F32)
                rot_c = in_region(ra, "rot_c", [P, 2, ROT_TILES, HD], F32)
                rot_s = in_region(ra, "rot_s", [P, 2, ROT_TILES, HD], F32)
                qn = in_region(ra, "qn", [P, 2, CCOLS], F32)
                q_turn = in_region(ra, "q_turn", [P, CCOLS], F32)
                sq = in_region(ra, "sq", [P, CCOLS], F32)
                sig_a = in_region(ra, "sig_a", [P, 512], F32)
                hstat = in_region(ra, "hstat", [P, 2, 3, 4], F32)
            rot_src = tok[:, 0:2, :].rearrange("p a b -> p (a b)").rearrange("p (x t d) -> p x t d", x=2, d=HD)
            rope_gain = tok[:, 2, 0:4 * HD]
            with ExitStack() as rb:
                q_st = in_region(rb, "q_st", [P, NH, TILES * P], F32R)
                k_st = in_region(rb, "k_st", [P, NKV, 2, TILES * P], F32R)
                probs = in_region(rb, "probs", [P, 2, N_PROMPT], F32)
                pT_hi = in_region(rb, "pT_hi", [P, 2, N_PROMPT], F32R)
                pT_lo = in_region(rb, "pT_lo", [P, 2, N_PROMPT], F32R)
                q_split = in_region(rb, "q_split", [P, NH, 2 * HD], F32)
                k_split = in_region(rb, "k_split", [P, NKV, 2, 2 * HD], F32)
                smx = in_region(rb, "smx", [P, 3, TILES * NH], F32)
                osum = in_region(rb, "osum", [P, 2, HD], F32)
        with ExitStack() as rc:
            wo_hi = in_region(rc, "wo_hi", [P, KD, D], F32R)
            wo_lo = in_region(rc, "wo_lo", [P, KD, D], F32R)
            rowp = in_region(rc, "rowp", [P, ROWS - ROW_LNG], F32)
            wo_raw = in_region(rc, "wo_raw", [P, 2, D], F32)
            wr_sb = in_region(rc, "wr_sb", [P, KD, NE], F32)
            cn = in_region(rc, "cn", [P, CW], F32)
            cs = in_region(rc, "cs", [P, CW], F32)
            mix = in_region(rc, "mix", [P, D], F32)
            mT_hi = in_region(rc, "mT_hi", [P, 2, D], F32R)
            mT_lo = in_region(rc, "mT_lo", [P, 2, D], F32R)
            xres = in_region(rc, "xres", [P, 2, D], F32)
            x1 = in_region(rc, "x1", [P, 2, D], F32)
            h2 = in_region(rc, "h2", [P, 2, D], F32)
            h2T = in_region(rc, "h2T", [P, D], F32)
            junk = in_region(rc, "junk", [P, D], F32)
            e16 = in_region(rc, "e16", [P, NE], F32)
            affp = in_region(rc, "affp", [P, 2, SEL_ROWS], F32)
            bst = in_region(rc, "bst", [P, 8], F32)
        with ExitStack() as re_:
            raw = in_region(re_, "raw", [P, RAW_SLOTS, CH], F32)
            w_hi = in_region(re_, "w_hi", [P, SPLIT_SLOTS, CH], F32R)
            w_lo = in_region(re_, "w_lo", [P, SPLIT_SLOTS, CH], F32R)
            xg_p = in_region(re_, "xg_p", [P, D], F32)
            xg_s = in_region(re_, "xg_s", [CAP_S, D], F32)
            xgT_hi = in_region(re_, "xgT_hi", [P, KD, CAP], F32R)
            xgT_lo = in_region(re_, "xgT_lo", [P, KD, CAP], F32R)
            hid_hi = in_region(re_, "hid_hi", [P, 2 * PAIRS, CAP], F32R)
            hid_lo = in_region(re_, "hid_lo", [P, 2 * PAIRS, CAP], F32R)
            act_g = in_region(re_, "act_g", [P, 2, 2 * CAP], F32)
            hid = in_region(re_, "hid", [P, 2, 2 * CAP], F32)
            outT = in_region(re_, "outT", [P, 4, 2 * CAP], F32)
            o_p = in_region(re_, "o_p", [P, D], F32)
            o_s = in_region(re_, "o_s", [CAP_S, D], F32)
            cur_p = in_region(re_, "cur_p", [P, 1], U32)
            cur_sg = in_region(re_, "cur_sg", [CAP_S, 1], U32)
            put_p = in_region(re_, "put_p", [P, 1], U32)
            put_s = in_region(re_, "put_s", [CAP_S, 1], U32)
            cur_g = in_region(re_, "cur_g", [P, 2], F32)

        consts_in = sem("consts_in"); tables_in = sem("tables_in")
        pads_zero = sem("pads_zero"); rot_ready = sem("rot_ready")
        x_in = [sem(f"x_in{i}") for i in range(2)]
        x_sq = sem("x_sq"); x_var = sem("x_var"); x_std = sem("x_std"); x_rstd = sem("x_rstd"); x_norm = sem("x_norm")
        xT = sem("xT"); hT_h = sem("hT_h"); hT_l = sem("hT_l")
        wi_in = [sem(f"wi_in{i}") for i in range(2)]
        wi_h = sem("wi_h"); wi_l = sem("wi_l")
        pr_glu = sem("pr_glu"); glu_sig = sem("glu_sig"); glu_u = sem("glu_u")
        pr_tok = sem("pr_tok"); t_sq = sem("t_sq"); t_ssq = sem("t_ssq"); t_var = sem("t_var"); t_std = sem("t_std")
        t_rstd = sem("t_rstd"); t_norm = sem("t_norm"); rope_a = sem("rope_a"); rope_b = sem("rope_b"); rope_c = sem("rope_c")
        v_hi = sem("v_hi"); v_lo = sem("v_lo"); conv_tap = sem("conv_tap")
        qk_hi = sem("qk_hi"); qk_lo = sem("qk_lo"); qk_T = sem("qk_T"); q_st_ok = sem("q_st_ok"); k_st_ok = sem("k_st_ok")
        scored = sem("scored"); s_max = sem("s_max"); s_exp = sem("s_exp"); pT = sem("pT"); pT_h = sem("pT_h"); pT_l = sem("pT_l")
        pv = sem("pv"); o_rec = sem("o_rec"); o_sum = sem("o_sum"); attn_ok = sem("attn_ok")
        wo_in = [sem(f"wo_in{i}") for i in range(2)]
        wo_h = sem("wo_h"); wo_l = sem("wo_l"); rows_in = sem("rows_in")
        cT = sem("cT"); c_bn = sem("c_bn"); c_var = sem("c_var"); c_std = sem("c_std"); c_rstd = sem("c_rstd")
        c_cen = sem("c_cen"); c_ln = sem("c_ln"); c_act = sem("c_act"); m_sq = sem("m_sq"); m_var = sem("m_var"); m_std = sem("m_std")
        m_rstd = sem("m_rstd"); m_ok = sem("m_ok"); mT = sem("mT"); mT_h = sem("mT_h"); mT_l = sem("mT_l"); proj = sem("proj")
        xr_in = [sem(f"xr_in{i}") for i in range(2)]
        x1_ok = sem("x1_ok"); f_sq = sem("f_sq"); f_var = sem("f_var"); f_std = sem("f_std"); f_rstd = sem("f_rstd"); h2_ok = sem("h2_ok")
        y_out = [sem(f"y_out{i}") for i in range(2)]; h_out = [sem(f"h_out{i}") for i in range(2)]
        h2_T = sem("h2_T"); h2T_ok = sem("h2T_ok"); logit = sem("logit"); l_max = sem("l_max"); l_exp = sem("l_exp"); l_rec = sem("l_rec")
        a_ok = sem("a_ok"); a_T = sem("a_T"); a_sel = sem("a_sel")
        aff_fill = sem("aff_fill"); affp_zero = sem("affp_zero"); pick = sem("pick"); picked = sem("picked"); selT = sem("selT"); sel_ok = sem("sel_ok")
        raw_in = [sem(f"raw_in{i}") for i in range(RAW_SLOTS)]
        e_hi = sem("e_hi"); e_lo = sem("e_lo"); e_used = sem("e_used")
        dma_turn = sem("dma_turn"); cur_ok = sem("cur_ok"); put_ok = sem("put_ok"); gathered = sem("gathered"); xgT = sem("xgT"); xg_h = sem("xg_h"); xg_l = sem("xg_l")
        g_act = sem("g_act"); h_mul = sem("h_mul"); h_hi = sem("h_hi"); h_lo = sem("h_lo")
        g_cur = sem("g_cur"); oT_ok = sem("oT_ok"); o_T = sem("o_T"); o_ok = sem("o_ok"); added = sem("added")

        GLU_BLOCKS = [(g, c, b) for g in range(2) for c in range(NC_CONV) for b in range(GROUPS[g][2] // 512)]
        glu_no = {key: n for n, key in enumerate(GLU_BLOCKS)}
        glu_by = [sum(k[0] < g for k in GLU_BLOCKS) for g in range(3)]
        TOK_STEPS = [(g, c, t) for g in range(2) for c in range(3) for t in range(GROUPS[g][0], GROUPS[g][0] + GROUPS[g][1])]
        tok_no = {key: n for n, key in enumerate(TOK_STEPS)}
        tok_by = [sum(k[0] < g for k in TOK_STEPS) for g in range(3)]
        UNITS = [(g, h, t) for g in range(2) for h in range(NH) for t in range(GROUPS[g][0], GROUPS[g][0] + GROUPS[g][1])]
        HALVES = [GROUPS[g][2] // 512 for g, _, _ in UNITS]
        half_no = [sum(HALVES[:n]) for n in range(len(UNITS) + 1)]
        TAPS = NC_CONV * CONV_K
        NU = len(UNITS)

        def glu_bank(n):
            return 4 + 2 * (n % 2)

        def tok_bank(n):
            return 4 + n % 4

        def flat(banks):
            return banks.rearrange("p a b -> p (a b)")

        def wi_multiplied(eng, n):
            g, c = n // CHUNKS, n % CHUNKS
            if c < NC_CONV:
                eng.wait_ge(pr_glu, glu_no[g, c, GROUPS[g][2] // 512 - 1] + 1)
            else:
                eng.wait_ge(pr_tok, tok_no[g, c - NC_CONV, GROUPS[g][0] + GROUPS[g][1] - 1] + 1)

        def y_stored(eng):
            for i in range(2):
                eng.wait_ge(y_out[i], 16 * TILES // 2)
                eng.wait_ge(h_out[i], 16 * TILES // 2)

        block = ctx.enter_context(nc.Block())

        @block.sync
        def _(sp):
            sp.dma_start(ident[:, :], ident_in).then_inc(consts_in, 16)
            sp.dma_start(colp[:, :], cols).then_inc(consts_in, 16)

            def load_x(t):
                if t >= 2:
                    sp.wait_ge(xT, t - 1)
                sp.dma_start(xin[:, t % 2, :], x_rows(t)).then_inc(x_in[t % 2], 16)

            def load_wi(g, c):
                n = CHUNKS * g + c
                for hf in range(2):
                    ks = slice(hf * KD // 2, (hf + 1) * KD // 2)
                    if n >= 1:
                        sp.wait_ge(wi_l, 2 * (n - 1) + hf + 1)
                    if c < NC_CONV:
                        c0, c1 = AW + 2 * NKV * HD + c * P, AW + 2 * NKV * HD + CW + c * P
                    else:
                        c0 = (c - NC_CONV) * CCOLS
                        c1 = c0 + P
                    sp.dma_start(wi_raw[:, hf, :, 0:P], wi[:, ks, c0:c0 + P]).then_inc(wi_in[hf], 16)
                    sp.dma_start(wi_raw[:, hf, :, P:CCOLS], wi[:, ks, c1:c1 + P]).then_inc(wi_in[hf], 16)

            load_x(0)
            load_x(1)
            load_wi(0, 0)
            sp.dma_start(rot_src, rotary).then_inc(tables_in, 16)
            sp.dma_start(rope_gain, rows[0, 0:4 * HD].partition_broadcast(P)).then_inc(tables_in, 16)
            for t in range(2, ROT_TILES):
                load_x(t)
            for c in range(1, CHUNKS):
                load_wi(0, c)
            for t in range(ROT_TILES, TILES):
                load_x(t)
            for c in range(CHUNKS):
                load_wi(1, c)

            sp.wait_ge(attn_ok, NU)
            sp.dma_start(rowp[:, :], rows[0, ROW_LNG:ROWS].partition_broadcast(P)).then_inc(rows_in, 16)
            sp.dma_start(wr_sb[:, :, :], wr).then_inc(rows_in, 16)
            for k in range(KD):
                if k >= 2:
                    sp.wait_ge(wo_l, k - 1)
                sp.dma_start(wo_raw[:, k % 2, :], wo[:, k, :]).then_inc(wo_in[k % 2], 16)
            for t in range(TILES + 1):
                if t < TILES:
                    if t >= 2:
                        sp.wait_ge(x1_ok, t - 1)
                    sp.dma_start(xres[:, t % 2, :], x_rows(t)).then_inc(xr_in[t % 2], 16)
                if t >= 1:
                    s = t - 1
                    sp.wait_ge(x1_ok, s + 1)
                    sp.dma_start(y_rows(s), x1[:, s % 2, :]).then_inc(y_out[s % 2], 16)
                    sp.wait_ge(h2_ok, s + 1)
                    sp.dma_start(h_rows[s * P:(s + 1) * P, :], h2[:, s % 2, :]).then_inc(h_out[s % 2], 16)

            sp.wait_ge(proj, TILES)

            def load_chunk(e, j):
                if j < 2 * PAIRS:
                    src = (gate_cols, up_cols)[j % 2][e, :, :, (j // 2) * CCOLS:(j // 2 + 1) * CCOLS]
                    dst = raw[:, j % RAW_SLOTS, :].rearrange("p (k f) -> p k f", k=KD)
                else:
                    src = down_rows[e, j - 2 * PAIRS]
                    dst = raw[:, j % RAW_SLOTS, :].rearrange("p (k d) -> p k d", k=2)
                sp.dma_start(dst, src).then_inc(raw_in[j % RAW_SLOTS], 16)

            for j in range(EC):
                if j >= RAW_SLOTS:
                    sp.wait_ge(e_lo, j - RAW_SLOTS + 1)
                load_chunk(0, j)
            with sp.Fori(1, NE) as e:
                for j in range(EC):
                    sp.wait_ge(proj, TILES)
                    sp.wait_ge(e_lo, e * EC + (j - RAW_SLOTS + 1))
                    load_chunk(e, j)
            y_stored(sp)
            sp.wait_ge(added, 32 * NE)

        @block.gpsimd
        def _(pool):
            pool.memset(conv[:, :, :], 0.0).then_inc(pads_zero, 1)
            pool.memset(aff[:, :], -1.0).then_inc(aff_fill, 1)

            pool.wait_ge(tables_in, 32)
            for x in range(2):
                for which, dst in ((0, rot_c), (1, rot_s)):
                    gain = rope_gain[:, (2 * x + which) * HD:(2 * x + which + 1) * HD]
                    pool.tensor_tensor(dst[:, x, :, :], rot_src[:, which, :, :],
                                       gain.unsqueeze(1).broadcast_to([P, ROT_TILES, HD]), ALU.mult).then_inc(rot_ready, 1)
            pool.wait_ge(rot_ready, 4)
            for tab in (rot_c, rot_s):
                pool.tensor_scalar(tab[:, 0, :, :], tab[:, 0, :, :], float(HD) ** -0.5, None, ALU.mult).then_inc(rot_ready, 1)
            pool.wait_ge(rot_ready, 6)

            for n, (g, c, t) in enumerate(TOK_STEPS):
                heads = 4 if c < 2 else NKV
                w, r, x = heads * HD, t - GROUPS[g][0], (0 if c < 2 else 1)

                def by_head(table):
                    return table[:, x, r, :].unsqueeze(1).broadcast_to([P, heads, HD])

                s_pairs = by_head(rot_s).rearrange("p h (d two) -> p h d two", two=2)
                src = qn[:, n % 2, 0:w].rearrange("p (h d) -> p h d", h=heads)
                pair = qn[:, n % 2, 0:w].rearrange("p (h d two) -> p h d two", h=heads, two=2)
                turn = q_turn[:, 0:w].rearrange("p (h d two) -> p h d two", h=heads, two=2)
                dst = tok[:, t, c * CCOLS:(c + 1) * CCOLS] if c < 2 else k_tok[:, t, :]
                pool.wait_ge(t_norm, n + 1)
                if n >= 1:
                    pool.wait_ge(rope_c, n)
                pool.tensor_tensor(turn[:, :, :, 0], pair[:, :, :, 1], s_pairs[:, :, :, 0], ALU.mult)
                pool.tensor_tensor(turn[:, :, :, 1], pair[:, :, :, 0], s_pairs[:, :, :, 1], ALU.mult).then_inc(rope_a, 1)
                pool.wait_ge(rope_a, n + 1)
                pool.tensor_tensor(src, src, by_head(rot_c), ALU.mult).then_inc(rope_b, 1)
                pool.wait_ge(rope_b, n + 1)
                pool.tensor_tensor(dst, qn[:, n % 2, 0:w], q_turn[:, 0:w], ALU.add).then_inc(rope_c, 1)

            pool.wait_ge(qk_lo, 3 * TILES)
            for u, (g, h, t) in enumerate(UNITS):
                pool.wait_ge(o_sum, u + 1)
                pool.tensor_scalar(tok[:, t, h * HD:(h + 1) * HD], osum[:, u % 2, :],
                                   smx[:, 2, u:u + 1], None, ALU.mult).then_inc(attn_ok, 1)

            pool.wait_ge(sel_ok, 4)
            y_stored(pool)

            def gather(e):
                pool.tensor_copy(cur_p[:, :], rows_p[:, bass.ds(e, 1)]).then_inc(cur_ok, 1)
                pool.tensor_copy(cur_sg[:, :], rows_sg[:, bass.ds(e, 1)]).then_inc(cur_ok, 1)
                pool.wait_ge(cur_ok, 2 * e + 2)
                pool.sem_inc(dma_turn, 1)
                pool.indirect_dma_start(xg_p[:, :], None, h_rows, bass.IndirectOffsetOnAxis(ap=cur_p[:, :], axis=0)
                                        ).then_inc(gathered, 16)
                pool.indirect_dma_start(xg_s[:, :], None, h_rows, bass.IndirectOffsetOnAxis(ap=cur_sg[:, :], axis=0)
                                        ).then_inc(gathered, 16)

            def scatter(e):
                pool.wait_ge(added, 32 * e)
                pool.tensor_copy(put_p[:, :], rows_p[:, bass.ds(e, 1)]).then_inc(put_ok, 1)
                pool.tensor_copy(put_s[:, :], rows_s[:, bass.ds(e, 1)]).then_inc(put_ok, 1)
                pool.wait_ge(put_ok, 2 * e + 2)
                pool.wait_ge(o_ok, 2 * e + 2)
                pool.sem_inc(dma_turn, 1)
                pool.indirect_dma_start(y_prompt[0], bass.IndirectOffsetOnAxis(ap=put_p[:, :], axis=0), o_p[:, :], None,
                                        compute_op=ALU.add).then_inc(added, 16)
                pool.indirect_dma_start(y_sample[0], bass.IndirectOffsetOnAxis(ap=put_s[:, :], axis=0), o_s[:, :], None,
                                        compute_op=ALU.add).then_inc(added, 16)

            gather(0)
            with pool.Fori(0, NE - 1) as e:
                pool.wait_ge(xgT, e + 1)
                gather(e + 1)
                scatter(e)
            scatter(NE - 1)

        @block.scalar
        def _(act):
            act.wait_ge(consts_in, 32)

            def square_x(t):
                act.wait_ge(x_in[t % 2], 16 * (t // 2 + 1))
                act.activation(flat(psum[:, 2:4, :]), xin[:, t % 2, :], ACT.Square,
                               accum_out=stat[:, t, 0:1]).then_inc(x_sq, 1)
                act.wait_ge(x_var, t + 1)
                act.activation(stat[:, t, 2:3], stat[:, t, 1:2], ACT.Sqrt).then_inc(x_std, 1)

            def split_x(g, t):
                i = t - GROUPS[g][0]
                act.wait_ge(xT, t + 1)
                act.copy(hT_hi[:, :, i * P:(i + 1) * P],
                         psum[:, 0:2, :].rearrange("p a (k b) -> p (a k) b", k=4)).then_inc(hT_h, 1)

            def split_wi(g, c):
                n = CHUNKS * g + c
                if n >= 2:
                    wi_multiplied(act, n - 2)
                for hf in range(2):
                    act.wait_ge(wi_in[hf], 32 * (n + 1))
                    for k in range(KD // 2):
                        kk = hf * KD // 2 + k
                        last = act.activation(wi_hi[:, n % 2, kk, :], wi_raw[:, hf, k, :], ACT.Copy,
                                              scale=colp[:, COL_NORM + kk:COL_NORM + kk + 1])
                    last.then_inc(wi_h, 1)

            for g in range(2):
                t0, nt = GROUPS[g][0], GROUPS[g][1]
                square_x(t0)
                if g == 1:
                    wi_multiplied(act, CHUNKS - 1)
                for t in range(t0, t0 + nt):
                    if t + 1 < t0 + nt:
                        square_x(t + 1)
                    split_x(g, t)
                split_wi(g, 0)
                for c in range(NC_CONV):
                    split_wi(g, c + 1)
                    for b in range(GROUPS[g][2] // 512):
                        n = glu_no[g, c, b]
                        act.wait_ge(pr_glu, n + 1)
                        if n >= 1:
                            act.wait_ge(glu_u, n)
                        act.activation(sig_a[:, :], psum[:, glu_bank(n) + 1, :], ACT.Sigmoid).then_inc(glu_sig, 1)
                for c in range(3):
                    if c + 1 < 3:
                        split_wi(g, NC_CONV + c + 1)
                    for t in range(t0, t0 + nt):
                        n = tok_no[g, c, t]
                        bank = tok_bank(n)
                        w = CCOLS if c < 2 else NKV * HD
                        act.wait_ge(pr_tok, n + 1)
                        if n >= 1:
                            act.wait_ge(t_ssq, n)
                        act.activation(sq[:, 0:w], psum[:, bank, 0:w], ACT.Square).then_inc(t_sq, 1)
                        if c == 2:
                            act.copy(val[:, t, :, 0:HD],
                                     psum[:, bank, w:CCOLS].rearrange("p (h d) -> p h d", h=NKV)).then_inc(v_hi, 1)
                        act.wait_ge(t_var, n + 1)
                        act.activation(hstat[:, n % 2, 1, 0:w // HD], hstat[:, n % 2, 0, 0:w // HD], ACT.Sqrt).then_inc(t_std, 1)

            act.wait_ge(rope_c, len(TOK_STEPS))
            wi_multiplied(act, 2 * CHUNKS - 1)
            for t in range(TILES):
                if t >= 1:
                    act.wait_ge(qk_T, t)
                act.copy(q_split[:, :, 0:HD].bitcast(F32R), tok[:, t, :].rearrange("p (h d) -> p h d", h=NH)).then_inc(qk_hi, 1)
                kt = k_tok[:, t, :].rearrange("p (h d) -> p h d", h=NKV)
                act.copy(k_split[:, :, 0, 0:HD].bitcast(F32R), kt).then_inc(qk_hi, 1)
                act.copy(k_split[:, :, 0, HD:2 * HD].bitcast(F32R), kt).then_inc(qk_hi, 1)
                act.wait_ge(qk_T, t + 1)
                act.copy(q_st[:, :, t * P:(t + 1) * P],
                         psum[:, 0:2, :].rearrange("p a (h b) -> p (a h) b", h=4)).then_inc(q_st_ok, 1)

            def exp_unit(u):
                n = GROUPS[UNITS[u][0]][2]
                act.wait_ge(s_max, u + 1)
                if u >= 2:
                    act.wait_ge(pT, half_no[u - 1])
                act.activation(probs[:, u % 2, 0:n], flat(psum[:, 2 * (u % 2):2 * (u % 2) + 2, :])[:, 0:n], ACT.Exp,
                               bias=smx[:, 0, u:u + 1], accum_out=smx[:, 1, u:u + 1]).then_inc(s_exp, 1)

            exp_unit(0)
            for u in range(NU):
                if u + 1 < NU:
                    exp_unit(u + 1)
                if u >= 2:
                    act.wait_ge(pv, u - 1)
                for hf in range(HALVES[u]):
                    m = half_no[u] + hf
                    act.wait_ge(pT, m + 1)
                    act.copy(pT_hi[:, u % 2, hf * 512:(hf + 1) * 512], psum[:, 4 + m % 3, :]).then_inc(pT_h, 1)

            act.wait_ge(pv, NU)
            act.wait_ge(attn_ok, NU)
            for k in range(KD):
                act.wait_ge(wo_in[k % 2], 16 * (k // 2 + 1))
                act.copy(wo_hi[:, k, :], wo_raw[:, k % 2, :]).then_inc(wo_h, 1)
            for s in range(TILES + 4):
                if s < TILES:
                    act.wait_ge(c_var, s + 1)
                    act.activation(stat[:, s, 5:6], stat[:, s, 4:5], ACT.Sqrt).then_inc(c_std, 1)
                    act.wait_ge(c_ln, s + 1)
                    if s >= 1:
                        act.wait_ge(m_ok, 2 * s)
                    act.activation(cs[:, :], cn[:, :], ACT.Silu).then_inc(c_act, 1)
                    act.wait_ge(c_act, s + 1)
                    if s >= 3:
                        act.wait_ge(f_sq, s - 2)
                    act.activation(junk[:, 0:CW], cs[:, :], ACT.Square, accum_out=stat[:, s, 7:8]).then_inc(m_sq, 1)
                    act.activation(junk[:, CW:D], tok[:, s, :], ACT.Square, accum_out=stat[:, s, 6:7]).then_inc(m_sq, 1)
                    act.wait_ge(m_var, s + 1)
                    act.activation(stat[:, s, 10:12], stat[:, s, 8:10], ACT.Sqrt).then_inc(m_std, 1)
                if 0 <= s - 1 < TILES:
                    t = s - 1
                    act.wait_ge(mT, t + 1)
                    if t >= 2:
                        act.wait_ge(proj, t - 1)
                    act.copy(mT_hi[:, t % 2, :], flat(psum[:, 1:3, :])).then_inc(mT_h, 1)
                if 0 <= s - 4 < TILES:
                    t = s - 4
                    act.wait_ge(l_max, t + 1)
                    if t >= 1:
                        act.wait_ge(a_ok, t)
                    act.activation(e16[:, :], psum[:, 7, 0:NE], ACT.Exp, bias=stat[:, t, 14:15],
                                   accum_out=stat[:, t, 15:16]).then_inc(l_exp, 1)
                if 0 <= s - 2 < TILES:
                    t = s - 2
                    act.wait_ge(x1_ok, t + 1)
                    act.wait_ge(m_sq, 2 * min(s + 1, TILES))
                    if t >= 1:
                        act.wait_ge(f_sq, t)
                    act.activation(junk[:, :], x1[:, t % 2, :], ACT.Square, accum_out=stat[:, t, 0:1]).then_inc(f_sq, 1)
                    act.wait_ge(f_var, t + 1)
                    act.activation(stat[:, t, 2:3], stat[:, t, 1:2], ACT.Sqrt).then_inc(f_std, 1)
                if 0 <= s - 3 < TILES:
                    t = s - 3
                    act.wait_ge(h2_T, t + 1)
                    if t >= 1:
                        act.wait_ge(logit, t)
                    act.copy(h2T[:, :], flat(psum[:, 5:7, :])).then_inc(h2T_ok, 1)

            def hi_chunk(e, j, first=False):
                act.wait_ge(raw_in[j % RAW_SLOTS], e * (EC // RAW_SLOTS * 16) + (j // RAW_SLOTS + 1) * 16)
                if not first:
                    act.wait_ge(e_used, e * EC + (j - SPLIT_SLOTS + 1))
                act.copy(w_hi[:, j % SPLIT_SLOTS, :], raw[:, j % RAW_SLOTS, :]).then_inc(e_hi, 1)

            def gate_act(e, m):
                act.wait_ge(e_used, e * EC + (2 * m + 2))
                act.activation(act_g[:, m % 2, :], psum[:, m % 2, 0:2 * CAP], ACT.Silu).then_inc(g_act, 1)

            def hid_high(e, m):
                act.wait_ge(h_mul, e * PAIRS + (m + 1))
                act.copy(hid_hi[:, 2 * m:2 * m + 2, :].rearrange("p a b -> p (a b)"), hid[:, m % 2, :]).then_inc(h_hi, 1)

            def gathered_high(e):
                act.wait_ge(xgT, e + 1)
                act.copy(xgT_hi[:, :, :].rearrange("p (a b) c -> p a (b c)", a=4), psum[:, 0:4, 0:2 * CAP]).then_inc(xg_h, 1)

            def out_columns(e):
                act.wait_ge(e_used, e * EC + EC)
                act.copy(outT[:, :, :], psum[:, 4:8, 0:2 * CAP]).then_inc(oT_ok, 1)

            def out_rows(e):
                act.wait_ge(o_T, e + 1)
                act.wait_ge(g_cur, 2 * e + 2)
                act.wait_ge(added, 32 * e)
                act.activation(o_p[:, :], flat(psum[:, 4:6, :]), ACT.Copy, scale=cur_g[:, 0:1]).then_inc(o_ok, 1)
                act.activation(o_s[:, :], flat(psum[0:CAP_S, 6:8, :]), ACT.Copy,
                               scale=cur_g[0:CAP_S, 1:2]).then_inc(o_ok, 1)

            def early(e, j):
                hi_chunk(e, j, first=isinstance(e, int) and j < SPLIT_SLOTS)
                if j >= 3 and j % 2 == 1:
                    gate_act(e, (j - 3) // 2)
                if j >= 4 and j % 2 == 0:
                    hid_high(e, (j - 4) // 2)

            def late(e, last):
                for j in range(TURN, EC):
                    hi_chunk(e, j)
                    if j % 2 == 1 and (j - 3) // 2 < PAIRS:
                        gate_act(e, (j - 3) // 2)
                    if j % 2 == 0 and (j - 4) // 2 < PAIRS:
                        hid_high(e, (j - 4) // 2)
                    if j == 20 and not last:
                        gathered_high(e + 1)

            act.wait_ge(proj, TILES)
            for j in range(SPLIT_SLOTS):
                early(0, j)
            gathered_high(0)
            for j in range(SPLIT_SLOTS, TURN):
                early(0, j)
            with act.Fori(0, NE - 1) as e:
                late(e, False)
                for j in range(TURN):
                    if j == 2:
                        out_columns(e)
                    early(e + 1, j)
                out_rows(e)
            late(NE - 1, True)
            out_columns(NE - 1)
            out_rows(NE - 1)

        @block.vector
        def _(dve):
            conv_done = [0]

            def conv_run(n):
                for w in range(conv_done[0], min(conv_done[0] + n, 2 * TAPS)):
                    g, c, k = w // TAPS, w % TAPS // CONV_K, w % CONV_K
                    T, base = GROUPS[g][2], GROUPS[g][3]
                    out = conv[:, c, base + PAD:base + PAD + T]
                    u = conv[:, c + 1, base + k:base + k + T]
                    tap = colp[:, COL_TAP + c * CONV_K + k:COL_TAP + c * CONV_K + k + 1]
                    if k == 0:
                        dve.wait_ge(glu_u, glu_no[g, c, T // 512 - 1] + 1)
                        if w:
                            dve.wait_ge(conv_tap, w)
                        dve.tensor_scalar(out, u, tap, colp[:, COL_BIAS + c:COL_BIAS + c + 1], ALU.mult, ALU.add
                                          ).then_inc(conv_tap, 1)
                    else:
                        dve.wait_ge(conv_tap, w)
                        dve.scalar_tensor_tensor(out=out, in0=u, scalar=tap, in1=out, op0=ALU.mult, op1=ALU.add
                                                 ).then_inc(conv_tap, 1)
                    conv_done[0] = w + 1

            dve.wait_ge(consts_in, 32)
            dve.wait_ge(pads_zero, 1)

            def norm_x(t):
                dve.wait_ge(x_sq, t + 1)
                dve.tensor_scalar(stat[:, t, 1:2], stat[:, t, 0:1], 1.0 / D, EPS, ALU.mult, ALU.add).then_inc(x_var, 1)
                dve.wait_ge(x_std, t + 1)
                dve.reciprocal(stat[:, t, 3:4], stat[:, t, 2:3]).then_inc(x_rstd, 1)
                dve.wait_ge(x_rstd, t + 1)
                dve.tensor_scalar(xin[:, t % 2, :], xin[:, t % 2, :], stat[:, t, 3:4], None, ALU.mult).then_inc(x_norm, 1)

            def split_x(g, t):
                i = t - GROUPS[g][0]
                dve.wait_ge(hT_h, t + 1)
                dve.tensor_tensor(hT_lo[:, :, i * P:(i + 1) * P],
                                  psum[:, 0:2, :].rearrange("p a (k b) -> p (a k) b", k=4),
                                  hT_hi[:, :, i * P:(i + 1) * P].bitcast(F32), ALU.subtract).then_inc(hT_l, 1)

            def split_wi(g, c):
                n = CHUNKS * g + c
                for hf in range(2):
                    dve.wait_ge(wi_h, 2 * n + hf + 1)
                    for k in range(KD // 2):
                        kk = hf * KD // 2 + k
                        last = dve.scalar_tensor_tensor(
                            out=wi_lo[:, n % 2, kk, :], in0=wi_raw[:, hf, k, :],
                            scalar=colp[:, COL_NORM + kk:COL_NORM + kk + 1],
                            in1=wi_hi[:, n % 2, kk, :].bitcast(F32), op0=ALU.mult, op1=ALU.subtract)
                    last.then_inc(wi_l, 1)

            for g in range(2):
                t0, nt, T, base = GROUPS[g]
                norm_x(t0)
                for t in range(t0, t0 + nt):
                    if t + 1 < t0 + nt:
                        norm_x(t + 1)
                    split_x(g, t)
                split_wi(g, 0)
                for c in range(NC_CONV):
                    split_wi(g, c + 1)
                    for b in range(T // 512):
                        n = glu_no[g, c, b]
                        dve.wait_ge(glu_sig, n + 1)
                        dve.tensor_tensor(conv[:, c + 1, base + PAD + b * 512:base + PAD + (b + 1) * 512],
                                          psum[:, glu_bank(n), :], sig_a[:, :], ALU.mult).then_inc(glu_u, 1)
                        if c >= 1 or g == 1:
                            conv_run(6)
                for c in range(3):
                    if c + 1 < 3:
                        split_wi(g, NC_CONV + c + 1)
                    for t in range(t0, t0 + nt):
                        n = tok_no[g, c, t]
                        heads = 4 if c < 2 else NKV
                        w = heads * HD
                        hs = hstat[:, n % 2, :, 0:heads]
                        dve.wait_ge(t_sq, n + 1)
                        dve.tensor_reduce(hs[:, 2, :], sq[:, 0:w].rearrange("p (h d) -> p h d", h=heads), AX_X, ALU.add
                                          ).then_inc(t_ssq, 1)
                        dve.wait_ge(t_ssq, n + 1)
                        dve.tensor_scalar(hs[:, 0, :], hs[:, 2, :], 1.0 / HD, EPS, ALU.mult, ALU.add).then_inc(t_var, 1)
                        conv_run(1)
                        dve.wait_ge(t_std, n + 1)
                        dve.reciprocal(hs[:, 2, :], hs[:, 1, :]).then_inc(t_rstd, 1)
                        dve.wait_ge(t_rstd, n + 1)
                        if n >= 2:
                            dve.wait_ge(rope_c, n - 1)
                        dve.tensor_tensor(qn[:, n % 2, 0:w].rearrange("p (h d) -> p h d", h=heads),
                                          psum[:, tok_bank(n), 0:w].rearrange("p (h d) -> p h d", h=heads),
                                          hs[:, 2, :].unsqueeze(2).broadcast_to([P, heads, HD]), ALU.mult).then_inc(t_norm, 1)
                        if c == 2:
                            dve.wait_ge(v_hi, t + 1)
                            dve.tensor_tensor(val[:, t, :, HD:2 * HD],
                                              psum[:, tok_bank(n), w:CCOLS].rearrange("p (h d) -> p h d", h=NKV),
                                              val[:, t, :, 0:HD].bitcast(F32), ALU.subtract).then_inc(v_lo, 1)

            for t in range(TILES):
                conv_run(1)
                dve.wait_ge(qk_hi, 3 * t + 3)
                dve.tensor_tensor(q_split[:, :, HD:2 * HD].bitcast(F32R), tok[:, t, :].rearrange("p (h d) -> p h d", h=NH),
                                  q_split[:, :, 0:HD], ALU.subtract).then_inc(qk_lo, 1)
                kt = k_tok[:, t, :].rearrange("p (h d) -> p h d", h=NKV)
                for hf in range(2):
                    dve.tensor_tensor(k_split[:, :, 1, hf * HD:(hf + 1) * HD].bitcast(F32R), kt,
                                      k_split[:, :, 0, 0:HD], ALU.subtract).then_inc(qk_lo, 1)
                dve.wait_ge(qk_T, t + 1)
                dve.tensor_copy(k_st[:, :, :, t * P:(t + 1) * P],
                                psum[:, 2, :].rearrange("p (h x b) -> p h x b", h=NKV, x=2)).then_inc(k_st_ok, 1)

            def max_unit(u):
                n = GROUPS[UNITS[u][0]][2]
                dve.wait_ge(scored, u + 1)
                dve.tensor_reduce(smx[:, 0, u:u + 1], flat(psum[:, 2 * (u % 2):2 * (u % 2) + 2, :])[:, 0:n],
                                  AX_X, ALU.max, negate=True).then_inc(s_max, 1)

            def rows_unit(u):
                dve.wait_ge(pv, u + 1)
                dve.wait_ge(s_exp, u + 1)
                dve.reciprocal(smx[:, 2, u:u + 1], smx[:, 1, u:u + 1])
                if u >= 2:
                    dve.wait_ge(attn_ok, u - 1)
                dve.tensor_reduce(osum[:, u % 2, :], psum[:, 7, 0:2 * HD].rearrange("p (x d) -> p d x", x=2),
                                  AX_X, ALU.add).then_inc(o_sum, 1)

            max_unit(0)
            for u in range(NU):
                if u + 1 < NU:
                    max_unit(u + 1)
                if u >= 2:
                    rows_unit(u - 2)
                for hf in range(HALVES[u]):
                    m = half_no[u] + hf
                    dve.wait_ge(pT_h, m + 1)
                    dve.tensor_tensor(pT_lo[:, u % 2, hf * 512:(hf + 1) * 512], psum[:, 4 + m % 3, :],
                                      pT_hi[:, u % 2, hf * 512:(hf + 1) * 512].bitcast(F32), ALU.subtract).then_inc(pT_l, 1)
                conv_run(2)
            rows_unit(NU - 2)
            rows_unit(NU - 1)
            conv_run(2 * TAPS)

            dve.wait_ge(attn_ok, NU)
            dve.memset(affp[:, :, :], 0.0).then_inc(affp_zero, 1)
            for k in range(KD):
                dve.wait_ge(wo_h, k + 1)
                dve.tensor_tensor(wo_lo[:, k, :], wo_raw[:, k % 2, :], wo_hi[:, k, :].bitcast(F32), ALU.subtract
                                  ).then_inc(wo_l, 1)
            dve.wait_ge(rows_in, 32)
            lng, lnb = rowp[:, 0:CW], rowp[:, CW:2 * CW]
            mix_gain = rowp[:, ROW_MIX - ROW_LNG:ROW_MIX - ROW_LNG + D]
            ffn_gain = rowp[:, ROW_FFN - ROW_LNG:ROW_FFN - ROW_LNG + D]
            for s in range(TILES + 4):
                if s < TILES:
                    dve.wait_ge(cT, s + 1)
                    dve.bn_stats(bst[:, 0:6], psum[:, 0, :]).then_inc(c_bn, 1)
                    dve.wait_ge(c_bn, 2 * s + 1)
                    dve.bn_aggr(bst[:, 6:8], bst[:, 0:6]).then_inc(c_bn, 1)
                    dve.wait_ge(c_bn, 2 * s + 2)
                    dve.tensor_scalar(stat[:, s, 4:5], bst[:, 7:8], EPS, None, ALU.add).then_inc(c_var, 1)
                    if s >= 1:
                        dve.wait_ge(c_act, s)
                    dve.scalar_tensor_tensor(out=cn[:, :], in0=psum[:, 0, :], scalar=bst[:, 6:7], in1=lng,
                                             op0=ALU.subtract, op1=ALU.mult).then_inc(c_cen, 1)
                    dve.wait_ge(c_std, s + 1)
                    dve.reciprocal(stat[:, s, 5:6], stat[:, s, 5:6]).then_inc(c_rstd, 1)
                    dve.wait_ge(c_rstd, s + 1)
                    dve.wait_ge(c_cen, s + 1)
                    dve.scalar_tensor_tensor(out=cn[:, :], in0=cn[:, :], scalar=stat[:, s, 5:6], in1=lnb,
                                             op0=ALU.mult, op1=ALU.add).then_inc(c_ln, 1)
                    dve.wait_ge(m_sq, 2 * s + 2)
                    dve.tensor_scalar(stat[:, s, 8:10], stat[:, s, 6:8], 1.0 / AW, EPS, ALU.mult, ALU.add).then_inc(m_var, 1)
                    dve.wait_ge(m_std, s + 1)
                    dve.reciprocal(stat[:, s, 12:14], stat[:, s, 10:12]).then_inc(m_rstd, 1)
                    dve.wait_ge(m_rstd, s + 1)
                    if s >= 1:
                        dve.wait_ge(mT, s)
                    dve.scalar_tensor_tensor(out=mix[:, 0:AW], in0=tok[:, s, :], scalar=stat[:, s, 12:13],
                                             in1=mix_gain[:, 0:AW], op0=ALU.mult, op1=ALU.mult).then_inc(m_ok, 1)
                    dve.scalar_tensor_tensor(out=mix[:, AW:D], in0=cs[:, :], scalar=stat[:, s, 13:14],
                                             in1=mix_gain[:, AW:D], op0=ALU.mult, op1=ALU.mult).then_inc(m_ok, 1)
                if 0 <= s - 1 < TILES:
                    t = s - 1
                    dve.wait_ge(mT_h, t + 1)
                    dve.tensor_tensor(mT_lo[:, t % 2, :], flat(psum[:, 1:3, :]), mT_hi[:, t % 2, :].bitcast(F32),
                                      ALU.subtract).then_inc(mT_l, 1)
                if 0 <= s - 4 < TILES:
                    t = s - 4
                    dve.wait_ge(logit, t + 1)
                    dve.tensor_reduce(stat[:, t, 14:15], psum[:, 7, 0:NE], AX_X, ALU.max, negate=True).then_inc(l_max, 1)
                    dve.wait_ge(l_exp, t + 1)
                    dve.reciprocal(stat[:, t, 15:16], stat[:, t, 15:16]).then_inc(l_rec, 1)
                    dve.wait_ge(l_rec, t + 1)
                    if t >= 1:
                        dve.wait_ge(a_T, t)
                    else:
                        dve.wait_ge(affp_zero, 1)
                    place = affp[:, 0, 0:NE] if t < ROT_TILES else affp[:, 1, SAMPLE_ROW:SEL_ROWS]
                    dve.tensor_scalar(place, e16[:, :], stat[:, t, 15:16], None, ALU.mult).then_inc(a_ok, 1)
                if 0 <= s - 2 < TILES:
                    t = s - 2
                    dve.wait_ge(proj, t + 1)
                    dve.wait_ge(xr_in[t % 2], 16 * (t // 2 + 1))
                    if t >= 2:
                        dve.wait_ge(y_out[t % 2], 16 * (t // 2))
                        dve.wait_ge(f_sq, t - 1)
                    dve.tensor_tensor(x1[:, t % 2, :], flat(psum[:, 3:5, :]), xres[:, t % 2, :], ALU.add).then_inc(x1_ok, 1)
                    dve.wait_ge(f_sq, t + 1)
                    dve.tensor_scalar(stat[:, t, 1:2], stat[:, t, 0:1], 1.0 / D, EPS, ALU.mult, ALU.add).then_inc(f_var, 1)
                    dve.wait_ge(f_std, t + 1)
                    dve.reciprocal(stat[:, t, 3:4], stat[:, t, 2:3]).then_inc(f_rstd, 1)
                    dve.wait_ge(f_rstd, t + 1)
                    if t >= 2:
                        dve.wait_ge(h_out[t % 2], 16 * (t // 2))
                        dve.wait_ge(h2_T, t - 1)
                    dve.scalar_tensor_tensor(out=h2[:, t % 2, :], in0=x1[:, t % 2, :], scalar=stat[:, t, 3:4],
                                             in1=ffn_gain, op0=ALU.mult, op1=ALU.mult).then_inc(h2_ok, 1)
                if 0 <= s - 4 < TILES:
                    t = s - 4
                    dve.wait_ge(a_T, t + 1)
                    if t == 0:
                        dve.wait_ge(aff_fill, 1)
                    if t < ROT_TILES:
                        dve.tensor_copy(aff[0:NE, t * P:(t + 1) * P], psum[0:NE, 7, P:2 * P]).then_inc(a_sel, 1)
                    else:
                        i = t - ROT_TILES
                        dve.tensor_copy(aff[SAMPLE_ROW:SEL_ROWS, i * P:(i + 1) * P],
                                        psum[SAMPLE_ROW:SEL_ROWS, 7, P:2 * P]).then_inc(a_sel, 1)

            dve.wait_ge(a_sel, TILES)
            for r in range(CAP_P // 8):
                v, vi = top[:, 8 * r:8 * r + 8], topi[:, 8 * r:8 * r + 8]
                if r:
                    dve.wait_ge(pick, 3 * r)
                dve.max(v, aff[:, :]).then_inc(pick, 1)
                dve.wait_ge(pick, 3 * r + 1)
                dve.max_index(vi, v, aff[:, :]).then_inc(pick, 1)
                dve.match_replace(aff[:, :], v, aff[:, :], -2.0).then_inc(pick, 1)
            dve.wait_ge(pick, 3 * CAP_P // 8)
            dve.tensor_copy(topf[:, :], topi[:, :]).then_inc(picked, 1)
            dve.wait_ge(selT, 1)
            dve.tensor_copy(gates[:, :], psum[:, 0, 0:SEL_ROWS]).then_inc(sel_ok, 1)
            dve.tensor_copy(rows_p[:, :], psum[:, 0, 64:64 + NE]).then_inc(sel_ok, 1)
            dve.tensor_copy(rows_s[:, :], psum[0:CAP_S, 0, 64 + SAMPLE_ROW:64 + SEL_ROWS]).then_inc(sel_ok, 1)
            dve.tensor_scalar(rows_sg[:, :], psum[0:CAP_S, 0, 64 + SAMPLE_ROW:64 + SEL_ROWS], float(N_PROMPT), None,
                              ALU.add).then_inc(sel_ok, 1)

            def lo_chunk(e, j):
                dve.wait_ge(e_hi, e * EC + (j + 1))
                dve.tensor_tensor(w_lo[:, j % SPLIT_SLOTS, :], raw[:, j % RAW_SLOTS, :],
                                  w_hi[:, j % SPLIT_SLOTS, :].bitcast(F32), ALU.subtract).then_inc(e_lo, 1)

            def hid_mul(e, m):
                dve.wait_ge(g_act, e * PAIRS + (m + 1))
                dve.tensor_tensor(hid[:, m % 2, :], psum[:, 2 + m % 2, 0:2 * CAP], act_g[:, m % 2, :], ALU.mult
                                  ).then_inc(h_mul, 1)

            def hid_low(e, m):
                dve.wait_ge(h_hi, e * PAIRS + (m + 1))
                dve.tensor_tensor(hid_lo[:, 2 * m:2 * m + 2, :].rearrange("p a b -> p (a b)"), hid[:, m % 2, :],
                                  hid_hi[:, 2 * m:2 * m + 2, :].rearrange("p a b -> p (a b)").bitcast(F32), ALU.subtract
                                  ).then_inc(h_lo, 1)

            def gathered_low(e):
                dve.wait_ge(xg_h, e + 1)
                dve.tensor_tensor(xgT_lo[:, :, :].rearrange("p (a b) c -> p a (b c)", a=4), psum[:, 0:4, 0:2 * CAP],
                                  xgT_hi[:, :, :].rearrange("p (a b) c -> p a (b c)", a=4).bitcast(F32), ALU.subtract
                                  ).then_inc(xg_l, 1)

            def gates_of(e):
                dve.wait_ge(o_ok, 2 * e)
                dve.tensor_copy(cur_g[:, 0:1], gates[:, bass.ds(e, 1)]).then_inc(g_cur, 1)
                dve.tensor_copy(cur_g[0:CAP_S, 1:2], gates[0:CAP_S, bass.ds(e + SAMPLE_ROW, 1)]).then_inc(g_cur, 1)

            def early(e, j):
                lo_chunk(e, j)
                if j >= 3 and j % 2 == 1:
                    hid_mul(e, (j - 3) // 2)
                if j >= 4 and j % 2 == 0:
                    hid_low(e, (j - 4) // 2)

            def late(e, last):
                for j in range(TURN, EC):
                    lo_chunk(e, j)
                    if j % 2 == 1 and (j - 3) // 2 < PAIRS:
                        hid_mul(e, (j - 3) // 2)
                    if j % 2 == 0 and (j - 4) // 2 < PAIRS:
                        hid_low(e, (j - 4) // 2)
                    if j == 20 and not last:
                        gathered_low(e + 1)

            for j in range(SPLIT_SLOTS):
                early(0, j)
            gathered_low(0)
            for j in range(SPLIT_SLOTS, TURN):
                early(0, j)
            with dve.Fori(0, NE - 1) as e:
                late(e, False)
                gates_of(e)
                for j in range(TURN):
                    early(e + 1, j)
            late(NE - 1, True)
            gates_of(NE - 1)

        @block.tensor
        def _(pe):
            def product3(out, a_hi, a_lo, b_hi, b_lo, start, stop, shared=False):
                pe.matmul(out, a_hi, b_hi, start=start, stop=False, skip_group_check=shared)
                pe.matmul(out, a_hi, b_lo, start=False, stop=False, skip_group_check=shared)
                return pe.matmul(out, a_lo, b_hi, start=False, stop=stop, skip_group_check=shared)

            pe.wait_ge(consts_in, 32)
            for g in range(2):
                t0, nt, T, base = GROUPS[g]
                for t in range(t0, t0 + nt):
                    pe.wait_ge(x_norm, t + 1)
                    if t:
                        pe.wait_ge(hT_l, t)
                    for k in range(KD):
                        last = pe.transpose(psum[:, k // 4, k % 4 * P:(k % 4 + 1) * P], xin[:, t % 2, k * P:(k + 1) * P],
                                            ident[:, :])
                    last.then_inc(xT, 1)
                pe.wait_ge(hT_l, t0 + nt)
                for c in range(NC_CONV):
                    ch = CHUNKS * g + c
                    ws = ch % 2
                    pe.wait_ge(wi_l, 2 * ch + 2)
                    for b in range(T // 512):
                        n = glu_no[g, c, b]
                        if n - glu_by[g] < 2 and g == 1:
                            pe.wait_ge(t_norm, tok_by[1])
                            pe.wait_ge(v_lo, GROUPS[0][1])
                        if n >= 2:
                            pe.wait_ge(glu_u, n - 1)
                        for half in range(2):
                            for k in range(KD):
                                ws_k = (wi_hi[:, ws, k, half * P:(half + 1) * P], wi_lo[:, ws, k, half * P:(half + 1) * P])
                                last = product3(psum[:, glu_bank(n) + half, :], *ws_k,
                                                hT_hi[:, k, b * 512:(b + 1) * 512], hT_lo[:, k, b * 512:(b + 1) * 512],
                                                k == 0, k == KD - 1)
                        last.then_inc(pr_glu, 1)
                for c in range(3):
                    ch = CHUNKS * g + NC_CONV + c
                    ws = ch % 2
                    pe.wait_ge(wi_l, 2 * ch + 2)
                    for t in range(t0, t0 + nt):
                        n, i = tok_no[g, c, t], t - t0
                        if n - tok_by[g] < 4:
                            pe.wait_ge(glu_u, glu_by[g + 1])
                        else:
                            pe.wait_ge(t_norm, n - 3)
                            if c == 2 and i >= 4:
                                pe.wait_ge(v_lo, t - 3)
                        for k in range(KD):
                            last = product3(psum[:, tok_bank(n), 0:CCOLS],
                                            hT_hi[:, k, i * P:(i + 1) * P], hT_lo[:, k, i * P:(i + 1) * P],
                                            wi_hi[:, ws, k, :], wi_lo[:, ws, k, :], k == 0, k == KD - 1)
                        last.then_inc(pr_tok, 1)

            for t in range(TILES):
                pe.wait_ge(qk_lo, 3 * t + 3)
                if t:
                    pe.wait_ge(q_st_ok, t)
                    pe.wait_ge(k_st_ok, t)
                for h in range(NH):
                    pe.transpose(psum[:, h // 4, h % 4 * P:(h % 4 + 1) * P], q_split[:, h, :], ident[:, :])
                for h in range(NKV):
                    for x in range(2):
                        last = pe.transpose(psum[:, 2, (2 * h + x) * P:(2 * h + x + 1) * P], k_split[:, h, x, :], ident[:, :])
                last.then_inc(qk_T, 1)
            pe.wait_ge(q_st_ok, TILES)
            pe.wait_ge(k_st_ok, TILES)
            pe.wait_ge(t_norm, len(TOK_STEPS))
            pe.wait_ge(v_lo, TILES)

            def scores(u):
                g, h, t = UNITS[u]
                key0 = GROUPS[g][0] * P
                if u >= 2:
                    pe.wait_ge(s_exp, u - 1)
                for hf in range(HALVES[u]):
                    for x in range(2):
                        last = pe.matmul(psum[:, 2 * (u % 2) + hf, :], q_st[:, h, t * P:(t + 1) * P],
                                         k_st[:, h // (NH // NKV), x, key0 + hf * 512:key0 + (hf + 1) * 512],
                                         start=(x == 0), stop=(x == 1))
                last.then_inc(scored, 1)

            def transposes(u):
                pe.wait_ge(s_exp, u + 1)
                for hf in range(HALVES[u]):
                    m = half_no[u] + hf
                    if m >= 3:
                        pe.wait_ge(pT_l, m - 2)
                    for i in range(4):
                        last = pe.transpose(psum[:, 4 + m % 3, i * P:(i + 1) * P],
                                            probs[:, u % 2, (4 * hf + i) * P:(4 * hf + i + 1) * P], ident[:, :])
                    last.then_inc(pT, 1)

            def weighted(u):
                g, h, t = UNITS[u]
                pe.wait_ge(pT_l, half_no[u + 1])
                if u:
                    pe.wait_ge(o_sum, u)
                nk = 4 * HALVES[u]
                for i in range(nk):
                    v = val[:, GROUPS[g][0] + i, h // (NH // NKV), :]
                    pe.matmul(psum[:, 7, 0:2 * HD], pT_hi[:, u % 2, i * P:(i + 1) * P], v,
                              start=(i == 0), stop=False, skip_group_check=True)
                    last = pe.matmul(psum[:, 7, 0:HD], pT_lo[:, u % 2, i * P:(i + 1) * P], v[:, 0:HD],
                                     start=False, stop=(i == nk - 1), skip_group_check=True)
                last.then_inc(pv, 1)

            scores(0)
            for u in range(NU):
                if u + 1 < NU:
                    scores(u + 1)
                transposes(u)
                if u:
                    weighted(u - 1)
            weighted(NU - 1)

            pe.wait_ge(s_exp, NU)
            pe.wait_ge(o_sum, NU)
            pe.wait_ge(wo_l, KD)
            pe.wait_ge(rows_in, 32)
            for s in range(TILES + 4):
                if s < TILES:
                    g = 0 if s < ROT_TILES else 1
                    col = GROUPS[g][3] + PAD + (s - GROUPS[g][0]) * P
                    pe.wait_ge(conv_tap, TAPS * (g + 1))
                    if s:
                        pe.wait_ge(c_cen, s)
                    for c in range(NC_CONV):
                        last = pe.transpose(psum[:, 0, c * P:(c + 1) * P], conv[:, c, col:col + P], ident[:, :])
                    last.then_inc(cT, 1)
                if 0 <= s - 4 < TILES:
                    t = s - 4
                    pe.wait_ge(h2T_ok, t + 1)
                    if t:
                        pe.wait_ge(a_sel, t)
                    for k in range(KD):
                        last = pe.matmul(psum[:, 7, 0:NE], h2T[:, k * P:(k + 1) * P], wr_sb[:, k, :],
                                         start=(k == 0), stop=(k == KD - 1))
                    last.then_inc(logit, 1)
                if 0 <= s - 1 < TILES:
                    t = s - 1
                    pe.wait_ge(m_ok, 2 * t + 2)
                    if t:
                        pe.wait_ge(mT_l, t)
                    for k in range(KD):
                        last = pe.transpose(psum[:, 1 + k // 4, k % 4 * P:(k % 4 + 1) * P], mix[:, k * P:(k + 1) * P], ident[:, :])
                    last.then_inc(mT, 1)
                if 0 <= s - 2 < TILES:
                    t = s - 2
                    pe.wait_ge(mT_l, t + 1)
                    if t:
                        pe.wait_ge(x1_ok, t)
                    for half in range(2):
                        for k in range(KD):
                            last = product3(psum[:, 3 + half, :],
                                            mT_hi[:, t % 2, k * P:(k + 1) * P], mT_lo[:, t % 2, k * P:(k + 1) * P],
                                            wo_hi[:, k, half * 512:(half + 1) * 512], wo_lo[:, k, half * 512:(half + 1) * 512],
                                            k == 0, k == KD - 1)
                    last.then_inc(proj, 1)
                if 0 <= s - 4 < TILES:
                    t = s - 4
                    pe.wait_ge(a_ok, t + 1)
                    if t < ROT_TILES:
                        pe.transpose(psum[0:NE, 7, P:2 * P], affp[:, 0, 0:NE], ident[:, :]).then_inc(a_T, 1)
                    else:
                        pe.transpose(psum[0:SEL_ROWS, 7, P:2 * P], affp[:, 1, :], ident[:, :]).then_inc(a_T, 1)
                if 0 <= s - 3 < TILES:
                    t = s - 3
                    pe.wait_ge(h2_ok, t + 1)
                    if t:
                        pe.wait_ge(h2T_ok, t)
                    for k in range(KD):
                        last = pe.transpose(psum[:, 5 + k // 4, k % 4 * P:(k % 4 + 1) * P], h2[:, t % 2, k * P:(k + 1) * P], ident[:, :])
                    last.then_inc(h2_T, 1)

            pe.wait_ge(picked, 1)
            pe.transpose(psum[:, 0, 0:SEL_ROWS], top[:, :], ident[0:SEL_ROWS, 0:SEL_ROWS])
            pe.transpose(psum[:, 0, 64:64 + SEL_ROWS], topf[:, :], ident[0:SEL_ROWS, 0:SEL_ROWS]).then_inc(selT, 1)

            def gathered_T(e):
                pe.wait_ge(gathered, 32 * e + 32)
                pe.wait_ge(h_mul, e * PAIRS)
                for k in range(KD):
                    c0 = k % 2 * CAP
                    pe.transpose(psum[:, k // 2, c0:c0 + CAP_P], xg_p[:, k * P:(k + 1) * P], ident[:, :])
                    last = pe.transpose(psum[:, k // 2, c0 + CAP_P:c0 + CAP], xg_s[:, k * P:(k + 1) * P],
                                        ident[0:CAP_S, 0:CAP_S])
                last.then_inc(xgT, 1)

            def out_T(e):
                pe.wait_ge(oT_ok, e + 1)
                for k in range(KD):
                    c0 = k % 2 * CAP
                    pe.transpose(psum[:, 4 + k // 4, k % 4 * P:(k % 4 + 1) * P], outT[:, k // 2, c0:c0 + CAP_P], ident[:, :])
                    last = pe.transpose(psum[0:CAP_S, 6 + k // 4, k % 4 * P:(k % 4 + 1) * P],
                                        outT[:, k // 2, c0 + CAP_P:c0 + CAP], ident[:, :])
                last.then_inc(o_T, 1)

            def chunk(e, j):
                slot = j % SPLIT_SLOTS
                pe.wait_ge(e_lo, e * EC + (j + 1))
                if j < 2 * PAIRS:
                    m, up = j // 2, j % 2
                    if j == 0:
                        pe.wait_ge(xg_l, e + 1)
                    if m >= 2 and not up:
                        pe.wait_ge(h_mul, e * PAIRS + (m - 1))
                    for i in range(2):
                        for k in range(KD):
                            w0 = k * CCOLS + i * P
                            last = product3(psum[:, 2 * up + m % 2, i * CAP:(i + 1) * CAP],
                                            w_hi[:, slot, w0:w0 + P], w_lo[:, slot, w0:w0 + P],
                                            xgT_hi[:, k, :], xgT_lo[:, k, :], k == 0, k == KD - 1)
                else:
                    jj = j - 2 * PAIRS
                    if jj == 0:
                        pe.wait_ge(o_ok, 2 * e)
                    pe.wait_ge(h_lo, e * PAIRS + (jj + 1))
                    for i in range(2):
                        for d in range(KD):
                            w0 = i * D + d * P
                            last = product3(psum[:, 4 + d // 2, d % 2 * CAP:(d % 2 + 1) * CAP],
                                            w_hi[:, slot, w0:w0 + P], w_lo[:, slot, w0:w0 + P],
                                            hid_hi[:, 2 * jj + i, :], hid_lo[:, 2 * jj + i, :],
                                            jj == 0 and i == 0 and d % 2 == 0, j == EC - 1 and i == 1, shared=True)
                last.then_inc(e_used, 1)

            def late(e, last):
                for j in range(TURN, EC):
                    chunk(e, j)
                    if j == 17 and not last:
                        gathered_T(e + 1)

            gathered_T(0)
            for j in range(TURN):
                chunk(0, j)
            with pe.Fori(0, NE - 1) as e:
                late(e, False)
                for j in range(TURN):
                    chunk(e + 1, j)
                    if j == 3:
                        out_T(e)
            late(NE - 1, True)
            out_T(NE - 1)


def rotary_tables():
    grid_w, axis = 64, HD // 2
    pos = np.arange(N_PROMPT)
    inv_freq = 10000.0 ** (-np.arange(0, axis, 2, dtype=np.float32) / np.float32(axis))
    ang = np.concatenate([(pos // grid_w).astype(np.float32)[:, None] * inv_freq.astype(np.float32),
                          (pos % grid_w).astype(np.float32)[:, None] * inv_freq.astype(np.float32)], axis=-1)
    cos = np.repeat(np.cos(ang), 2, axis=-1)
    sin = np.stack([-np.sin(ang), np.sin(ang)], axis=-1).reshape(N_PROMPT, HD)
    both = np.stack([cos, sin]).reshape(2, ROT_TILES, P, HD).transpose(2, 0, 1, 3)
    return np.ascontiguousarray(both.astype(np.float32))


def kernel(**inputs):
    import concourse.bacc as _bacc
    from concourse.bass_utils import run_bass_kernel_spmd as _run

    a = {k: np.asarray(v) for k, v in inputs.items()}

    def other_of_pair(g):
        return g.reshape(HD // 2, 2)[:, ::-1].reshape(HD)

    cols = np.concatenate([
        a["attn_norm_g"].reshape(KD, P).T,
        a["conv_dw_w"].reshape(CONV_K, NC_CONV, P).transpose(2, 1, 0).reshape(P, NC_CONV * CONV_K),
        a["conv_dw_b"].reshape(NC_CONV, P).T,
    ], axis=1)
    q_g, k_g = a["q_norm_g"][0], a["k_norm_g"][0]
    rows = np.concatenate([q_g, other_of_pair(q_g), k_g, other_of_pair(k_g), a["conv_ln_g"][0], a["conv_ln_b"][0],
                           a["attn_out_g"][0], a["conv_out_g"][0], a["ffn_norm_g"][0]])[None]
    ins = {
        "x_prompt": a["x_prompt"], "x_sample": a["x_sample"], "w_in": a["w_in"], "w_out": a["w_out"],
        "w_router": a["w_router"], "w_gate": a["w_gate"], "w_up": a["w_up"], "w_down": a["w_down"],
        "cols": cols, "rows": rows, "rotary": rotary_tables(), "ident": np.eye(P, dtype=np.float32),
    }
    nc = _bacc.Bacc("TRN2", target_bir_lowering=False, num_devices=1)
    arrays, args = {}, []
    for name, v in ins.items():
        v = np.ascontiguousarray(v)
        arrays[f"in_{name}_dram"] = v
        args.append(nc.dram_tensor(f"in_{name}_dram", v.shape, mybir.dt.from_np(v.dtype), kind="ExternalInput").ap())
    outs = [(1, N_PROMPT, D), (1, N_SAMPLE, D)]
    for i, shape in enumerate(outs):
        args.append(nc.dram_tensor(f"out_{i}_dram", shape, F32, kind="ExternalOutput").ap())
    encoder_layer_kernel(nc, *args)
    r = _run(nc, [arrays], core_ids=[0])
    return tuple(r.results[0][f"out_{i}_dram"] for i in range(len(outs)))
```

```python
from contextlib import ExitStack

import concourse.bass as bass
from concourse import mybir
import numpy as np

F32 = mybir.dt.float32
F32R = mybir.dt.float32r
U32 = mybir.dt.uint32
ALU = mybir.AluOpType
ACT = mybir.ActivationFunctionType
AX_X = mybir.AxisListType.X

P = 128
D = 1024
KD = D // P
N_PROMPT, N_SAMPLE = 1024, 512
TILES = (N_PROMPT + N_SAMPLE) // P
HD = 64
NH, NKV = 8, 2
AW = NH * HD
CW = D - AW
NC_CONV = CW // P
CONV_K = 31
PAD = CONV_K // 2
ROT_TILES = N_PROMPT // P
EPS = 1e-6
NE = 16
FF = 2 * D
CAP_P, CAP_S = 2 * N_PROMPT // NE, 2 * N_SAMPLE // NE
CAP = CAP_P + CAP_S

GROUPS = [(0, N_PROMPT // P, N_PROMPT, 0), (N_PROMPT // P, N_SAMPLE // P, N_SAMPLE, N_PROMPT + 2 * PAD)]
SLOT = N_PROMPT + N_SAMPLE + 4 * PAD
CHUNKS = 7
CCOLS = 256
SEL_ROWS = 48
SAMPLE_ROW = 32

COL_NORM, COL_TAP, COL_BIAS = 0, KD, KD + NC_CONV * CONV_K
COLS = COL_BIAS + NC_CONV
ROW_Q, ROW_K, ROW_LNG, ROW_LNB, ROW_MIX, ROW_FFN = 0, 2 * HD, 4 * HD, 4 * HD + CW, 4 * HD + 2 * CW, 4 * HD + 2 * CW + D
ROWS = ROW_FFN + D

EC = 24
CH = 2048
RAW_SLOTS, SPLIT_SLOTS = 4, 3
PAIRS = 8
TURN = 8


def encoder_layer_kernel(nc, x_prompt, x_sample, w_in, w_out, w_router, w_gate, w_up, w_down,
                         cols, rows, rotary, ident_in, y_prompt, y_sample):
    h_rows = nc.dram_tensor("h_rows", [N_PROMPT + N_SAMPLE, D], F32).ap()
    wi = w_in.rearrange("l (k p) n -> p (l k) n", p=P)
    wo = w_out.rearrange("l (k p) n -> p (l k) n", p=P)
    wr = w_router.rearrange("l (k p) n -> p (l k) n", p=P)
    gate_cols = w_gate.rearrange("l e (k p) f -> (l e) p k f", p=P)
    up_cols = w_up.rearrange("l e (k p) f -> (l e) p k f", p=P)
    down_rows = w_down.rearrange("l e (j k p) d -> (l e) j p k d", p=P, k=2)

    def x_rows(t):
        src, i = (x_prompt, t) if t < ROT_TILES else (x_sample, t - ROT_TILES)
        return src[0, i * P:(i + 1) * P, :]

    def y_rows(t):
        dst, i = (y_prompt, t) if t < ROT_TILES else (y_sample, t - ROT_TILES)
        return dst[0, i * P:(i + 1) * P, :]

    with ExitStack() as ctx:
        def sem(name):
            return ctx.enter_context(nc.semaphore(name))

        def in_region(stack, name, shape, dt):
            return stack.enter_context(nc.sbuf_tensor(name, shape, dt))

        psum = ctx.enter_context(nc.psum_tensor("psum", [P, 8, 512], F32))

        ident = in_region(ctx, "ident", [P, P], F32)
        colp = in_region(ctx, "colp", [P, COLS], F32)
        conv = in_region(ctx, "conv", [P, NC_CONV + 1, SLOT], F32)
        tok = in_region(ctx, "tok", [P, TILES, AW], F32)
        stat = in_region(ctx, "stat", [P, TILES, 16], F32)
        aff = in_region(ctx, "aff", [SEL_ROWS, N_PROMPT], F32)
        top = in_region(ctx, "top", [SEL_ROWS, CAP_P], F32)
        topi = in_region(ctx, "topi", [SEL_ROWS, CAP_P], U32)
        topf = in_region(ctx, "topf", [SEL_ROWS, CAP_P], F32)
        gates = in_region(ctx, "gates", [P, SEL_ROWS], F32)
        rows_p = in_region(ctx, "rows_p", [P, NE], U32)
        rows_s = in_region(ctx, "rows_s", [CAP_S, NE], U32)
        rows_sg = in_region(ctx, "rows_sg", [CAP_S, NE], U32)

        with ExitStack() as region:
            k_tok = in_region(region, "k_tok", [P, TILES, NKV * HD], F32)
            val = in_region(region, "val", [P, TILES, NKV * HD], F32)
            with ExitStack() as ra:
                hT_hi = in_region(ra, "hT_hi", [P, KD, N_PROMPT], F32R)
                hT_lo = in_region(ra, "hT_lo", [P, KD, N_PROMPT], F32R)
                wi_raw = in_region(ra, "wi_raw", [P, 2, KD // 2, CCOLS], F32)
                wi_hi = in_region(ra, "wi_hi", [P, 2, KD, CCOLS], F32R)
                wi_lo = in_region(ra, "wi_lo", [P, 2, KD, CCOLS], F32R)
                xin = in_region(ra, "xin", [P, 2, D], F32)
                rot_c = in_region(ra, "rot_c", [P, 2, ROT_TILES, HD], F32)
                rot_s = in_region(ra, "rot_s", [P, 2, ROT_TILES, HD], F32)
                qn = in_region(ra, "qn", [P, 2, CCOLS], F32)
                q_turn = in_region(ra, "q_turn", [P, CCOLS], F32)
                sq = in_region(ra, "sq", [P, CCOLS], F32)
                sig_a = in_region(ra, "sig_a", [P, 512], F32)
                hstat = in_region(ra, "hstat", [P, 2, 3, 4], F32)
            rot_src = tok[:, 0:2, :].rearrange("p a b -> p (a b)").rearrange("p (x t d) -> p x t d", x=2, d=HD)
            rope_gain = tok[:, 2, 0:4 * HD]
            with ExitStack() as rb:
                q_st = in_region(rb, "q_st", [P, NH, TILES * P], F32R)
                k_st = in_region(rb, "k_st", [P, NKV, 2, TILES * P], F32R)
                probs = in_region(rb, "probs", [P, 2, N_PROMPT], F32)
                probs_T = in_region(rb, "probs_T", [P, 2, N_PROMPT], F32)
                q_split = in_region(rb, "q_split", [P, NH, 2 * HD], F32)
                k_split = in_region(rb, "k_split", [P, NKV, 2, 2 * HD], F32)
                smx = in_region(rb, "smx", [P, 3, TILES * NH], F32)
        with ExitStack() as rc:
            wo_hi = in_region(rc, "wo_hi", [P, KD, D], F32R)
            wo_lo = in_region(rc, "wo_lo", [P, KD, D], F32R)
            rowp = in_region(rc, "rowp", [P, ROWS - ROW_LNG], F32)
            wo_raw = in_region(rc, "wo_raw", [P, 2, D], F32)
            wr_sb = in_region(rc, "wr_sb", [P, KD, NE], F32)
            cn = in_region(rc, "cn", [P, CW], F32)
            cs = in_region(rc, "cs", [P, CW], F32)
            mix = in_region(rc, "mix", [P, D], F32)
            mT_hi = in_region(rc, "mT_hi", [P, 2, D], F32R)
            mT_lo = in_region(rc, "mT_lo", [P, 2, D], F32R)
            xres = in_region(rc, "xres", [P, 2, D], F32)
            x1 = in_region(rc, "x1", [P, 2, D], F32)
            h2 = in_region(rc, "h2", [P, 2, D], F32)
            h2T = in_region(rc, "h2T", [P, D], F32)
            junk = in_region(rc, "junk", [P, D], F32)
            e16 = in_region(rc, "e16", [P, NE], F32)
            affp = in_region(rc, "affp", [P, 2, SEL_ROWS], F32)
            bst = in_region(rc, "bst", [P, 8], F32)
        with ExitStack() as re_:
            raw = in_region(re_, "raw", [P, RAW_SLOTS, CH], F32)
            w_hi = in_region(re_, "w_hi", [P, SPLIT_SLOTS, CH], F32R)
            w_lo = in_region(re_, "w_lo", [P, SPLIT_SLOTS, CH], F32R)
            xg_p = in_region(re_, "xg_p", [P, D], F32)
            xg_s = in_region(re_, "xg_s", [CAP_S, D], F32)
            xgT = in_region(re_, "xgT", [P, KD, 2 * CAP], F32R)
            hid_st = in_region(re_, "hid_st", [P, 2 * PAIRS, 2 * CAP], F32R)
            low_g = in_region(re_, "low_g", [P, 2, CAP], F32)
            low_u = in_region(re_, "low_u", [P, 2, CAP], F32)
            gsum = in_region(re_, "gsum", [P, 2, CAP], F32)
            usum = in_region(re_, "usum", [P, 2, CAP], F32)
            hid = in_region(re_, "hid", [P, 2, CAP], F32)
            out_lo = in_region(re_, "out_lo", [CAP_S, D], F32)
            o_p = in_region(re_, "o_p", [P, D], F32)
            o_s = in_region(re_, "o_s", [CAP_S, D], F32)
            cur_p = in_region(re_, "cur_p", [P, 1], U32)
            cur_sg = in_region(re_, "cur_sg", [CAP_S, 1], U32)
            put_p = in_region(re_, "put_p", [P, 1], U32)
            put_s = in_region(re_, "put_s", [CAP_S, 1], U32)
            cur_g = in_region(re_, "cur_g", [P, 2], F32)

        consts_in = sem("consts_in"); tables_in = sem("tables_in")
        pads_zero = sem("pads_zero"); rot_ready = sem("rot_ready")
        x_in = [sem(f"x_in{i}") for i in range(2)]
        x_sq = sem("x_sq"); x_var = sem("x_var"); x_std = sem("x_std"); x_rstd = sem("x_rstd"); x_norm = sem("x_norm")
        xT = sem("xT"); hT_h = sem("hT_h"); hT_l = sem("hT_l")
        wi_in = [sem(f"wi_in{i}") for i in range(2)]
        wi_h = sem("wi_h"); wi_l = sem("wi_l")
        pr_glu = sem("pr_glu"); glu_sig = sem("glu_sig"); glu_u = sem("glu_u")
        pr_tok = sem("pr_tok"); t_sq = sem("t_sq"); t_ssq = sem("t_ssq"); t_var = sem("t_var"); t_std = sem("t_std")
        t_rstd = sem("t_rstd"); t_norm = sem("t_norm"); rope_a = sem("rope_a"); rope_b = sem("rope_b"); rope_c = sem("rope_c")
        v_ok = sem("v_ok"); conv_tap = sem("conv_tap")
        qk_hi = sem("qk_hi"); qk_lo = sem("qk_lo"); qk_T = sem("qk_T"); q_st_ok = sem("q_st_ok"); k_st_ok = sem("k_st_ok")
        scored = sem("scored"); s_max = sem("s_max"); s_exp = sem("s_exp"); pT = sem("pT"); pT_ok = sem("pT_ok")
        pv = sem("pv"); o_rec = sem("o_rec"); attn_ok = sem("attn_ok")
        wo_in = [sem(f"wo_in{i}") for i in range(2)]
        wo_h = sem("wo_h"); wo_l = sem("wo_l"); rows_in = sem("rows_in")
        cT = sem("cT"); c_bn = sem("c_bn"); c_var = sem("c_var"); c_std = sem("c_std"); c_rstd = sem("c_rstd")
        c_cen = sem("c_cen"); c_ln = sem("c_ln"); c_act = sem("c_act"); m_sq = sem("m_sq"); m_var = sem("m_var"); m_std = sem("m_std")
        m_rstd = sem("m_rstd"); m_ok = sem("m_ok"); mT = sem("mT"); mT_h = sem("mT_h"); mT_l = sem("mT_l"); proj = sem("proj")
        xr_in = [sem(f"xr_in{i}") for i in range(2)]
        x1_ok = sem("x1_ok"); f_sq = sem("f_sq"); f_var = sem("f_var"); f_std = sem("f_std"); f_rstd = sem("f_rstd"); h2_ok = sem("h2_ok")
        y_out = [sem(f"y_out{i}") for i in range(2)]; h_out = [sem(f"h_out{i}") for i in range(2)]
        h2_T = sem("h2_T"); h2T_ok = sem("h2T_ok"); logit = sem("logit"); l_max = sem("l_max"); l_exp = sem("l_exp"); l_rec = sem("l_rec")
        a_ok = sem("a_ok"); a_T = sem("a_T"); a_sel = sem("a_sel")
        aff_fill = sem("aff_fill"); affp_zero = sem("affp_zero"); pick = sem("pick"); picked = sem("picked"); selT = sem("selT"); sel_ok = sem("sel_ok")
        raw_in = [sem(f"raw_in{i}") for i in range(RAW_SLOTS)]
        e_hi = sem("e_hi"); e_lo = sem("e_lo"); e_used = sem("e_used")
        dma_turn = sem("dma_turn"); cur_ok = sem("cur_ok"); put_ok = sem("put_ok"); gathered = sem("gathered"); xg_T = sem("xg_T"); xg_h = sem("xg_h"); xg_l = sem("xg_l")
        g_low = sem("g_low"); g_sum = sem("g_sum"); g_act = sem("g_act"); u_low = sem("u_low"); u_sum = sem("u_sum")
        h_mul = sem("h_mul"); h_hi = sem("h_hi"); h_lo = sem("h_lo")
        g_cur = sem("g_cur"); o_low = sem("o_low"); o_add = sem("o_add"); o_ok = sem("o_ok"); added = sem("added"); put_free = sem("put_free")

        GLU_BLOCKS = [(g, c, b) for g in range(2) for c in range(NC_CONV) for b in range(GROUPS[g][2] // 512)]
        glu_no = {key: n for n, key in enumerate(GLU_BLOCKS)}
        glu_by = [sum(k[0] < g for k in GLU_BLOCKS) for g in range(3)]
        TOK_STEPS = [(g, c, t) for g in range(2) for c in range(3) for t in range(GROUPS[g][0], GROUPS[g][0] + GROUPS[g][1])]
        tok_no = {key: n for n, key in enumerate(TOK_STEPS)}
        tok_by = [sum(k[0] < g for k in TOK_STEPS) for g in range(3)]
        UNITS = [(g, h, t) for g in range(2) for h in range(NH) for t in range(GROUPS[g][0], GROUPS[g][0] + GROUPS[g][1])]
        HALVES = [GROUPS[g][2] // 512 for g, _, _ in UNITS]
        half_no = [sum(HALVES[:n]) for n in range(len(UNITS) + 1)]
        TAPS = NC_CONV * CONV_K
        NU = len(UNITS)

        def glu_bank(n):
            return 4 + 2 * (n % 2)

        def tok_bank(n):
            return 4 + n % 4

        def flat(banks):
            return banks.rearrange("p a b -> p (a b)")

        def wi_multiplied(eng, n):
            g, c = n // CHUNKS, n % CHUNKS
            if c < NC_CONV:
                eng.wait_ge(pr_glu, glu_no[g, c, GROUPS[g][2] // 512 - 1] + 1)
            else:
                eng.wait_ge(pr_tok, tok_no[g, c - NC_CONV, GROUPS[g][0] + GROUPS[g][1] - 1] + 1)

        def y_stored(eng):
            for i in range(2):
                eng.wait_ge(y_out[i], 16 * TILES // 2)
                eng.wait_ge(h_out[i], 16 * TILES // 2)

        block = ctx.enter_context(nc.Block())

        @block.sync
        def _(sp):
            sp.dma_start(ident[:, :], ident_in).then_inc(consts_in, 16)
            sp.dma_start(colp[:, :], cols).then_inc(consts_in, 16)

            def load_x(t):
                if t >= 2:
                    sp.wait_ge(xT, t - 1)
                sp.dma_start(xin[:, t % 2, :], x_rows(t)).then_inc(x_in[t % 2], 16)

            def load_wi(g, c):
                n = CHUNKS * g + c
                for hf in range(2):
                    ks = slice(hf * KD // 2, (hf + 1) * KD // 2)
                    if n >= 1:
                        sp.wait_ge(wi_l, 2 * (n - 1) + hf + 1)
                    if c < NC_CONV:
                        c0, c1 = AW + 2 * NKV * HD + c * P, AW + 2 * NKV * HD + CW + c * P
                    else:
                        c0 = (c - NC_CONV) * CCOLS
                        c1 = c0 + P
                    sp.dma_start(wi_raw[:, hf, :, 0:P], wi[:, ks, c0:c0 + P]).then_inc(wi_in[hf], 16)
                    sp.dma_start(wi_raw[:, hf, :, P:CCOLS], wi[:, ks, c1:c1 + P]).then_inc(wi_in[hf], 16)

            load_x(0)
            load_x(1)
            load_wi(0, 0)
            sp.dma_start(rot_src, rotary).then_inc(tables_in, 16)
            sp.dma_start(rope_gain, rows[0, 0:4 * HD].partition_broadcast(P)).then_inc(tables_in, 16)
            for t in range(2, ROT_TILES):
                load_x(t)
            for c in range(1, CHUNKS):
                load_wi(0, c)
            for t in range(ROT_TILES, TILES):
                load_x(t)
            for c in range(CHUNKS):
                load_wi(1, c)

            sp.wait_ge(attn_ok, NU)
            sp.dma_start(rowp[:, :], rows[0, ROW_LNG:ROWS].partition_broadcast(P)).then_inc(rows_in, 16)
            sp.dma_start(wr_sb[:, :, :], wr).then_inc(rows_in, 16)
            for k in range(KD):
                if k >= 2:
                    sp.wait_ge(wo_l, k - 1)
                sp.dma_start(wo_raw[:, k % 2, :], wo[:, k, :]).then_inc(wo_in[k % 2], 16)
            for t in range(TILES + 1):
                if t < TILES:
                    if t >= 2:
                        sp.wait_ge(x1_ok, t - 1)
                    sp.dma_start(xres[:, t % 2, :], x_rows(t)).then_inc(xr_in[t % 2], 16)
                if t >= 1:
                    s = t - 1
                    sp.wait_ge(x1_ok, s + 1)
                    sp.dma_start(y_rows(s), x1[:, s % 2, :]).then_inc(y_out[s % 2], 16)
                    sp.wait_ge(h2_ok, s + 1)
                    sp.dma_start(h_rows[s * P:(s + 1) * P, :], h2[:, s % 2, :]).then_inc(h_out[s % 2], 16)

            sp.wait_ge(proj, TILES)

            def load_chunk(e, j):
                if j < 2 * PAIRS:
                    src = (gate_cols, up_cols)[j % 2][e, :, :, (j // 2) * CCOLS:(j // 2 + 1) * CCOLS]
                    dst = raw[:, j % RAW_SLOTS, :].rearrange("p (k f) -> p k f", k=KD)
                else:
                    src = down_rows[e, j - 2 * PAIRS]
                    dst = raw[:, j % RAW_SLOTS, :].rearrange("p (k d) -> p k d", k=2)
                sp.dma_start(dst, src).then_inc(raw_in[j % RAW_SLOTS], 16)

            for j in range(EC):
                if j >= RAW_SLOTS:
                    sp.wait_ge(e_lo, j - RAW_SLOTS + 1)
                load_chunk(0, j)
            with sp.Fori(1, NE) as e:
                for j in range(EC):
                    sp.wait_ge(proj, TILES)
                    sp.wait_ge(e_lo, e * EC + (j - RAW_SLOTS + 1))
                    load_chunk(e, j)
            y_stored(sp)
            sp.wait_ge(added, 32 * NE)

        @block.gpsimd
        def _(pool):
            pool.memset(conv[:, :, :], 0.0).then_inc(pads_zero, 1)
            pool.memset(aff[:, :], -1.0).then_inc(aff_fill, 1)

            pool.wait_ge(tables_in, 32)
            for x in range(2):
                for which, dst in ((0, rot_c), (1, rot_s)):
                    gain = rope_gain[:, (2 * x + which) * HD:(2 * x + which + 1) * HD]
                    pool.tensor_tensor(dst[:, x, :, :], rot_src[:, which, :, :],
                                       gain.unsqueeze(1).broadcast_to([P, ROT_TILES, HD]), ALU.mult).then_inc(rot_ready, 1)
            pool.wait_ge(rot_ready, 4)
            for tab in (rot_c, rot_s):
                pool.tensor_scalar(tab[:, 0, :, :], tab[:, 0, :, :], float(HD) ** -0.5, None, ALU.mult).then_inc(rot_ready, 1)
            pool.wait_ge(rot_ready, 6)

            for n, (g, c, t) in enumerate(TOK_STEPS):
                heads = 4 if c < 2 else NKV
                w, r, x = heads * HD, t - GROUPS[g][0], (0 if c < 2 else 1)

                def by_head(table):
                    return table[:, x, r, :].unsqueeze(1).broadcast_to([P, heads, HD])

                s_pairs = by_head(rot_s).rearrange("p h (d two) -> p h d two", two=2)
                src = qn[:, n % 2, 0:w].rearrange("p (h d) -> p h d", h=heads)
                pair = qn[:, n % 2, 0:w].rearrange("p (h d two) -> p h d two", h=heads, two=2)
                turn = q_turn[:, 0:w].rearrange("p (h d two) -> p h d two", h=heads, two=2)
                dst = tok[:, t, c * CCOLS:(c + 1) * CCOLS] if c < 2 else k_tok[:, t, :]
                pool.wait_ge(t_norm, n + 1)
                if n >= 1:
                    pool.wait_ge(rope_c, n)
                pool.tensor_tensor(turn[:, :, :, 0], pair[:, :, :, 1], s_pairs[:, :, :, 0], ALU.mult)
                pool.tensor_tensor(turn[:, :, :, 1], pair[:, :, :, 0], s_pairs[:, :, :, 1], ALU.mult).then_inc(rope_a, 1)
                pool.wait_ge(rope_a, n + 1)
                pool.tensor_tensor(src, src, by_head(rot_c), ALU.mult).then_inc(rope_b, 1)
                pool.wait_ge(rope_b, n + 1)
                pool.tensor_tensor(dst, qn[:, n % 2, 0:w], q_turn[:, 0:w], ALU.add).then_inc(rope_c, 1)

            pool.wait_ge(sel_ok, 4)
            y_stored(pool)

            def gather(e):
                pool.tensor_copy(cur_p[:, :], rows_p[:, bass.ds(e, 1)]).then_inc(cur_ok, 1)
                pool.tensor_copy(cur_sg[:, :], rows_sg[:, bass.ds(e, 1)]).then_inc(cur_ok, 1)
                pool.wait_ge(cur_ok, 2 * e + 2)
                pool.sem_inc(dma_turn, 1)
                pool.indirect_dma_start(xg_p[:, :], None, h_rows, bass.IndirectOffsetOnAxis(ap=cur_p[:, :], axis=0)
                                        ).then_inc(gathered, 16)
                pool.indirect_dma_start(xg_s[:, :], None, h_rows, bass.IndirectOffsetOnAxis(ap=cur_sg[:, :], axis=0)
                                        ).then_inc(gathered, 16)

            def scatter(e):
                pool.tensor_copy(put_p[:, :], rows_p[:, bass.ds(e, 1)]).then_inc(put_ok, 1)
                pool.tensor_copy(put_s[:, :], rows_s[:, bass.ds(e, 1)]).then_inc(put_ok, 1)
                pool.wait_ge(put_ok, 2 * e + 2)
                pool.wait_ge(o_ok, 2 * e + 3)
                pool.sem_inc(dma_turn, 1)
                pool.indirect_dma_start(y_prompt[0], bass.IndirectOffsetOnAxis(ap=put_p[:, :], axis=0), o_p[:, :], None,
                                        compute_op=ALU.add).then_inc(added, 16)
                pool.indirect_dma_start(y_sample[0], bass.IndirectOffsetOnAxis(ap=put_s[:, :], axis=0), o_s[:, :], None,
                                        compute_op=ALU.add).then_inc(added, 16)
                pool.wait_ge(added, 32 * e + 32)
                pool.sem_inc(put_free, 1)

            pool.sem_inc(put_free, 1)
            gather(0)
            with pool.Fori(0, NE - 1) as e:
                pool.wait_ge(xg_T, e + 1)
                gather(e + 1)
                scatter(e)
            scatter(NE - 1)

        @block.scalar
        def _(act):
            act.wait_ge(consts_in, 32)

            def square_x(t):
                act.wait_ge(x_in[t % 2], 16 * (t // 2 + 1))
                act.activation(flat(psum[:, 2:4, :]), xin[:, t % 2, :], ACT.Square,
                               accum_out=stat[:, t, 0:1]).then_inc(x_sq, 1)
                act.wait_ge(x_var, t + 1)
                act.activation(stat[:, t, 2:3], stat[:, t, 1:2], ACT.Sqrt).then_inc(x_std, 1)

            def split_x(g, t):
                i = t - GROUPS[g][0]
                act.wait_ge(xT, t + 1)
                act.copy(hT_hi[:, :, i * P:(i + 1) * P],
                         psum[:, 0:2, :].rearrange("p a (k b) -> p (a k) b", k=4)).then_inc(hT_h, 1)

            def split_wi(g, c):
                n = CHUNKS * g + c
                if n >= 2:
                    wi_multiplied(act, n - 2)
                for hf in range(2):
                    act.wait_ge(wi_in[hf], 32 * (n + 1))
                    for k in range(KD // 2):
                        kk = hf * KD // 2 + k
                        last = act.activation(wi_hi[:, n % 2, kk, :], wi_raw[:, hf, k, :], ACT.Copy,
                                              scale=colp[:, COL_NORM + kk:COL_NORM + kk + 1])
                    last.then_inc(wi_h, 1)

            for g in range(2):
                t0, nt = GROUPS[g][0], GROUPS[g][1]
                square_x(t0)
                if g == 1:
                    wi_multiplied(act, CHUNKS - 1)
                for t in range(t0, t0 + nt):
                    if t + 1 < t0 + nt:
                        square_x(t + 1)
                    split_x(g, t)
                split_wi(g, 0)
                for c in range(NC_CONV):
                    split_wi(g, c + 1)
                    for b in range(GROUPS[g][2] // 512):
                        n = glu_no[g, c, b]
                        act.wait_ge(pr_glu, n + 1)
                        if n >= 1:
                            act.wait_ge(glu_u, n)
                        act.activation(sig_a[:, :], psum[:, glu_bank(n) + 1, :], ACT.Sigmoid).then_inc(glu_sig, 1)
                for c in range(3):
                    if c + 1 < 3:
                        split_wi(g, NC_CONV + c + 1)
                    for t in range(t0, t0 + nt):
                        n = tok_no[g, c, t]
                        bank = tok_bank(n)
                        w = CCOLS if c < 2 else NKV * HD
                        act.wait_ge(pr_tok, n + 1)
                        if n >= 1:
                            act.wait_ge(t_ssq, n)
                        act.activation(sq[:, 0:w], psum[:, bank, 0:w], ACT.Square).then_inc(t_sq, 1)
                        if c == 2:
                            act.copy(val[:, t, :], psum[:, bank, w:CCOLS]).then_inc(v_ok, 1)
                        act.wait_ge(t_var, n + 1)
                        act.activation(hstat[:, n % 2, 1, 0:w // HD], hstat[:, n % 2, 0, 0:w // HD], ACT.Sqrt).then_inc(t_std, 1)

            act.wait_ge(rope_c, len(TOK_STEPS))
            wi_multiplied(act, 2 * CHUNKS - 1)
            for t in range(TILES):
                if t >= 1:
                    act.wait_ge(qk_T, t)
                act.copy(q_split[:, :, 0:HD].bitcast(F32R), tok[:, t, :].rearrange("p (h d) -> p h d", h=NH)).then_inc(qk_hi, 1)
                kt = k_tok[:, t, :].rearrange("p (h d) -> p h d", h=NKV)
                act.copy(k_split[:, :, 0, 0:HD].bitcast(F32R), kt).then_inc(qk_hi, 1)
                act.copy(k_split[:, :, 0, HD:2 * HD].bitcast(F32R), kt).then_inc(qk_hi, 1)
                act.wait_ge(qk_T, t + 1)
                act.copy(q_st[:, :, t * P:(t + 1) * P],
                         psum[:, 0:2, :].rearrange("p a (h b) -> p (a h) b", h=4)).then_inc(q_st_ok, 1)

            def exp_unit(u):
                n = GROUPS[UNITS[u][0]][2]
                act.wait_ge(s_max, u + 1)
                if u >= 2:
                    act.wait_ge(pT, half_no[u - 1])
                act.activation(probs[:, u % 2, 0:n], flat(psum[:, 2 * (u % 2):2 * (u % 2) + 2, :])[:, 0:n], ACT.Exp,
                               bias=smx[:, 0, u:u + 1], accum_out=smx[:, 1, u:u + 1]).then_inc(s_exp, 1)

            exp_unit(0)
            for u in range(NU):
                if u >= 2:
                    act.wait_ge(pv, u - 1)
                for hf in range(HALVES[u]):
                    m = half_no[u] + hf
                    act.wait_ge(pT, m + 1)
                    act.copy(probs_T[:, u % 2, hf * 512:(hf + 1) * 512], psum[:, 4 + m % 3, :]).then_inc(pT_ok, 1)
                if u + 1 < NU:
                    exp_unit(u + 1)

            act.wait_ge(pv, NU)
            act.wait_ge(attn_ok, NU)
            for k in range(KD):
                act.wait_ge(wo_in[k % 2], 16 * (k // 2 + 1))
                act.copy(wo_hi[:, k, :], wo_raw[:, k % 2, :]).then_inc(wo_h, 1)
            for s in range(TILES + 4):
                if s < TILES:
                    act.wait_ge(c_var, s + 1)
                    act.activation(stat[:, s, 5:6], stat[:, s, 4:5], ACT.Sqrt).then_inc(c_std, 1)
                    act.wait_ge(c_ln, s + 1)
                    if s >= 1:
                        act.wait_ge(m_ok, 2 * s)
                    act.activation(cs[:, :], cn[:, :], ACT.Silu).then_inc(c_act, 1)
                    act.wait_ge(c_act, s + 1)
                    if s >= 3:
                        act.wait_ge(f_sq, s - 2)
                    act.activation(junk[:, 0:CW], cs[:, :], ACT.Square, accum_out=stat[:, s, 7:8]).then_inc(m_sq, 1)
                    act.activation(junk[:, CW:D], tok[:, s, :], ACT.Square, accum_out=stat[:, s, 6:7]).then_inc(m_sq, 1)
                    act.wait_ge(m_var, s + 1)
                    act.activation(stat[:, s, 10:12], stat[:, s, 8:10], ACT.Sqrt).then_inc(m_std, 1)
                if 0 <= s - 1 < TILES:
                    t = s - 1
                    act.wait_ge(mT, t + 1)
                    if t >= 2:
                        act.wait_ge(proj, t - 1)
                    act.copy(mT_hi[:, t % 2, :], flat(psum[:, 1:3, :])).then_inc(mT_h, 1)
                if 0 <= s - 4 < TILES:
                    t = s - 4
                    act.wait_ge(l_max, t + 1)
                    if t >= 1:
                        act.wait_ge(a_ok, t)
                    act.activation(e16[:, :], psum[:, 7, 0:NE], ACT.Exp, bias=stat[:, t, 14:15],
                                   accum_out=stat[:, t, 15:16]).then_inc(l_exp, 1)
                if 0 <= s - 2 < TILES:
                    t = s - 2
                    act.wait_ge(x1_ok, t + 1)
                    act.wait_ge(m_sq, 2 * min(s + 1, TILES))
                    if t >= 1:
                        act.wait_ge(f_sq, t)
                    act.activation(junk[:, :], x1[:, t % 2, :], ACT.Square, accum_out=stat[:, t, 0:1]).then_inc(f_sq, 1)
                    act.wait_ge(f_var, t + 1)
                    act.activation(stat[:, t, 2:3], stat[:, t, 1:2], ACT.Sqrt).then_inc(f_std, 1)
                if 0 <= s - 3 < TILES:
                    t = s - 3
                    act.wait_ge(h2_T, t + 1)
                    if t >= 1:
                        act.wait_ge(logit, t)
                    act.copy(h2T[:, :], flat(psum[:, 5:7, :])).then_inc(h2T_ok, 1)

            def hi_chunk(e, j, first=False):
                act.wait_ge(raw_in[j % RAW_SLOTS], e * (EC // RAW_SLOTS * 16) + (j // RAW_SLOTS + 1) * 16)
                if not first:
                    act.wait_ge(e_used, e * EC + (j - SPLIT_SLOTS + 1))
                act.copy(w_hi[:, j % SPLIT_SLOTS, :], raw[:, j % RAW_SLOTS, :]).then_inc(e_hi, 1)

            def low_columns(e, c):
                m = c // 2
                act.wait_ge(e_used, e * EC + (c + 1))
                if c % 2 == 0:
                    act.wait_ge(g_sum, e * PAIRS + m)
                    act.copy(low_g[:, :, :], psum[:, 0:2, CAP:2 * CAP]).then_inc(g_low, 1)
                else:
                    act.wait_ge(u_sum, e * PAIRS + m)
                    act.copy(low_u[:, :, :], psum[:, 2:4, CAP:2 * CAP]).then_inc(u_low, 1)

            def gate_act(e, m):
                act.wait_ge(g_sum, e * PAIRS + (m + 1))
                act.activation(gsum[:, :, :], gsum[:, :, :], ACT.Silu).then_inc(g_act, 1)

            def hid_high(e, m):
                act.wait_ge(h_mul, e * PAIRS + (m + 1))
                act.copy(hid_st[:, 2 * m:2 * m + 2, 0:CAP], hid[:, :, :]).then_inc(h_hi, 1)

            def gathered_high(e):
                act.wait_ge(xg_T, e + 1)
                act.copy(xgT[:, :, 0:CAP].rearrange("p (a b) c -> p a b c", a=4),
                         psum[:, 0:4, 0:2 * CAP].rearrange("p a (b c) -> p a b c", b=2)).then_inc(xg_h, 1)

            def out_low(e):
                act.wait_ge(e_used, e * EC + EC)
                act.wait_ge(o_add, e + 1)
                act.copy(out_lo[:, :], flat(psum[CAP_S:2 * CAP_S, 6:8, :])).then_inc(o_low, 1)

            def out_rows(e):
                act.wait_ge(g_cur, 2 * e + 2)
                act.wait_ge(put_free, e + 1)
                act.activation(o_p[:, :], flat(psum[:, 4:6, :]), ACT.Copy, scale=cur_g[:, 0:1]).then_inc(o_ok, 1)
                act.wait_ge(o_add, e + 2)
                act.activation(o_s[:, :], o_s[:, :], ACT.Copy, scale=cur_g[0:CAP_S, 1:2]).then_inc(o_ok, 1)

            def step(e, j, first=False):
                c = j - 3
                if 0 <= c < 2 * PAIRS:
                    low_columns(e, c)
                hi_chunk(e, j, first)
                if 0 <= c < 2 * PAIRS and c % 2 == 0:
                    gate_act(e, c // 2)
                if 0 <= c < 2 * PAIRS and c % 2 == 1:
                    hid_high(e, c // 2)

            def late(e, last):
                for j in range(TURN, EC):
                    step(e, j)
                    if j == 20 and not last:
                        gathered_high(e + 1)

            act.sem_inc(o_ok, 1)
            act.wait_ge(proj, TILES)
            for j in range(SPLIT_SLOTS):
                step(0, j, first=True)
            gathered_high(0)
            for j in range(SPLIT_SLOTS, TURN):
                step(0, j)
            with act.Fori(0, NE - 1) as e:
                late(e, False)
                for j in range(TURN):
                    step(e + 1, j)
                    if j == 3:
                        out_low(e)
                out_rows(e)
            late(NE - 1, True)
            out_low(NE - 1)
            out_rows(NE - 1)

        @block.vector
        def _(dve):
            conv_done = [0]

            def conv_run(n):
                for w in range(conv_done[0], min(conv_done[0] + n, 2 * TAPS)):
                    g, c, k = w // TAPS, w % TAPS // CONV_K, w % CONV_K
                    T, base = GROUPS[g][2], GROUPS[g][3]
                    out = conv[:, c, base + PAD:base + PAD + T]
                    u = conv[:, c + 1, base + k:base + k + T]
                    tap = colp[:, COL_TAP + c * CONV_K + k:COL_TAP + c * CONV_K + k + 1]
                    if k == 0:
                        dve.wait_ge(glu_u, glu_no[g, c, T // 512 - 1] + 1)
                        if w:
                            dve.wait_ge(conv_tap, w)
                        dve.tensor_scalar(out, u, tap, colp[:, COL_BIAS + c:COL_BIAS + c + 1], ALU.mult, ALU.add
                                          ).then_inc(conv_tap, 1)
                    else:
                        dve.wait_ge(conv_tap, w)
                        dve.scalar_tensor_tensor(out=out, in0=u, scalar=tap, in1=out, op0=ALU.mult, op1=ALU.add
                                                 ).then_inc(conv_tap, 1)
                    conv_done[0] = w + 1

            dve.wait_ge(consts_in, 32)
            dve.wait_ge(pads_zero, 1)

            def norm_x(t):
                dve.wait_ge(x_sq, t + 1)
                dve.tensor_scalar(stat[:, t, 1:2], stat[:, t, 0:1], 1.0 / D, EPS, ALU.mult, ALU.add).then_inc(x_var, 1)
                dve.wait_ge(x_std, t + 1)
                dve.reciprocal(stat[:, t, 3:4], stat[:, t, 2:3]).then_inc(x_rstd, 1)
                dve.wait_ge(x_rstd, t + 1)
                dve.tensor_scalar(xin[:, t % 2, :], xin[:, t % 2, :], stat[:, t, 3:4], None, ALU.mult).then_inc(x_norm, 1)

            def split_x(g, t):
                i = t - GROUPS[g][0]
                dve.wait_ge(hT_h, t + 1)
                dve.tensor_tensor(hT_lo[:, :, i * P:(i + 1) * P],
                                  psum[:, 0:2, :].rearrange("p a (k b) -> p (a k) b", k=4),
                                  hT_hi[:, :, i * P:(i + 1) * P].bitcast(F32), ALU.subtract).then_inc(hT_l, 1)

            def split_wi(g, c):
                n = CHUNKS * g + c
                for hf in range(2):
                    dve.wait_ge(wi_h, 2 * n + hf + 1)
                    for k in range(KD // 2):
                        kk = hf * KD // 2 + k
                        last = dve.scalar_tensor_tensor(
                            out=wi_lo[:, n % 2, kk, :], in0=wi_raw[:, hf, k, :],
                            scalar=colp[:, COL_NORM + kk:COL_NORM + kk + 1],
                            in1=wi_hi[:, n % 2, kk, :].bitcast(F32), op0=ALU.mult, op1=ALU.subtract)
                    last.then_inc(wi_l, 1)

            for g in range(2):
                t0, nt, T, base = GROUPS[g]
                norm_x(t0)
                for t in range(t0, t0 + nt):
                    if t + 1 < t0 + nt:
                        norm_x(t + 1)
                    split_x(g, t)
                split_wi(g, 0)
                for c in range(NC_CONV):
                    split_wi(g, c + 1)
                    for b in range(T // 512):
                        n = glu_no[g, c, b]
                        dve.wait_ge(glu_sig, n + 1)
                        dve.tensor_tensor(conv[:, c + 1, base + PAD + b * 512:base + PAD + (b + 1) * 512],
                                          psum[:, glu_bank(n), :], sig_a[:, :], ALU.mult).then_inc(glu_u, 1)
                        if c >= 1 or g == 1:
                            conv_run(6)
                for c in range(3):
                    if c + 1 < 3:
                        split_wi(g, NC_CONV + c + 1)
                    for t in range(t0, t0 + nt):
                        n = tok_no[g, c, t]
                        heads = 4 if c < 2 else NKV
                        w = heads * HD
                        hs = hstat[:, n % 2, :, 0:heads]
                        dve.wait_ge(t_sq, n + 1)
                        dve.tensor_reduce(hs[:, 2, :], sq[:, 0:w].rearrange("p (h d) -> p h d", h=heads), AX_X, ALU.add
                                          ).then_inc(t_ssq, 1)
                        dve.wait_ge(t_ssq, n + 1)
                        dve.tensor_scalar(hs[:, 0, :], hs[:, 2, :], 1.0 / HD, EPS, ALU.mult, ALU.add).then_inc(t_var, 1)
                        conv_run(1)
                        dve.wait_ge(t_std, n + 1)
                        dve.reciprocal(hs[:, 2, :], hs[:, 1, :]).then_inc(t_rstd, 1)
                        dve.wait_ge(t_rstd, n + 1)
                        if n >= 2:
                            dve.wait_ge(rope_c, n - 1)
                        dve.tensor_tensor(qn[:, n % 2, 0:w].rearrange("p (h d) -> p h d", h=heads),
                                          psum[:, tok_bank(n), 0:w].rearrange("p (h d) -> p h d", h=heads),
                                          hs[:, 2, :].unsqueeze(2).broadcast_to([P, heads, HD]), ALU.mult).then_inc(t_norm, 1)

            for t in range(TILES):
                conv_run(1)
                dve.wait_ge(qk_hi, 3 * t + 3)
                dve.tensor_tensor(q_split[:, :, HD:2 * HD].bitcast(F32R), tok[:, t, :].rearrange("p (h d) -> p h d", h=NH),
                                  q_split[:, :, 0:HD], ALU.subtract).then_inc(qk_lo, 1)
                kt = k_tok[:, t, :].rearrange("p (h d) -> p h d", h=NKV)
                for hf in range(2):
                    dve.tensor_tensor(k_split[:, :, 1, hf * HD:(hf + 1) * HD].bitcast(F32R), kt,
                                      k_split[:, :, 0, 0:HD], ALU.subtract).then_inc(qk_lo, 1)
                dve.wait_ge(qk_T, t + 1)
                dve.tensor_copy(k_st[:, :, :, t * P:(t + 1) * P],
                                psum[:, 2, :].rearrange("p (h x b) -> p h x b", h=NKV, x=2)).then_inc(k_st_ok, 1)

            def max_unit(u):
                n = GROUPS[UNITS[u][0]][2]
                dve.wait_ge(scored, u + 1)
                dve.tensor_reduce(smx[:, 0, u:u + 1], flat(psum[:, 2 * (u % 2):2 * (u % 2) + 2, :])[:, 0:n],
                                  AX_X, ALU.max, negate=True).then_inc(s_max, 1)

            def rows_unit(u):
                g, h, t = UNITS[u]
                kv = h // (NH // NKV)
                dve.wait_ge(s_exp, u + 1)
                dve.reciprocal(smx[:, 2, u:u + 1], smx[:, 1, u:u + 1]).then_inc(o_rec, 1)
                dve.wait_ge(o_rec, u + 1)
                dve.wait_ge(pv, u + 1)
                dve.tensor_scalar(tok[:, t, h * HD:(h + 1) * HD], psum[:, 7, kv * HD:(kv + 1) * HD],
                                  smx[:, 2, u:u + 1], None, ALU.mult).then_inc(attn_ok, 1)

            max_unit(0)
            for u in range(NU):
                if u >= 2:
                    rows_unit(u - 2)
                if u + 1 < NU:
                    max_unit(u + 1)
                conv_run((3 if conv_done[0] >= TAPS else 2 - u % 2) if HALVES[u] == 2 else 1)
            rows_unit(NU - 2)
            rows_unit(NU - 1)
            conv_run(2 * TAPS)

            dve.wait_ge(attn_ok, NU)
            dve.memset(affp[:, :, :], 0.0).then_inc(affp_zero, 1)
            for k in range(KD):
                dve.wait_ge(wo_h, k + 1)
                dve.tensor_tensor(wo_lo[:, k, :], wo_raw[:, k % 2, :], wo_hi[:, k, :].bitcast(F32), ALU.subtract
                                  ).then_inc(wo_l, 1)
            dve.wait_ge(rows_in, 32)
            lng, lnb = rowp[:, 0:CW], rowp[:, CW:2 * CW]
            mix_gain = rowp[:, ROW_MIX - ROW_LNG:ROW_MIX - ROW_LNG + D]
            ffn_gain = rowp[:, ROW_FFN - ROW_LNG:ROW_FFN - ROW_LNG + D]
            for s in range(TILES + 4):
                if s < TILES:
                    dve.wait_ge(cT, s + 1)
                    dve.bn_stats(bst[:, 0:6], psum[:, 0, :]).then_inc(c_bn, 1)
                    dve.wait_ge(c_bn, 2 * s + 1)
                    dve.bn_aggr(bst[:, 6:8], bst[:, 0:6]).then_inc(c_bn, 1)
                    dve.wait_ge(c_bn, 2 * s + 2)
                    dve.tensor_scalar(stat[:, s, 4:5], bst[:, 7:8], EPS, None, ALU.add).then_inc(c_var, 1)
                    if s >= 1:
                        dve.wait_ge(c_act, s)
                    dve.scalar_tensor_tensor(out=cn[:, :], in0=psum[:, 0, :], scalar=bst[:, 6:7], in1=lng,
                                             op0=ALU.subtract, op1=ALU.mult).then_inc(c_cen, 1)
                    dve.wait_ge(c_std, s + 1)
                    dve.reciprocal(stat[:, s, 5:6], stat[:, s, 5:6]).then_inc(c_rstd, 1)
                    dve.wait_ge(c_rstd, s + 1)
                    dve.wait_ge(c_cen, s + 1)
                    dve.scalar_tensor_tensor(out=cn[:, :], in0=cn[:, :], scalar=stat[:, s, 5:6], in1=lnb,
                                             op0=ALU.mult, op1=ALU.add).then_inc(c_ln, 1)
                    dve.wait_ge(m_sq, 2 * s + 2)
                    dve.tensor_scalar(stat[:, s, 8:10], stat[:, s, 6:8], 1.0 / AW, EPS, ALU.mult, ALU.add).then_inc(m_var, 1)
                    dve.wait_ge(m_std, s + 1)
                    dve.reciprocal(stat[:, s, 12:14], stat[:, s, 10:12]).then_inc(m_rstd, 1)
                    dve.wait_ge(m_rstd, s + 1)
                    if s >= 1:
                        dve.wait_ge(mT, s)
                    dve.scalar_tensor_tensor(out=mix[:, 0:AW], in0=tok[:, s, :], scalar=stat[:, s, 12:13],
                                             in1=mix_gain[:, 0:AW], op0=ALU.mult, op1=ALU.mult).then_inc(m_ok, 1)
                    dve.scalar_tensor_tensor(out=mix[:, AW:D], in0=cs[:, :], scalar=stat[:, s, 13:14],
                                             in1=mix_gain[:, AW:D], op0=ALU.mult, op1=ALU.mult).then_inc(m_ok, 1)
                if 0 <= s - 1 < TILES:
                    t = s - 1
                    dve.wait_ge(mT_h, t + 1)
                    dve.tensor_tensor(mT_lo[:, t % 2, :], flat(psum[:, 1:3, :]), mT_hi[:, t % 2, :].bitcast(F32),
                                      ALU.subtract).then_inc(mT_l, 1)
                if 0 <= s - 4 < TILES:
                    t = s - 4
                    dve.wait_ge(logit, t + 1)
                    dve.tensor_reduce(stat[:, t, 14:15], psum[:, 7, 0:NE], AX_X, ALU.max, negate=True).then_inc(l_max, 1)
                    dve.wait_ge(l_exp, t + 1)
                    dve.reciprocal(stat[:, t, 15:16], stat[:, t, 15:16]).then_inc(l_rec, 1)
                    dve.wait_ge(l_rec, t + 1)
                    if t >= 1:
                        dve.wait_ge(a_T, t)
                    else:
                        dve.wait_ge(affp_zero, 1)
                    place = affp[:, 0, 0:NE] if t < ROT_TILES else affp[:, 1, SAMPLE_ROW:SEL_ROWS]
                    dve.tensor_scalar(place, e16[:, :], stat[:, t, 15:16], None, ALU.mult).then_inc(a_ok, 1)
                if 0 <= s - 2 < TILES:
                    t = s - 2
                    dve.wait_ge(proj, t + 1)
                    dve.wait_ge(xr_in[t % 2], 16 * (t // 2 + 1))
                    if t >= 2:
                        dve.wait_ge(y_out[t % 2], 16 * (t // 2))
                        dve.wait_ge(f_sq, t - 1)
                    dve.tensor_tensor(x1[:, t % 2, :], flat(psum[:, 3:5, :]), xres[:, t % 2, :], ALU.add).then_inc(x1_ok, 1)
                    dve.wait_ge(f_sq, t + 1)
                    dve.tensor_scalar(stat[:, t, 1:2], stat[:, t, 0:1], 1.0 / D, EPS, ALU.mult, ALU.add).then_inc(f_var, 1)
                    dve.wait_ge(f_std, t + 1)
                    dve.reciprocal(stat[:, t, 3:4], stat[:, t, 2:3]).then_inc(f_rstd, 1)
                    dve.wait_ge(f_rstd, t + 1)
                    if t >= 2:
                        dve.wait_ge(h_out[t % 2], 16 * (t // 2))
                        dve.wait_ge(h2_T, t - 1)
                    dve.scalar_tensor_tensor(out=h2[:, t % 2, :], in0=x1[:, t % 2, :], scalar=stat[:, t, 3:4],
                                             in1=ffn_gain, op0=ALU.mult, op1=ALU.mult).then_inc(h2_ok, 1)
                if 0 <= s - 4 < TILES:
                    t = s - 4
                    dve.wait_ge(a_T, t + 1)
                    if t == 0:
                        dve.wait_ge(aff_fill, 1)
                    if t < ROT_TILES:
                        dve.tensor_copy(aff[0:NE, t * P:(t + 1) * P], psum[0:NE, 7, P:2 * P]).then_inc(a_sel, 1)
                    else:
                        i = t - ROT_TILES
                        dve.tensor_copy(aff[SAMPLE_ROW:SEL_ROWS, i * P:(i + 1) * P],
                                        psum[SAMPLE_ROW:SEL_ROWS, 7, P:2 * P]).then_inc(a_sel, 1)

            dve.wait_ge(a_sel, TILES)
            for r in range(CAP_P // 8):
                v, vi = top[:, 8 * r:8 * r + 8], topi[:, 8 * r:8 * r + 8]
                if r:
                    dve.wait_ge(pick, 3 * r)
                dve.max(v, aff[:, :]).then_inc(pick, 1)
                dve.wait_ge(pick, 3 * r + 1)
                dve.max_index(vi, v, aff[:, :]).then_inc(pick, 1)
                dve.match_replace(aff[:, :], v, aff[:, :], -2.0).then_inc(pick, 1)
            dve.wait_ge(pick, 3 * CAP_P // 8)
            dve.tensor_copy(topf[:, :], topi[:, :]).then_inc(picked, 1)
            dve.wait_ge(selT, 1)
            dve.tensor_copy(gates[:, :], psum[:, 0, 0:SEL_ROWS]).then_inc(sel_ok, 1)
            dve.tensor_copy(rows_p[:, :], psum[:, 0, 64:64 + NE]).then_inc(sel_ok, 1)
            dve.tensor_copy(rows_s[:, :], psum[0:CAP_S, 0, 64 + SAMPLE_ROW:64 + SEL_ROWS]).then_inc(sel_ok, 1)
            dve.tensor_scalar(rows_sg[:, :], psum[0:CAP_S, 0, 64 + SAMPLE_ROW:64 + SEL_ROWS], float(N_PROMPT), None,
                              ALU.add).then_inc(sel_ok, 1)

            def lo_chunk(e, j):
                dve.wait_ge(e_hi, e * EC + (j + 1))
                dve.tensor_tensor(w_lo[:, j % SPLIT_SLOTS, :], raw[:, j % RAW_SLOTS, :],
                                  w_hi[:, j % SPLIT_SLOTS, :].bitcast(F32), ALU.subtract).then_inc(e_lo, 1)

            def gate_sum(e, m):
                dve.wait_ge(g_low, e * PAIRS + (m + 1))
                dve.wait_ge(h_mul, e * PAIRS + m)
                dve.tensor_tensor(gsum[:, :, :], psum[:, 0:2, 0:CAP], low_g[:, :, :], ALU.add).then_inc(g_sum, 1)

            def up_sum(e, m):
                dve.wait_ge(u_low, e * PAIRS + (m + 1))
                dve.wait_ge(h_mul, e * PAIRS + m)
                dve.tensor_tensor(usum[:, :, :], psum[:, 2:4, 0:CAP], low_u[:, :, :], ALU.add).then_inc(u_sum, 1)
                dve.wait_ge(g_act, e * PAIRS + (m + 1))
                dve.wait_ge(u_sum, e * PAIRS + (m + 1))
                dve.wait_ge(h_lo, 2 * (e * PAIRS + m))
                dve.tensor_tensor(hid[:, :, :], usum[:, :, :], gsum[:, :, :], ALU.mult).then_inc(h_mul, 1)

            def hid_low(e, m):
                dve.wait_ge(h_hi, e * PAIRS + (m + 1))
                st = hid_st[:, 2 * m:2 * m + 2, :]
                dve.tensor_tensor(st[:, :, CAP:CAP + CAP_S], hid[:, :, CAP_P:CAP], st[:, :, CAP_P:CAP].bitcast(F32),
                                  ALU.subtract).then_inc(h_lo, 1)
                dve.tensor_tensor(st[:, :, CAP + CAP_S:2 * CAP], hid[:, :, 0:CAP_P], st[:, :, 0:CAP_P].bitcast(F32),
                                  ALU.subtract).then_inc(h_lo, 1)

            def gathered_low(e):
                dve.wait_ge(xg_h, e + 1)
                halves = xgT[:, :, :].rearrange("p (a b) c -> p a b c", a=4)
                dve.tensor_tensor(halves[:, :, :, CAP:2 * CAP], psum[:, 0:4, 0:2 * CAP].rearrange("p a (b c) -> p a b c", b=2),
                                  halves[:, :, :, 0:CAP].bitcast(F32), ALU.subtract).then_inc(xg_l, 1)

            def out_add(e):
                dve.wait_ge(o_low, e + 1)
                dve.wait_ge(put_free, e + 1)
                dve.tensor_tensor(o_s[:, :], flat(psum[0:CAP_S, 6:8, :]), out_lo[:, :], ALU.add).then_inc(o_add, 1)

            def gates_of(e):
                dve.wait_ge(o_ok, 2 * e + 1)
                dve.tensor_copy(cur_g[:, 0:1], gates[:, bass.ds(e, 1)]).then_inc(g_cur, 1)
                dve.tensor_copy(cur_g[0:CAP_S, 1:2], gates[0:CAP_S, bass.ds(e + SAMPLE_ROW, 1)]).then_inc(g_cur, 1)

            def step(e, j):
                c = j - 3
                if 0 <= c < 2 * PAIRS:
                    (gate_sum, up_sum)[c % 2](e, c // 2)
                lo_chunk(e, j)
                if 0 <= c < 2 * PAIRS and c % 2 == 1:
                    hid_low(e, c // 2)

            def late(e, last):
                for j in range(TURN, EC):
                    step(e, j)
                    if j == 20 and not last:
                        gathered_low(e + 1)

            dve.sem_inc(o_add, 1)
            for j in range(SPLIT_SLOTS):
                step(0, j)
            gathered_low(0)
            for j in range(SPLIT_SLOTS, TURN):
                step(0, j)
            with dve.Fori(0, NE - 1) as e:
                late(e, False)
                gates_of(e)
                for j in range(TURN):
                    step(e + 1, j)
                    if j == 4:
                        out_add(e)
            late(NE - 1, True)
            gates_of(NE - 1)
            out_add(NE - 1)

        @block.tensor
        def _(pe):
            def product3(out, a_hi, a_lo, b_hi, b_lo, start, stop):
                pe.matmul(out, a_hi, b_hi, start=start, stop=False)
                pe.matmul(out, a_hi, b_lo, start=False, stop=False)
                return pe.matmul(out, a_lo, b_hi, start=False, stop=stop)

            pe.wait_ge(consts_in, 32)
            for g in range(2):
                t0, nt, T, base = GROUPS[g]
                for t in range(t0, t0 + nt):
                    pe.wait_ge(x_norm, t + 1)
                    if t:
                        pe.wait_ge(hT_l, t)
                    for k in range(KD):
                        last = pe.transpose(psum[:, k // 4, k % 4 * P:(k % 4 + 1) * P], xin[:, t % 2, k * P:(k + 1) * P],
                                            ident[:, :])
                    last.then_inc(xT, 1)
                pe.wait_ge(hT_l, t0 + nt)
                for c in range(NC_CONV):
                    ch = CHUNKS * g + c
                    ws = ch % 2
                    pe.wait_ge(wi_l, 2 * ch + 2)
                    for b in range(T // 512):
                        n = glu_no[g, c, b]
                        if n - glu_by[g] < 2 and g == 1:
                            pe.wait_ge(t_norm, tok_by[1])
                            pe.wait_ge(v_ok, GROUPS[0][1])
                        if n >= 2:
                            pe.wait_ge(glu_u, n - 1)
                        for half in range(2):
                            for k in range(KD):
                                ws_k = (wi_hi[:, ws, k, half * P:(half + 1) * P], wi_lo[:, ws, k, half * P:(half + 1) * P])
                                last = product3(psum[:, glu_bank(n) + half, :], *ws_k,
                                                hT_hi[:, k, b * 512:(b + 1) * 512], hT_lo[:, k, b * 512:(b + 1) * 512],
                                                k == 0, k == KD - 1)
                        last.then_inc(pr_glu, 1)
                for c in range(3):
                    ch = CHUNKS * g + NC_CONV + c
                    ws = ch % 2
                    pe.wait_ge(wi_l, 2 * ch + 2)
                    for t in range(t0, t0 + nt):
                        n, i = tok_no[g, c, t], t - t0
                        if n - tok_by[g] < 4:
                            pe.wait_ge(glu_u, glu_by[g + 1])
                        else:
                            pe.wait_ge(t_norm, n - 3)
                            if c == 2 and i >= 4:
                                pe.wait_ge(v_ok, t - 3)
                        for k in range(KD):
                            last = product3(psum[:, tok_bank(n), 0:CCOLS],
                                            hT_hi[:, k, i * P:(i + 1) * P], hT_lo[:, k, i * P:(i + 1) * P],
                                            wi_hi[:, ws, k, :], wi_lo[:, ws, k, :], k == 0, k == KD - 1)
                        last.then_inc(pr_tok, 1)

            for t in range(TILES):
                pe.wait_ge(qk_lo, 3 * t + 3)
                if t:
                    pe.wait_ge(q_st_ok, t)
                    pe.wait_ge(k_st_ok, t)
                for h in range(NH):
                    pe.transpose(psum[:, h // 4, h % 4 * P:(h % 4 + 1) * P], q_split[:, h, :], ident[:, :])
                for h in range(NKV):
                    for x in range(2):
                        last = pe.transpose(psum[:, 2, (2 * h + x) * P:(2 * h + x + 1) * P], k_split[:, h, x, :], ident[:, :])
                last.then_inc(qk_T, 1)
            pe.wait_ge(q_st_ok, TILES)
            pe.wait_ge(k_st_ok, TILES)
            pe.wait_ge(t_norm, len(TOK_STEPS))
            pe.wait_ge(v_ok, TILES)

            def scores(u):
                g, h, t = UNITS[u]
                key0 = GROUPS[g][0] * P
                if u >= 2:
                    pe.wait_ge(s_exp, u - 1)
                for hf in range(HALVES[u]):
                    for x in range(2):
                        last = pe.matmul(psum[:, 2 * (u % 2) + hf, :], q_st[:, h, t * P:(t + 1) * P],
                                         k_st[:, h // (NH // NKV), x, key0 + hf * 512:key0 + (hf + 1) * 512],
                                         start=(x == 0), stop=(x == 1))
                last.then_inc(scored, 1)

            def transposes(u):
                pe.wait_ge(s_exp, u + 1)
                for hf in range(HALVES[u]):
                    m = half_no[u] + hf
                    if m >= 3:
                        pe.wait_ge(pT_ok, m - 2)
                    for i in range(4):
                        last = pe.transpose(psum[:, 4 + m % 3, i * P:(i + 1) * P],
                                            probs[:, u % 2, (4 * hf + i) * P:(4 * hf + i + 1) * P], ident[:, :])
                    last.then_inc(pT, 1)

            def weighted(u):
                g, h, t = UNITS[u]
                pe.wait_ge(pT_ok, half_no[u + 1])
                if u:
                    pe.wait_ge(attn_ok, u)
                nk = 4 * HALVES[u]
                for i in range(nk):
                    last = pe.matmul(psum[:, 7, 0:NKV * HD], probs_T[:, u % 2, i * P:(i + 1) * P],
                                     val[:, GROUPS[g][0] + i, :], start=(i == 0), stop=(i == nk - 1))
                last.then_inc(pv, 1)

            scores(0)
            for u in range(NU):
                if u + 1 < NU:
                    scores(u + 1)
                transposes(u)
                if u:
                    weighted(u - 1)
            weighted(NU - 1)

            pe.wait_ge(s_exp, NU)
            pe.wait_ge(attn_ok, NU)
            pe.wait_ge(wo_l, KD)
            pe.wait_ge(rows_in, 32)
            for s in range(TILES + 4):
                if s < TILES:
                    g = 0 if s < ROT_TILES else 1
                    col = GROUPS[g][3] + PAD + (s - GROUPS[g][0]) * P
                    pe.wait_ge(conv_tap, TAPS * (g + 1))
                    if s:
                        pe.wait_ge(c_cen, s)
                    for c in range(NC_CONV):
                        last = pe.transpose(psum[:, 0, c * P:(c + 1) * P], conv[:, c, col:col + P], ident[:, :])
                    last.then_inc(cT, 1)
                if 0 <= s - 4 < TILES:
                    t = s - 4
                    pe.wait_ge(h2T_ok, t + 1)
                    if t:
                        pe.wait_ge(a_sel, t)
                    for k in range(KD):
                        last = pe.matmul(psum[:, 7, 0:NE], h2T[:, k * P:(k + 1) * P], wr_sb[:, k, :],
                                         start=(k == 0), stop=(k == KD - 1))
                    last.then_inc(logit, 1)
                if 0 <= s - 1 < TILES:
                    t = s - 1
                    pe.wait_ge(m_ok, 2 * t + 2)
                    if t:
                        pe.wait_ge(mT_l, t)
                    for k in range(KD):
                        last = pe.transpose(psum[:, 1 + k // 4, k % 4 * P:(k % 4 + 1) * P], mix[:, k * P:(k + 1) * P], ident[:, :])
                    last.then_inc(mT, 1)
                if 0 <= s - 2 < TILES:
                    t = s - 2
                    pe.wait_ge(mT_l, t + 1)
                    if t:
                        pe.wait_ge(x1_ok, t)
                    for half in range(2):
                        for k in range(KD):
                            last = product3(psum[:, 3 + half, :],
                                            mT_hi[:, t % 2, k * P:(k + 1) * P], mT_lo[:, t % 2, k * P:(k + 1) * P],
                                            wo_hi[:, k, half * 512:(half + 1) * 512], wo_lo[:, k, half * 512:(half + 1) * 512],
                                            k == 0, k == KD - 1)
                    last.then_inc(proj, 1)
                if 0 <= s - 4 < TILES:
                    t = s - 4
                    pe.wait_ge(a_ok, t + 1)
                    if t < ROT_TILES:
                        pe.transpose(psum[0:NE, 7, P:2 * P], affp[:, 0, 0:NE], ident[:, :]).then_inc(a_T, 1)
                    else:
                        pe.transpose(psum[0:SEL_ROWS, 7, P:2 * P], affp[:, 1, :], ident[:, :]).then_inc(a_T, 1)
                if 0 <= s - 3 < TILES:
                    t = s - 3
                    pe.wait_ge(h2_ok, t + 1)
                    if t:
                        pe.wait_ge(h2T_ok, t)
                    for k in range(KD):
                        last = pe.transpose(psum[:, 5 + k // 4, k % 4 * P:(k % 4 + 1) * P], h2[:, t % 2, k * P:(k + 1) * P], ident[:, :])
                    last.then_inc(h2_T, 1)

            pe.wait_ge(picked, 1)
            pe.transpose(psum[:, 0, 0:SEL_ROWS], top[:, :], ident[0:SEL_ROWS, 0:SEL_ROWS])
            pe.transpose(psum[:, 0, 64:64 + SEL_ROWS], topf[:, :], ident[0:SEL_ROWS, 0:SEL_ROWS]).then_inc(selT, 1)

            def gathered_T(e):
                pe.wait_ge(gathered, 32 * e + 32)
                pe.wait_ge(g_sum, e * PAIRS)
                pe.wait_ge(u_sum, e * PAIRS)
                for k in range(KD):
                    c0 = k % 2 * CAP
                    pe.transpose(psum[:, k // 2, c0:c0 + CAP_P], xg_p[:, k * P:(k + 1) * P], ident[:, :])
                    last = pe.transpose(psum[:, k // 2, c0 + CAP_P:c0 + CAP], xg_s[:, k * P:(k + 1) * P],
                                        ident[0:CAP_S, 0:CAP_S])
                last.then_inc(xg_T, 1)

            def chunk(e, j):
                slot = j % SPLIT_SLOTS
                pe.wait_ge(e_lo, e * EC + (j + 1))
                if j < 2 * PAIRS:
                    m, up = j // 2, j % 2
                    if j == 0:
                        pe.wait_ge(xg_l, e + 1)
                    pe.wait_ge((g_sum, u_sum)[up], e * PAIRS + m)
                    for i in range(2):
                        for k in range(KD):
                            w0 = k * CCOLS + i * P
                            bank = psum[:, 2 * up + i, :]
                            pe.matmul(bank[:, 0:2 * CAP], w_hi[:, slot, w0:w0 + P], xgT[:, k, :],
                                      start=(k == 0), stop=False, skip_group_check=True)
                            last = pe.matmul(bank[:, 0:CAP], w_lo[:, slot, w0:w0 + P], xgT[:, k, 0:CAP],
                                             start=False, stop=(k == KD - 1), skip_group_check=True)
                else:
                    jj = j - 2 * PAIRS
                    if jj == 0:
                        pe.wait_ge(o_ok, 2 * e + 1)
                    pe.wait_ge(h_lo, 2 * (e * PAIRS + (jj + 1)))
                    for i in range(2):
                        st = hid_st[:, 2 * jj + i, :]
                        first, end = jj == 0 and i == 0, j == EC - 1 and i == 1
                        for half in range(2):
                            w0 = i * D + half * 512
                            hi, lo = w_hi[:, slot, w0:w0 + 512], w_lo[:, slot, w0:w0 + 512]
                            product3(psum[:, 4 + half, :], st[:, 0:CAP_P], st[:, CAP + CAP_S:2 * CAP], hi, lo, first, end)
                            both = st[:, CAP_P:CAP + CAP_S]
                            pe.matmul(psum[:, 6 + half, :], both, hi, start=first, stop=False)
                            last = pe.matmul(psum[:, 6 + half, :], both, lo, start=False, stop=end)
                last.then_inc(e_used, 1)

            def late(e, last):
                for j in range(TURN, EC):
                    chunk(e, j)
                    if j == 17 and not last:
                        gathered_T(e + 1)

            gathered_T(0)
            for j in range(TURN):
                chunk(0, j)
            with pe.Fori(0, NE - 1) as e:
                late(e, False)
                for j in range(TURN):
                    chunk(e + 1, j)
            late(NE - 1, True)


def rotary_tables():
    grid_w, axis = 64, HD // 2
    pos = np.arange(N_PROMPT)
    inv_freq = 10000.0 ** (-np.arange(0, axis, 2, dtype=np.float32) / np.float32(axis))
    ang = np.concatenate([(pos // grid_w).astype(np.float32)[:, None] * inv_freq.astype(np.float32),
                          (pos % grid_w).astype(np.float32)[:, None] * inv_freq.astype(np.float32)], axis=-1)
    cos = np.repeat(np.cos(ang), 2, axis=-1)
    sin = np.stack([-np.sin(ang), np.sin(ang)], axis=-1).reshape(N_PROMPT, HD)
    both = np.stack([cos, sin]).reshape(2, ROT_TILES, P, HD).transpose(2, 0, 1, 3)
    return np.ascontiguousarray(both.astype(np.float32))


def kernel(**inputs):
    import concourse.bacc as _bacc
    from concourse.bass_utils import run_bass_kernel_spmd as _run

    a = {k: np.asarray(v) for k, v in inputs.items()}

    def other_of_pair(g):
        return g.reshape(HD // 2, 2)[:, ::-1].reshape(HD)

    cols = np.concatenate([
        a["attn_norm_g"].reshape(KD, P).T,
        a["conv_dw_w"].reshape(CONV_K, NC_CONV, P).transpose(2, 1, 0).reshape(P, NC_CONV * CONV_K),
        a["conv_dw_b"].reshape(NC_CONV, P).T,
    ], axis=1)
    q_g, k_g = a["q_norm_g"][0], a["k_norm_g"][0]
    rows = np.concatenate([q_g, other_of_pair(q_g), k_g, other_of_pair(k_g), a["conv_ln_g"][0], a["conv_ln_b"][0],
                           a["attn_out_g"][0], a["conv_out_g"][0], a["ffn_norm_g"][0]])[None]
    ins = {
        "x_prompt": a["x_prompt"], "x_sample": a["x_sample"], "w_in": a["w_in"], "w_out": a["w_out"],
        "w_router": a["w_router"], "w_gate": a["w_gate"], "w_up": a["w_up"], "w_down": a["w_down"],
        "cols": cols, "rows": rows, "rotary": rotary_tables(), "ident": np.eye(P, dtype=np.float32),
    }
    nc = _bacc.Bacc("TRN2", target_bir_lowering=False, num_devices=1)
    arrays, args = {}, []
    for name, v in ins.items():
        v = np.ascontiguousarray(v)
        arrays[f"in_{name}_dram"] = v
        args.append(nc.dram_tensor(f"in_{name}_dram", v.shape, mybir.dt.from_np(v.dtype), kind="ExternalInput").ap())
    outs = [(1, N_PROMPT, D), (1, N_SAMPLE, D)]
    for i, shape in enumerate(outs):
        args.append(nc.dram_tensor(f"out_{i}_dram", shape, F32, kind="ExternalOutput").ap())
    encoder_layer_kernel(nc, *args)
    r = _run(nc, [arrays], core_ids=[0])
    return tuple(r.results[0][f"out_{i}_dram"] for i in range(len(outs)))
```

```python
from contextlib import ExitStack

import concourse.bass as bass
from concourse import mybir
import numpy as np

F32 = mybir.dt.float32
F32R = mybir.dt.float32r
U32 = mybir.dt.uint32
ALU = mybir.AluOpType
ACT = mybir.ActivationFunctionType
AX_X = mybir.AxisListType.X

P = 128
D = 1024
KD = D // P
N_PROMPT, N_SAMPLE = 1024, 512
TILES = (N_PROMPT + N_SAMPLE) // P
HD = 64
NH, NKV = 8, 2
AW = NH * HD
CW = D - AW
NC_CONV = CW // P
CONV_K = 31
PAD = CONV_K // 2
ROT_TILES = N_PROMPT // P
EPS = 1e-6
NE = 16
CAP_P, CAP_S = 2 * N_PROMPT // NE, 2 * N_SAMPLE // NE
CAP = CAP_P + CAP_S

GROUPS = [(0, N_PROMPT // P, N_PROMPT, 0), (N_PROMPT // P, N_SAMPLE // P, N_SAMPLE, N_PROMPT + 2 * PAD)]
SLOT = N_PROMPT + N_SAMPLE + 4 * PAD
CHUNKS = 7
CCOLS = 256
HALF = N_PROMPT // 2
SEL_ROWS = 3 * NE
SAMPLE_ROW = 2 * NE

COL_NORM, COL_TAP, COL_BIAS = 0, KD, KD + NC_CONV * CONV_K
COLS = COL_BIAS + NC_CONV
ROW_Q, ROW_K, ROW_LNG, ROW_LNB, ROW_MIX, ROW_FFN = 0, 2 * HD, 4 * HD, 4 * HD + CW, 4 * HD + 2 * CW, 4 * HD + 2 * CW + D
ROWS = ROW_FFN + D

EC = 24
CH = 2048
RAW_SLOTS, SPLIT_SLOTS = 4, 3
PAIRS = 8
UNDER_CONV_TOK = (NC_CONV + 1) * SLOT + 2 * TILES * NKV * HD
WO_SLOTS = 7
EARLY = 2
CV, C_STD, C_RSTD, M_SSQ, M_MS, M_STD, M_RSTD = 0, 1, 2, 3, 5, 7, 9
TURN = 8


def encoder_layer_kernel(nc, x_prompt, x_sample, w_in, w_out, w_router, w_gate, w_up, w_down,
                         cols, rows, rotary, ident_in, y_prompt, y_sample):
    h_rows = nc.dram_tensor("h_rows", [N_PROMPT + N_SAMPLE, D], F32).ap()
    wi = w_in.rearrange("l (k p) n -> p (l k) n", p=P)
    wo = w_out.rearrange("l (k p) n -> p (l k) n", p=P)
    wr = w_router.rearrange("l (k p) n -> p (l k) n", p=P)
    gate_cols = w_gate.rearrange("l e (k p) f -> (l e) p k f", p=P)
    up_cols = w_up.rearrange("l e (k p) f -> (l e) p k f", p=P)
    down_rows = w_down.rearrange("l e (j k p) d -> (l e) j p k d", p=P, k=2)

    def x_rows(t):
        src, i = (x_prompt, t) if t < ROT_TILES else (x_sample, t - ROT_TILES)
        return src[0, i * P:(i + 1) * P, :]

    def y_rows(t):
        dst, i = (y_prompt, t) if t < ROT_TILES else (y_sample, t - ROT_TILES)
        return dst[0, i * P:(i + 1) * P, :]

    with ExitStack() as ctx:
        def sem(name):
            return ctx.enter_context(nc.semaphore(name))

        def in_region(stack, name, shape, dt):
            return stack.enter_context(nc.sbuf_tensor(name, shape, dt))

        psum = ctx.enter_context(nc.psum_tensor("psum", [P, 8, 512], F32))

        ident2 = in_region(ctx, "ident2", [P, 2 * P], F32)
        ident, reversal = ident2[:, 0:P], ident2[:, P:2 * P]
        colp = in_region(ctx, "colp", [P, COLS], F32)
        tok = in_region(ctx, "tok", [P, TILES, AW], F32)
        stat = in_region(ctx, "stat", [P, TILES, 16], F32)
        aff = in_region(ctx, "aff", [SEL_ROWS, HALF], F32)
        top = in_region(ctx, "top", [SEL_ROWS, CAP_P], F32)
        topi = in_region(ctx, "topi", [SEL_ROWS, CAP_P], U32)
        topf = in_region(ctx, "topf", [SEL_ROWS, CAP_P], F32)
        gates = in_region(ctx, "gates", [P, SEL_ROWS], F32)
        sel = in_region(ctx, "sel", [P, 2, SEL_ROWS], F32)
        second = in_region(ctx, "second", [P, NE], F32)
        from_first = in_region(ctx, "from_first", [P, NE], F32)
        row_f = in_region(ctx, "row_f", [P, NE], F32)
        rows_p = in_region(ctx, "rows_p", [P, NE], U32)
        rows_s = in_region(ctx, "rows_s", [CAP_S, NE], U32)
        rows_sg = in_region(ctx, "rows_sg", [CAP_S, NE], U32)
        lngb = in_region(ctx, "lngb", [P, 2, CW], F32)
        bst = in_region(ctx, "bst", [P, TILES, 8], F32)
        cst = in_region(ctx, "cst", [P, 11, TILES], F32)

        with ExitStack() as region:
            conv = in_region(region, "conv", [P, NC_CONV + 1, SLOT], F32)
            k_tok = in_region(region, "k_tok", [P, TILES, NKV * HD], F32)
            val = in_region(region, "val", [P, TILES, NKV * HD], F32)
            with ExitStack() as ra:
                rot_c = in_region(ra, "rot_c", [P, 2, ROT_TILES, HD], F32)
                rot_s = in_region(ra, "rot_s", [P, 2, ROT_TILES, HD], F32)
                qn = in_region(ra, "qn", [P, 2, CCOLS], F32)
                q_turn = in_region(ra, "q_turn", [P, CCOLS], F32)
                sq = in_region(ra, "sq", [P, CCOLS], F32)
                tapped = in_region(ra, "tapped", [P, N_SAMPLE], F32)
                hstat = in_region(ra, "hstat", [P, 2, 3, 4], F32)
                hT_hi = in_region(ra, "hT_hi", [P, KD, N_PROMPT], F32R)
                hT_lo = in_region(ra, "hT_lo", [P, KD, N_PROMPT], F32R)
                wi_raw = in_region(ra, "wi_raw", [P, 2, KD // 2, CCOLS], F32)
                wi_hi = in_region(ra, "wi_hi", [P, 2, KD, CCOLS], F32R)
                wi_lo = in_region(ra, "wi_lo", [P, 2, KD, CCOLS], F32R)
                xin = in_region(ra, "xin", [P, 2, D], F32)
                sig_a = in_region(ra, "sig_a", [P, 512], F32)
            rot_src = tok[:, 0:2, :].rearrange("p a b -> p (a b)").rearrange("p (x t d) -> p x t d", x=2, d=HD)
            rope_gain = tok[:, 2, 0:4 * HD]
            with ExitStack() as rb:
                conv_tok = in_region(rb, "conv_tok", [P, TILES, CW], F32)
                q_st = in_region(rb, "q_st", [P, NH, TILES * P], F32R)
                k_st = in_region(rb, "k_st", [P, NKV, 2, TILES * P], F32R)
                probs = in_region(rb, "probs", [P, 2, N_PROMPT], F32)
                probs_T = in_region(rb, "probs_T", [P, 2, N_PROMPT], F32)
                q_split = in_region(rb, "q_split", [P, 2, NH, 2 * HD], F32)
                k_split = in_region(rb, "k_split", [P, 2, NKV, 2, 2 * HD], F32)
                smx = in_region(rb, "smx", [P, 3, TILES * NH], F32)
                junk = in_region(rb, "junk", [P, AW], F32)
        with ExitStack() as rc:
            with ExitStack() as rw:
                wo_raw = in_region(rw, "wo_raw", [P, WO_SLOTS, D], F32)
            x1 = in_region(rc, "x1", [P, 2, D], F32)
            h2 = in_region(rc, "h2", [P, 2, D], F32)
            h2T = in_region(rc, "h2T", [P, D], F32)
            xres = in_region(rc, "xres", [P, 2, D], F32)
            rowp = in_region(rc, "rowp", [P, ROWS - ROW_MIX], F32)
            in_region(rc, "under_conv_tok_c", [P, UNDER_CONV_TOK - 9 * D], F32)
            in_region(rc, "conv_tok_place", [P, TILES, CW], F32)
            wo_hi = in_region(rc, "wo_hi", [P, KD, D], F32R)
            wo_lo = in_region(rc, "wo_lo", [P, KD, D], F32R)
            wr_sb = in_region(rc, "wr_sb", [P, KD, NE], F32)
            mix = in_region(rc, "mix", [P, D], F32)
            mT_hi = in_region(rc, "mT_hi", [P, 2, D], F32R)
            mT_lo = in_region(rc, "mT_lo", [P, 2, D], F32R)
            csq = in_region(rc, "csq", [P, CW], F32)
            logit_T = in_region(rc, "logit_T", [NE, TILES * P], F32)
            e16 = in_region(rc, "e16", [P, TILES, NE], F32)
            aff_tok = in_region(rc, "aff_tok", [P, HALF // P, SEL_ROWS], F32)
            lst = in_region(rc, "lst", [P, 3, TILES], F32)
        with ExitStack() as re_:
            xg_p = in_region(re_, "xg_p", [P, D], F32)
            xg_s = in_region(re_, "xg_s", [CAP_S, D], F32)
            hid_st = in_region(re_, "hid_st", [P, 2 * PAIRS, 2 * CAP], F32R)
            o_p = in_region(re_, "o_p", [P, D], F32)
            o_s = in_region(re_, "o_s", [CAP_S, D], F32)
            in_region(re_, "under_conv_tok_e", [P, UNDER_CONV_TOK - 10 * D], F32)
            raw = in_region(re_, "raw", [P, RAW_SLOTS, CH], F32)
            w_hi = in_region(re_, "w_hi", [P, SPLIT_SLOTS, CH], F32R)
            w_lo = in_region(re_, "w_lo", [P, SPLIT_SLOTS, CH], F32R)
            xgT = in_region(re_, "xgT", [P, KD, 2 * CAP], F32R)
            low_g = in_region(re_, "low_g", [P, 2, CAP], F32)
            low_u = in_region(re_, "low_u", [P, 2, CAP], F32)
            gsum = in_region(re_, "gsum", [P, 2, CAP], F32)
            usum = in_region(re_, "usum", [P, 2, CAP], F32)
            hid = in_region(re_, "hid", [P, 2, CAP], F32)
            out_lo = in_region(re_, "out_lo", [CAP_S, D], F32)
            cur_p = in_region(re_, "cur_p", [P, 1], U32)
            cur_sg = in_region(re_, "cur_sg", [CAP_S, 1], U32)
            put_p = in_region(re_, "put_p", [P, 1], U32)
            put_s = in_region(re_, "put_s", [CAP_S, 1], U32)
            cur_g = in_region(re_, "cur_g", [P, 2], F32)

        consts_in = sem("consts_in"); tables_in = sem("tables_in")
        pads_zero = sem("pads_zero"); rot_ready = sem("rot_ready")
        x_in = [sem(f"x_in{i}") for i in range(2)]
        x_sq = sem("x_sq"); x_var = sem("x_var"); x_std = sem("x_std"); x_rstd = sem("x_rstd"); x_norm = sem("x_norm")
        xT = sem("xT"); hT_h = sem("hT_h"); hT_l = sem("hT_l")
        wi_in = [sem(f"wi_in{i}") for i in range(2)]
        wi_h = sem("wi_h"); wi_l = sem("wi_l")
        pr_glu = sem("pr_glu"); glu_sig = sem("glu_sig"); glu_u = sem("glu_u")
        pr_tok = sem("pr_tok"); t_sq = sem("t_sq"); t_ssq = sem("t_ssq"); t_var = sem("t_var"); t_std = sem("t_std")
        t_rstd = sem("t_rstd"); t_norm = sem("t_norm"); rope_a = sem("rope_a"); rope_b = sem("rope_b"); rope_c = sem("rope_c")
        v_ok = sem("v_ok"); conv_tap = sem("conv_tap"); pool_tap = sem("pool_tap"); pool_mul = sem("pool_mul")
        qk_hi = sem("qk_hi"); qk_lo = sem("qk_lo"); qk_T = sem("qk_T"); q_st_ok = sem("q_st_ok"); k_st_ok = sem("k_st_ok")
        scored = sem("scored"); s_max = sem("s_max"); s_exp = sem("s_exp"); pT = sem("pT"); pT_ok = sem("pT_ok")
        pv = sem("pv"); o_rec = sem("o_rec"); attn_ok = sem("attn_ok")
        wo_in = [sem(f"wo_in{i}") for i in range(WO_SLOTS)]
        wo_h = sem("wo_h"); wo_l = sem("wo_l"); rows_in = sem("rows_in")
        lngb_in = sem("lngb_in"); cT = sem("cT"); c_bn = sem("c_bn"); c_var = sem("c_var"); c_cen = sem("c_cen"); a_sq = sem("a_sq")
        c_std = sem("c_std"); c_rstd = sem("c_rstd"); c_ln = sem("c_ln"); c_act = sem("c_act"); c_sq = sem("c_sq")
        m_var = sem("m_var"); m_std = sem("m_std")
        m_rstd = sem("m_rstd"); m_ok = sem("m_ok"); mT = sem("mT"); mT_h = sem("mT_h"); mT_l = sem("mT_l"); proj = sem("proj")
        xr_in = [sem(f"xr_in{i}") for i in range(2)]
        x1_ok = sem("x1_ok"); f_sq = sem("f_sq"); f_var = sem("f_var"); f_std = sem("f_std"); f_rstd = sem("f_rstd"); h2_ok = sem("h2_ok")
        y_out = [sem(f"y_out{i}") for i in range(2)]; h_out = [sem(f"h_out{i}") for i in range(2)]
        h2_T = sem("h2_T"); h2T_ok = sem("h2T_ok"); logit = sem("logit"); logit_ok = sem("logit_ok"); l_T = sem("l_T")
        l_max = sem("l_max"); l_sub = sem("l_sub"); l_exp = sem("l_exp"); l_sum = sem("l_sum"); l_rec = sem("l_rec")
        a_ok = sem("a_ok"); a_T = sem("a_T"); a_sel = sem("a_sel")
        merge = sem("merge"); reversed_b = sem("reversed_b"); pick = sem("pick"); picked = sem("picked"); selT = sem("selT"); sel_ok = sem("sel_ok")
        raw_in = [sem(f"raw_in{i}") for i in range(RAW_SLOTS)]
        e_hi = sem("e_hi"); e_lo = sem("e_lo"); e_used = sem("e_used")
        dma_turn = sem("dma_turn"); cur_ok = sem("cur_ok"); put_ok = sem("put_ok"); gathered = sem("gathered"); xg_T = sem("xg_T"); xg_h = sem("xg_h"); xg_l = sem("xg_l")
        g_low = sem("g_low"); g_sum = sem("g_sum"); g_act = sem("g_act"); u_low = sem("u_low"); u_sum = sem("u_sum")
        h_mul = sem("h_mul"); h_hi = sem("h_hi"); h_lo = sem("h_lo")
        g_cur = sem("g_cur"); o_low = sem("o_low"); o_add = sem("o_add"); o_ok = sem("o_ok"); added = sem("added"); put_free = sem("put_free")

        GLU_BLOCKS = [(g, c, b) for g in range(2) for c in range(NC_CONV) for b in range(GROUPS[g][2] // 512)]
        glu_no = {key: n for n, key in enumerate(GLU_BLOCKS)}
        glu_by = [sum(k[0] < g for k in GLU_BLOCKS) for g in range(3)]
        TOK_STEPS = [(g, c, t) for g in range(2) for c in range(3) for t in range(GROUPS[g][0], GROUPS[g][0] + GROUPS[g][1])]
        tok_no = {key: n for n, key in enumerate(TOK_STEPS)}
        tok_by = [sum(k[0] < g for k in TOK_STEPS) for g in range(3)]
        UNITS = [(g, h, t) for g in range(2) for h in range(NH) for t in range(GROUPS[g][0], GROUPS[g][0] + GROUPS[g][1])]
        HALVES = [GROUPS[g][2] // 512 for g, _, _ in UNITS]
        half_no = [sum(HALVES[:n]) for n in range(len(UNITS) + 1)]
        TAPS = [(0, c, k) for c in range(NC_CONV) for k in range(CONV_K)] + [(1, c, k) for c in (1, 2, 3) for k in range(CONV_K)]
        POOL_TAPS = [(1, 0, k) for k in range(CONV_K)]

        def conv_operands(g, c, k):
            T, base = GROUPS[g][2], GROUPS[g][3]
            return (conv[:, c, base + PAD:base + PAD + T], conv[:, c + 1, base + k:base + k + T],
                    colp[:, COL_TAP + c * CONV_K + k:COL_TAP + c * CONV_K + k + 1])

        NU = len(UNITS)
        PROMPT_UNITS = NH * GROUPS[0][1]
        NORM_UNIT = NU - 6

        def conv_tile_at(u):
            i = u - PROMPT_UNITS
            return i // 2 if i >= 0 and i % 2 == 0 and i // 2 < TILES else None

        def square_tile_at(u):
            i = u - PROMPT_UNITS - 4
            return i if 0 <= i < ROT_TILES else None

        def glu_bank(n):
            return 4 + 2 * (n % 2)

        def tok_bank(n):
            return 4 + n % 4

        def sample_tiles_at(g, c, t):
            ahead = ROT_TILES + t - 2 if (g, c) == (0, 2) and 2 <= t < 2 + TILES - ROT_TILES else None
            now = ROT_TILES + t - 3 if (g, c) == (0, 2) and 3 <= t < 3 + TILES - ROT_TILES else None
            return ahead, now

        def x_transposed(t):
            return psum[:, 2 * (t % 2):2 * (t % 2) + 2, :].rearrange("p a (k b) -> p (a k) b", k=4)

        def flat(banks):
            return banks.rearrange("p a b -> p (a b)")

        def wi_multiplied(eng, n):
            g, c = n // CHUNKS, n % CHUNKS
            if c < NC_CONV:
                eng.wait_ge(pr_glu, glu_no[g, c, GROUPS[g][2] // 512 - 1] + 1)
            else:
                eng.wait_ge(pr_tok, tok_no[g, c - NC_CONV, GROUPS[g][0] + GROUPS[g][1] - 1] + 1)

        def y_stored(eng):
            for i in range(2):
                eng.wait_ge(y_out[i], 16 * TILES // 2)
                eng.wait_ge(h_out[i], 16 * TILES // 2)

        def k_twice(t):
            return k_tok[:, t, :].rearrange("p (h d) -> p h d", h=NKV).unsqueeze(2).broadcast_to([P, NKV, 2, HD])

        block = ctx.enter_context(nc.Block())

        @block.sync
        def _(sp):
            def load_x(t):
                if t >= 2:
                    sp.wait_ge(xT, t - 1)
                sp.dma_start(xin[:, t % 2, :], x_rows(t)).then_inc(x_in[t % 2], 16)

            def load_wi(g, c):
                n = CHUNKS * g + c
                for hf in range(2):
                    ks = slice(hf * KD // 2, (hf + 1) * KD // 2)
                    if n >= 1:
                        sp.wait_ge(wi_l, 2 * (n - 1) + hf + 1)
                    if c < NC_CONV:
                        c0, c1 = AW + 2 * NKV * HD + c * P, AW + 2 * NKV * HD + CW + c * P
                    else:
                        c0 = (c - NC_CONV) * CCOLS
                        c1 = c0 + P
                    sp.dma_start(wi_raw[:, hf, :, 0:P], wi[:, ks, c0:c0 + P]).then_inc(wi_in[hf], 16)
                    sp.dma_start(wi_raw[:, hf, :, P:CCOLS], wi[:, ks, c1:c1 + P]).then_inc(wi_in[hf], 16)

            load_x(0)
            sp.dma_start(ident2[:, :], ident_in).then_inc(consts_in, 16)
            load_x(1)
            sp.dma_start(colp[:, :], cols).then_inc(consts_in, 16)
            load_wi(0, 0)
            load_x(2)
            load_x(3)
            sp.dma_start(rot_src, rotary).then_inc(tables_in, 16)
            sp.dma_start(rope_gain, rows[0, 0:4 * HD].partition_broadcast(P)).then_inc(tables_in, 16)
            for i, r0 in enumerate((ROW_LNG, ROW_LNB)):
                sp.dma_start(lngb[:, i, :], rows[0, r0:r0 + CW].partition_broadcast(P)).then_inc(lngb_in, 16)
            for t in range(4, ROT_TILES):
                load_x(t)
            for c in range(1, CHUNKS):
                load_wi(0, c)
            load_x(ROT_TILES)
            load_x(ROT_TILES + 1)
            load_wi(1, 0)
            for t in range(ROT_TILES + 2, TILES):
                load_x(t)
            for c in range(1, CHUNKS):
                load_wi(1, c)

            sp.wait_ge(cT, TILES)
            for k in range(WO_SLOTS):
                sp.dma_start(wo_raw[:, k, :], wo[:, k, :]).then_inc(wo_in[k], 16)
            sp.wait_ge(attn_ok, NU)
            sp.dma_start(rowp[:, :], rows[0, ROW_MIX:ROWS].partition_broadcast(P)).then_inc(rows_in, 16)
            sp.dma_start(wr_sb[:, :, :], wr).then_inc(rows_in, 16)
            for k in range(WO_SLOTS, KD):
                sp.wait_ge(wo_l, k - WO_SLOTS + 1)
                sp.dma_start(wo_raw[:, k - WO_SLOTS, :], wo[:, k, :]).then_inc(wo_in[k - WO_SLOTS], 16)
            sp.wait_ge(wo_l, KD)
            for t in range(TILES + 1):
                if t < TILES:
                    if t >= 2:
                        sp.wait_ge(x1_ok, t - 1)
                    sp.dma_start(xres[:, t % 2, :], x_rows(t)).then_inc(xr_in[t % 2], 16)
                if t >= 1:
                    s = t - 1
                    sp.wait_ge(x1_ok, s + 1)
                    sp.dma_start(y_rows(s), x1[:, s % 2, :]).then_inc(y_out[s % 2], 16)
                    sp.wait_ge(h2_ok, s + 1)
                    sp.dma_start(h_rows[s * P:(s + 1) * P, :], h2[:, s % 2, :]).then_inc(h_out[s % 2], 16)

            sp.wait_ge(proj, TILES)

            def load_chunk(e, j):
                if j < 2 * PAIRS:
                    src = (gate_cols, up_cols)[j % 2][e, :, :, (j // 2) * CCOLS:(j // 2 + 1) * CCOLS]
                    dst = raw[:, j % RAW_SLOTS, :].rearrange("p (k f) -> p k f", k=KD)
                else:
                    src = down_rows[e, j - 2 * PAIRS]
                    dst = raw[:, j % RAW_SLOTS, :].rearrange("p (k d) -> p k d", k=2)
                sp.dma_start(dst, src).then_inc(raw_in[j % RAW_SLOTS], 16)

            for j in range(EC):
                if j >= RAW_SLOTS:
                    sp.wait_ge(e_lo, j - RAW_SLOTS + 1)
                load_chunk(0, j)
            with sp.Fori(1, NE) as e:
                for j in range(EC):
                    sp.wait_ge(proj, TILES)
                    sp.wait_ge(e_lo, e * EC + (j - RAW_SLOTS + 1))
                    load_chunk(e, j)
            y_stored(sp)
            sp.wait_ge(added, 32 * NE)

        @block.gpsimd
        def _(pool):
            pool.memset(conv[:, :, :], 0.0).then_inc(pads_zero, 1)

            pool.wait_ge(tables_in, 32)
            for x in range(2):
                for which, dst in ((0, rot_c), (1, rot_s)):
                    gain = rope_gain[:, (2 * x + which) * HD:(2 * x + which + 1) * HD]
                    pool.tensor_tensor(dst[:, x, :, :], rot_src[:, which, :, :],
                                       gain.unsqueeze(1).broadcast_to([P, ROT_TILES, HD]), ALU.mult).then_inc(rot_ready, 1)
            pool.wait_ge(rot_ready, 4)
            for tab in (rot_c, rot_s):
                pool.tensor_scalar(tab[:, 0, :, :], tab[:, 0, :, :], float(HD) ** -0.5, None, ALU.mult).then_inc(rot_ready, 1)
            pool.wait_ge(rot_ready, 6)

            for n, (g, c, t) in enumerate(TOK_STEPS):
                heads = 4 if c < 2 else NKV
                w, r, x = heads * HD, t - GROUPS[g][0], (0 if c < 2 else 1)

                def by_head(table):
                    return table[:, x, r, :].unsqueeze(1).broadcast_to([P, heads, HD])

                s_pairs = by_head(rot_s).rearrange("p h (d two) -> p h d two", two=2)
                src = qn[:, n % 2, 0:w].rearrange("p (h d) -> p h d", h=heads)
                pair = qn[:, n % 2, 0:w].rearrange("p (h d two) -> p h d two", h=heads, two=2)
                turn = q_turn[:, 0:w].rearrange("p (h d two) -> p h d two", h=heads, two=2)
                dst = tok[:, t, c * CCOLS:(c + 1) * CCOLS] if c < 2 else k_tok[:, t, :]
                pool.wait_ge(t_norm, n + 1)
                if n >= 1:
                    pool.wait_ge(rope_c, n)
                pool.tensor_tensor(turn[:, :, :, 0], pair[:, :, :, 1], s_pairs[:, :, :, 0], ALU.mult)
                pool.tensor_tensor(turn[:, :, :, 1], pair[:, :, :, 0], s_pairs[:, :, :, 1], ALU.mult).then_inc(rope_a, 1)
                pool.wait_ge(rope_a, n + 1)
                pool.tensor_tensor(src, src, by_head(rot_c), ALU.mult).then_inc(rope_b, 1)
                pool.wait_ge(rope_b, n + 1)
                pool.tensor_tensor(dst, qn[:, n % 2, 0:w], q_turn[:, 0:w], ALU.add).then_inc(rope_c, 1)

            for w, (g, c, k) in enumerate(POOL_TAPS):
                out, u, tap = conv_operands(g, c, k)
                if w:
                    pool.wait_ge(pool_tap, w)
                if k == 0:
                    pool.wait_ge(glu_u, glu_no[g, c, 0] + 1)
                    pool.tensor_scalar(out, u, tap, colp[:, COL_BIAS + c:COL_BIAS + c + 1], ALU.mult, ALU.add
                                       ).then_inc(pool_tap, 1)
                else:
                    pool.tensor_scalar(tapped[:, :], u, tap, None, ALU.mult).then_inc(pool_mul, 1)
                    pool.wait_ge(pool_mul, w)
                    pool.tensor_tensor(out, out, tapped[:, :], ALU.add).then_inc(pool_tap, 1)

            pool.wait_ge(sel_ok, 5)
            y_stored(pool)

            def gather(e):
                pool.tensor_copy(cur_p[:, :], rows_p[:, bass.ds(e, 1)]).then_inc(cur_ok, 1)
                pool.tensor_copy(cur_sg[:, :], rows_sg[:, bass.ds(e, 1)]).then_inc(cur_ok, 1)
                pool.wait_ge(cur_ok, 2 * e + 2)
                pool.sem_inc(dma_turn, 1)
                pool.indirect_dma_start(xg_p[:, :], None, h_rows, bass.IndirectOffsetOnAxis(ap=cur_p[:, :], axis=0)
                                        ).then_inc(gathered, 16)
                pool.indirect_dma_start(xg_s[:, :], None, h_rows, bass.IndirectOffsetOnAxis(ap=cur_sg[:, :], axis=0)
                                        ).then_inc(gathered, 16)

            def scatter(e):
                pool.tensor_copy(put_p[:, :], rows_p[:, bass.ds(e, 1)]).then_inc(put_ok, 1)
                pool.tensor_copy(put_s[:, :], rows_s[:, bass.ds(e, 1)]).then_inc(put_ok, 1)
                pool.wait_ge(put_ok, 2 * e + 2)
                pool.wait_ge(o_ok, 2 * e + 3)
                pool.sem_inc(dma_turn, 1)
                pool.indirect_dma_start(y_prompt[0], bass.IndirectOffsetOnAxis(ap=put_p[:, :], axis=0), o_p[:, :], None,
                                        compute_op=ALU.add).then_inc(added, 16)
                pool.indirect_dma_start(y_sample[0], bass.IndirectOffsetOnAxis(ap=put_s[:, :], axis=0), o_s[:, :], None,
                                        compute_op=ALU.add).then_inc(added, 16)
                pool.wait_ge(added, 32 * e + 32)
                pool.sem_inc(put_free, 1)

            pool.sem_inc(put_free, 1)
            gather(0)
            with pool.Fori(0, NE - 1) as e:
                pool.wait_ge(xg_T, e + 1)
                gather(e + 1)
                scatter(e)
            scatter(NE - 1)

        @block.scalar
        def _(act):
            def square_x(t):
                act.wait_ge(x_in[t % 2], 16 * (t // 2 + 1))
                i = t if t < ROT_TILES else t - ROT_TILES
                act.activation(hT_lo[:, :, i * P:(i + 1) * P], xin[:, t % 2, :].rearrange("p (k b) -> p k b", k=KD),
                               ACT.Square, accum_out=stat[:, t, 0:1]).then_inc(x_sq, 1)
                act.wait_ge(x_var, t + 1)
                act.activation(stat[:, t, 2:3], stat[:, t, 1:2], ACT.Sqrt).then_inc(x_std, 1)

            def split_x(g, t):
                i = t - GROUPS[g][0]
                act.wait_ge(xT, t + 1)
                act.copy(hT_hi[:, :, i * P:(i + 1) * P], x_transposed(t)).then_inc(hT_h, 1)

            def split_wi(g, c):
                n = CHUNKS * g + c
                if n == 0:
                    act.wait_ge(consts_in, 32)
                if n >= 2:
                    wi_multiplied(act, n - 2)
                for hf in range(2):
                    act.wait_ge(wi_in[hf], 32 * (n + 1))
                    for k in range(KD // 2):
                        kk = hf * KD // 2 + k
                        last = act.activation(wi_hi[:, n % 2, kk, :], wi_raw[:, hf, k, :], ACT.Copy,
                                              scale=colp[:, COL_NORM + kk:COL_NORM + kk + 1])
                    last.then_inc(wi_h, 1)

            for g in range(2):
                t0, nt = GROUPS[g][0], GROUPS[g][1]
                if g == 0:
                    square_x(0)
                    for t in range(nt):
                        if t + 1 < nt:
                            square_x(t + 1)
                        split_x(0, t)
                        if t == 2:
                            split_wi(0, 0)
                for c in range(NC_CONV):
                    split_wi(g, c + 1)
                    for b in range(GROUPS[g][2] // 512):
                        n = glu_no[g, c, b]
                        act.wait_ge(pr_glu, n + 1)
                        if n >= 1:
                            act.wait_ge(glu_u, n)
                        act.activation(sig_a[:, :], psum[:, glu_bank(n) + 1, :], ACT.Sigmoid).then_inc(glu_sig, 1)
                for c in range(3):
                    if c + 1 < 3:
                        split_wi(g, NC_CONV + c + 1)
                    for t in range(t0, t0 + nt):
                        if (g, c) == (0, 2) and t == nt - 1:
                            split_wi(1, 0)
                        n = tok_no[g, c, t]
                        bank = tok_bank(n)
                        w = CCOLS if c < 2 else NKV * HD
                        act.wait_ge(pr_tok, n + 1)
                        if n >= 1:
                            act.wait_ge(t_ssq, n)
                        act.activation(sq[:, 0:w], psum[:, bank, 0:w], ACT.Square).then_inc(t_sq, 1)
                        if c == 2:
                            act.copy(val[:, t, :], psum[:, bank, w:CCOLS]).then_inc(v_ok, 1)
                        act.wait_ge(t_var, n + 1)
                        act.activation(hstat[:, n % 2, 1, 0:w // HD], hstat[:, n % 2, 0, 0:w // HD], ACT.Sqrt).then_inc(t_std, 1)
                        ahead, now = sample_tiles_at(g, c, t)
                        if ahead is not None:
                            square_x(ahead)
                        if now is not None:
                            split_x(1, now)

            wi_multiplied(act, 2 * CHUNKS - 1)
            def split_high(t):
                act.wait_ge(rope_c, tok_by[1] if t < ROT_TILES else tok_no[1, 2, t] + 1)
                if t >= 2:
                    act.wait_ge(qk_T, t - 1)
                act.copy(q_split[:, t % 2, :, 0:HD].bitcast(F32R), tok[:, t, :].rearrange("p (h d) -> p h d", h=NH)).then_inc(qk_hi, 1)
                act.copy(k_split[:, t % 2, :, 0, :].rearrange("p h (x d) -> p h x d", x=2).bitcast(F32R), k_twice(t)).then_inc(qk_hi, 1)

            split_high(0)
            for t in range(TILES):
                if t + 1 < TILES:
                    split_high(t + 1)
                act.wait_ge(qk_T, t + 1)
                act.copy(q_st[:, :, t * P:(t + 1) * P],
                         psum[:, 4 * (t % 2):4 * (t % 2) + 2, :].rearrange("p a (h b) -> p (a h) b", h=4)).then_inc(q_st_ok, 1)

            def exp_unit(u):
                n = GROUPS[UNITS[u][0]][2]
                act.wait_ge(s_max, u + 1)
                if u >= 2:
                    act.wait_ge(pT, half_no[u - 1])
                act.activation(probs[:, u % 2, 0:n], flat(psum[:, 2 * (u % 2):2 * (u % 2) + 2, :])[:, 0:n], ACT.Exp,
                               bias=smx[:, 0, u:u + 1], accum_out=smx[:, 1, u:u + 1]).then_inc(s_exp, 1)

            def square_rows(t):
                act.wait_ge(attn_ok, PROMPT_UNITS if t < ROT_TILES else NU)
                if t:
                    act.wait_ge(a_sq, t)
                if t == ROT_TILES:
                    act.wait_ge(c_sq, TILES)
                act.activation((junk if t < ROT_TILES else csq)[:, :], tok[:, t, :], ACT.Square, accum_out=cst[:, M_SSQ, t:t + 1]).then_inc(a_sq, 1)

            exp_unit(0)
            for u in range(NU):
                if u >= 2:
                    act.wait_ge(pv, u - 1)
                for hf in range(HALVES[u]):
                    m = half_no[u] + hf
                    act.wait_ge(pT, m + 1)
                    act.copy(probs_T[:, u % 2, hf * 512:(hf + 1) * 512], psum[:, 4 + m % 3, :]).then_inc(pT_ok, 1)
                if u + 1 < NU:
                    exp_unit(u + 1)
                if square_tile_at(u) is not None:
                    square_rows(square_tile_at(u))
                if u == NORM_UNIT:
                    act.wait_ge(c_var, TILES)
                    act.activation(cst[:, C_STD, :], cst[:, CV, :], ACT.Sqrt).then_inc(c_std, 1)

            act.wait_ge(pv, NU)
            act.wait_ge(attn_ok, NU)

            def high_wo(k):
                act.wait_ge(wo_in[k % WO_SLOTS], 16 * (k // WO_SLOTS + 1))
                act.copy(wo_hi[:, k, :], wo_raw[:, k % WO_SLOTS, :]).then_inc(wo_h, 1)

            def conv_silu(t):
                act.wait_ge(c_ln, t + 1)
                act.activation(conv_tok[:, t, :], conv_tok[:, t, :], ACT.Silu).then_inc(c_act, 1)
                act.wait_ge(c_act, t + 1)
                if t:
                    act.wait_ge(c_sq, t)
                act.activation(csq[:, :], conv_tok[:, t, :], ACT.Square, accum_out=cst[:, M_SSQ + 1, t:t + 1]).then_inc(c_sq, 1)

            def out_roots(n, t0, t1):
                act.wait_ge(m_var, n + 1)
                act.activation(cst[:, M_STD:M_STD + 2, t0:t1], cst[:, M_MS:M_MS + 2, t0:t1], ACT.Sqrt).then_inc(m_std, 1)

            for t in range(EARLY):
                conv_silu(t)
            out_roots(0, 0, EARLY)
            high_wo(0)
            for s in range(TILES + 3):
                if s < TILES:
                    act.wait_ge(mT, s + 1)
                    if s >= 2:
                        act.wait_ge(proj, s - 1)
                    act.copy(mT_hi[:, s % 2, :], flat(psum[:, 1:3, :])).then_inc(mT_h, 1)
                if s == 0:
                    for k in range(1, KD):
                        high_wo(k)
                if s == EARLY - 1:
                    for t in range(EARLY, TILES):
                        conv_silu(t)
                    for t in range(ROT_TILES, TILES):
                        square_rows(t)
                    out_roots(1, EARLY, TILES)
                if 0 <= s - 2 < TILES:
                    t = s - 2
                    act.wait_ge(h2_T, t + 1)
                    if t >= 1:
                        act.wait_ge(logit, t)
                    act.copy(h2T[:, :], flat(psum[:, 5:7, :])).then_inc(h2T_ok, 1)
                if 0 <= s - 1 < TILES:
                    t = s - 1
                    act.wait_ge(x1_ok, t + 1)
                    if t >= 2:
                        act.wait_ge(h_out[t % 2], 16 * (t // 2))
                        act.wait_ge(h2_T, t - 1)
                        act.wait_ge(h2_ok, t - 1)
                    act.activation(h2[:, t % 2, :], x1[:, t % 2, :], ACT.Square, accum_out=stat[:, t, 0:1]).then_inc(f_sq, 1)
                    act.wait_ge(f_var, t + 1)
                    act.activation(stat[:, t, 2:3], stat[:, t, 1:2], ACT.Sqrt).then_inc(f_std, 1)
            act.wait_ge(l_sub, 1)
            act.activation(e16[:, :, :], e16[:, :, :], ACT.Exp).then_inc(l_exp, 1)

            def hi_chunk(e, j, first=False):
                act.wait_ge(raw_in[j % RAW_SLOTS], e * (EC // RAW_SLOTS * 16) + (j // RAW_SLOTS + 1) * 16)
                if not first:
                    act.wait_ge(e_used, e * EC + (j - SPLIT_SLOTS + 1))
                act.copy(w_hi[:, j % SPLIT_SLOTS, :], raw[:, j % RAW_SLOTS, :]).then_inc(e_hi, 1)

            def low_columns(e, c):
                m = c // 2
                act.wait_ge(e_used, e * EC + (c + 1))
                if c % 2 == 0:
                    act.wait_ge(g_sum, e * PAIRS + m)
                    act.copy(low_g[:, :, :], psum[:, 0:2, CAP:2 * CAP]).then_inc(g_low, 1)
                else:
                    act.wait_ge(u_sum, e * PAIRS + m)
                    act.copy(low_u[:, :, :], psum[:, 2:4, CAP:2 * CAP]).then_inc(u_low, 1)

            def gate_act(e, m):
                act.wait_ge(g_sum, e * PAIRS + (m + 1))
                act.activation(gsum[:, :, :], gsum[:, :, :], ACT.Silu).then_inc(g_act, 1)

            def hid_high(e, m):
                act.wait_ge(h_mul, e * PAIRS + (m + 1))
                act.copy(hid_st[:, 2 * m:2 * m + 2, 0:CAP], hid[:, :, :]).then_inc(h_hi, 1)

            def gathered_high(e):
                act.wait_ge(xg_T, e + 1)
                act.copy(xgT[:, :, 0:CAP].rearrange("p (a b) c -> p a b c", a=4),
                         psum[:, 0:4, 0:2 * CAP].rearrange("p a (b c) -> p a b c", b=2)).then_inc(xg_h, 1)

            def out_low(e):
                act.wait_ge(e_used, e * EC + EC)
                act.wait_ge(o_add, e + 1)
                act.copy(out_lo[:, :], flat(psum[CAP_S:2 * CAP_S, 6:8, :])).then_inc(o_low, 1)

            def out_rows(e):
                act.wait_ge(g_cur, 2 * e + 2)
                act.wait_ge(put_free, e + 1)
                act.activation(o_p[:, :], flat(psum[:, 4:6, :]), ACT.Copy, scale=cur_g[:, 0:1]).then_inc(o_ok, 1)
                act.wait_ge(o_add, e + 2)
                act.activation(o_s[:, :], o_s[:, :], ACT.Copy, scale=cur_g[0:CAP_S, 1:2]).then_inc(o_ok, 1)

            def step(e, j, first=False):
                c = j - 3
                if 0 <= c < 2 * PAIRS:
                    low_columns(e, c)
                hi_chunk(e, j, first)
                if 0 <= c < 2 * PAIRS and c % 2 == 0:
                    gate_act(e, c // 2)
                if 0 <= c < 2 * PAIRS and c % 2 == 1:
                    hid_high(e, c // 2)

            def late(e, last):
                for j in range(TURN, EC):
                    step(e, j)
                    if j == 20 and not last:
                        gathered_high(e + 1)

            act.sem_inc(o_ok, 1)
            act.wait_ge(proj, TILES)
            for j in range(SPLIT_SLOTS):
                step(0, j, first=True)
            gathered_high(0)
            for j in range(SPLIT_SLOTS, TURN):
                step(0, j)
            with act.Fori(0, NE - 1) as e:
                late(e, False)
                for j in range(TURN):
                    step(e + 1, j)
                    if j == 3:
                        out_low(e)
                out_rows(e)
            late(NE - 1, True)
            out_low(NE - 1)
            out_rows(NE - 1)

        @block.vector
        def _(dve):
            conv_done = [0]

            def conv_run(n):
                for w in range(conv_done[0], min(conv_done[0] + n, len(TAPS))):
                    g, c, k = TAPS[w]
                    out, u, tap = conv_operands(g, c, k)
                    if w:
                        dve.wait_ge(conv_tap, w)
                    if k == 0:
                        dve.wait_ge(glu_u, glu_no[g, c, GROUPS[g][2] // 512 - 1] + 1)
                        if g == 1:
                            dve.wait_ge(pool_tap, len(POOL_TAPS))
                        dve.tensor_scalar(out, u, tap, colp[:, COL_BIAS + c:COL_BIAS + c + 1], ALU.mult, ALU.add
                                          ).then_inc(conv_tap, 1)
                    else:
                        dve.scalar_tensor_tensor(out=out, in0=u, scalar=tap, in1=out, op0=ALU.mult, op1=ALU.add
                                                 ).then_inc(conv_tap, 1)
                    conv_done[0] = w + 1


            def norm_x(t):
                dve.wait_ge(x_sq, t + 1)
                dve.tensor_scalar(stat[:, t, 1:2], stat[:, t, 0:1], 1.0 / D, EPS, ALU.mult, ALU.add).then_inc(x_var, 1)
                dve.wait_ge(x_std, t + 1)
                dve.reciprocal(stat[:, t, 3:4], stat[:, t, 2:3]).then_inc(x_rstd, 1)
                dve.wait_ge(x_rstd, t + 1)
                dve.tensor_scalar(xin[:, t % 2, :], xin[:, t % 2, :], stat[:, t, 3:4], None, ALU.mult).then_inc(x_norm, 1)

            def split_x(g, t):
                i = t - GROUPS[g][0]
                dve.wait_ge(hT_h, t + 1)
                dve.tensor_tensor(hT_lo[:, :, i * P:(i + 1) * P], x_transposed(t),
                                  hT_hi[:, :, i * P:(i + 1) * P].bitcast(F32), ALU.subtract).then_inc(hT_l, 1)

            def split_wi(g, c):
                n = CHUNKS * g + c
                if n == 0:
                    dve.wait_ge(consts_in, 32)
                for hf in range(2):
                    dve.wait_ge(wi_h, 2 * n + hf + 1)
                    for k in range(KD // 2):
                        kk = hf * KD // 2 + k
                        last = dve.scalar_tensor_tensor(
                            out=wi_lo[:, n % 2, kk, :], in0=wi_raw[:, hf, k, :],
                            scalar=colp[:, COL_NORM + kk:COL_NORM + kk + 1],
                            in1=wi_hi[:, n % 2, kk, :].bitcast(F32), op0=ALU.mult, op1=ALU.subtract)
                    last.then_inc(wi_l, 1)

            for g in range(2):
                t0, nt, T, base = GROUPS[g]
                if g == 0:
                    norm_x(0)
                    for t in range(nt):
                        if t + 1 < nt:
                            norm_x(t + 1)
                        split_x(0, t)
                        if t == 2:
                            split_wi(0, 0)
                for c in range(NC_CONV):
                    split_wi(g, c + 1)
                    for b in range(T // 512):
                        n = glu_no[g, c, b]
                        dve.wait_ge(glu_sig, n + 1)
                        if n == 0:
                            dve.wait_ge(pads_zero, 1)
                        dve.tensor_tensor(conv[:, c + 1, base + PAD + b * 512:base + PAD + (b + 1) * 512],
                                          psum[:, glu_bank(n), :], sig_a[:, :], ALU.mult).then_inc(glu_u, 1)
                        if c >= 1 or g == 1:
                            conv_run(6 if g == 0 else 4)
                for c in range(3):
                    if c + 1 < 3:
                        split_wi(g, NC_CONV + c + 1)
                    for t in range(t0, t0 + nt):
                        if (g, c) == (0, 2) and t == nt - 1:
                            split_wi(1, 0)
                        n = tok_no[g, c, t]
                        heads = 4 if c < 2 else NKV
                        w = heads * HD
                        hs = hstat[:, n % 2, :, 0:heads]
                        dve.wait_ge(t_sq, n + 1)
                        dve.tensor_reduce(hs[:, 2, :], sq[:, 0:w].rearrange("p (h d) -> p h d", h=heads), AX_X, ALU.add
                                          ).then_inc(t_ssq, 1)
                        dve.wait_ge(t_ssq, n + 1)
                        dve.tensor_scalar(hs[:, 0, :], hs[:, 2, :], 1.0 / HD, EPS, ALU.mult, ALU.add).then_inc(t_var, 1)
                        if (g, c) != (0, 2):
                            conv_run(1)
                        dve.wait_ge(t_std, n + 1)
                        dve.reciprocal(hs[:, 2, :], hs[:, 1, :]).then_inc(t_rstd, 1)
                        dve.wait_ge(t_rstd, n + 1)
                        if n >= 2:
                            dve.wait_ge(rope_c, n - 1)
                        dve.tensor_tensor(qn[:, n % 2, 0:w].rearrange("p (h d) -> p h d", h=heads),
                                          psum[:, tok_bank(n), 0:w].rearrange("p (h d) -> p h d", h=heads),
                                          hs[:, 2, :].unsqueeze(2).broadcast_to([P, heads, HD]), ALU.mult).then_inc(t_norm, 1)
                        ahead, now = sample_tiles_at(g, c, t)
                        if ahead is not None:
                            norm_x(ahead)
                        if now is not None:
                            split_x(1, now)

            def split_low(t):
                dve.wait_ge(qk_hi, 2 * t + 2)
                qs, ks = q_split[:, t % 2, :, :], k_split[:, t % 2, :, :, :]
                dve.tensor_tensor(qs[:, :, HD:2 * HD].bitcast(F32R), tok[:, t, :].rearrange("p (h d) -> p h d", h=NH),
                                  qs[:, :, 0:HD], ALU.subtract).then_inc(qk_lo, 1)
                dve.tensor_tensor(ks[:, :, 1, :].rearrange("p h (x d) -> p h x d", x=2).bitcast(F32R), k_twice(t),
                                  ks[:, :, 0, :].rearrange("p h (x d) -> p h x d", x=2), ALU.subtract).then_inc(qk_lo, 1)

            split_low(0)
            for t in range(TILES):
                if t + 1 < TILES:
                    split_low(t + 1)
                dve.wait_ge(qk_T, t + 1)
                dve.tensor_copy(k_st[:, :, :, t * P:(t + 1) * P],
                                psum[:, 2 + 4 * (t % 2), :].rearrange("p (h x b) -> p h x b", h=NKV, x=2)).then_inc(k_st_ok, 1)

            def max_unit(u):
                n = GROUPS[UNITS[u][0]][2]
                dve.wait_ge(scored, u + 1)
                dve.tensor_reduce(smx[:, 0, u:u + 1], flat(psum[:, 2 * (u % 2):2 * (u % 2) + 2, :])[:, 0:n],
                                  AX_X, ALU.max, negate=True).then_inc(s_max, 1)

            def rows_unit(u):
                g, h, t = UNITS[u]
                kv = h // (NH // NKV)
                dve.wait_ge(s_exp, u + 1)
                dve.reciprocal(smx[:, 2, u:u + 1], smx[:, 1, u:u + 1]).then_inc(o_rec, 1)
                dve.wait_ge(o_rec, u + 1)
                dve.wait_ge(pv, u + 1)
                dve.tensor_scalar(tok[:, t, h * HD:(h + 1) * HD], psum[:, 7, kv * HD:(kv + 1) * HD],
                                  smx[:, 2, u:u + 1], None, ALU.mult).then_inc(attn_ok, 1)

            def conv_rows(t):
                rows_ps = psum[:, 1 + 2 * (t % 2), :]
                dve.wait_ge(cT, t + 1)
                if t == 0:
                    dve.wait_ge(lngb_in, 32)
                dve.bn_stats(bst[:, t, 0:6], rows_ps).then_inc(c_bn, 1)
                dve.wait_ge(c_bn, 2 * t + 1)
                dve.bn_aggr(bst[:, t, 6:8], bst[:, t, 0:6]).then_inc(c_bn, 1)
                dve.wait_ge(c_bn, 2 * t + 2)
                dve.tensor_scalar(cst[:, CV, t:t + 1], bst[:, t, 7:8], EPS, None, ALU.add).then_inc(c_var, 1)
                dve.scalar_tensor_tensor(out=conv_tok[:, t, :], in0=rows_ps, scalar=bst[:, t, 6:7], in1=lngb[:, 0, :],
                                         op0=ALU.subtract, op1=ALU.mult).then_inc(c_cen, 1)

            def conv_norm(t):
                dve.scalar_tensor_tensor(out=conv_tok[:, t, :], in0=conv_tok[:, t, :], scalar=cst[:, C_RSTD, t:t + 1],
                                         in1=lngb[:, 1, :], op0=ALU.mult, op1=ALU.add).then_inc(c_ln, 1)

            max_unit(0)
            for u in range(NU):
                if u >= 2:
                    rows_unit(u - 2)
                if u + 1 < NU:
                    max_unit(u + 1)
                sample_next = TAPS[min(conv_done[0], len(TAPS) - 1)][0] == 1
                if u < PROMPT_UNITS:
                    conv_run(3 - (u % 4 == 0) if sample_next else 2 - u % 2)
                else:
                    conv_run(len(TAPS))
                if conv_tile_at(u) is not None:
                    conv_rows(conv_tile_at(u))
                if u == NORM_UNIT + 1:
                    dve.wait_ge(c_std, 1)
                    dve.reciprocal(cst[:, C_RSTD, :], cst[:, C_STD, :]).then_inc(c_rstd, 1)
                    dve.wait_ge(c_rstd, 1)
                    dve.wait_ge(c_cen, TILES)
                if u > NORM_UNIT:
                    conv_norm(u - NORM_UNIT - 1)
            rows_unit(NU - 2)
            rows_unit(NU - 1)

            dve.wait_ge(attn_ok, NU)

            def low_wo(k):
                dve.wait_ge(wo_h, k + 1)
                dve.tensor_tensor(wo_lo[:, k, :], wo_raw[:, k % WO_SLOTS, :], wo_hi[:, k, :].bitcast(F32), ALU.subtract
                                  ).then_inc(wo_l, 1)

            def out_norms(n, t0, t1):
                dve.wait_ge(c_sq, t1)
                dve.wait_ge(a_sq, ROT_TILES if n == 0 else TILES)
                dve.tensor_scalar(cst[:, M_MS:M_MS + 2, t0:t1], cst[:, M_SSQ:M_SSQ + 2, t0:t1], 1.0 / AW, EPS,
                                  ALU.mult, ALU.add).then_inc(m_var, 1)
                dve.wait_ge(m_std, n + 1)
                dve.reciprocal(cst[:, M_RSTD:M_RSTD + 2, t0:t1], cst[:, M_STD:M_STD + 2, t0:t1]).then_inc(m_rstd, 1)
                dve.wait_ge(m_rstd, n + 1)

            out_norms(0, 0, EARLY)
            dve.wait_ge(rows_in, 32)
            mix_gain, ffn_gain = rowp[:, 0:D], rowp[:, D:2 * D]

            def mix_rows(t):
                if t:
                    dve.wait_ge(mT, t)
                for i, (src, c0) in enumerate(((tok, 0), (conv_tok, AW))):
                    dve.scalar_tensor_tensor(out=mix[:, c0:c0 + AW], in0=src[:, t, :], scalar=cst[:, M_RSTD + i, t:t + 1],
                                             in1=mix_gain[:, c0:c0 + AW], op0=ALU.mult, op1=ALU.mult).then_inc(m_ok, 1)

            mix_rows(0)
            low_wo(0)
            for s in range(TILES + 3):
                if s < TILES:
                    dve.wait_ge(mT_h, s + 1)
                    dve.tensor_tensor(mT_lo[:, s % 2, :], flat(psum[:, 1:3, :]), mT_hi[:, s % 2, :].bitcast(F32),
                                      ALU.subtract).then_inc(mT_l, 1)
                    if s == 0:
                        mix_rows(1)
                        for k in range(1, KD):
                            low_wo(k)
                        for t in range(NU - 1 - NORM_UNIT, TILES):
                            conv_norm(t)
                    elif s + 1 < TILES and s != EARLY - 1:
                        mix_rows(s + 1)
                if 0 <= s - 1 < TILES:
                    t = s - 1
                    dve.wait_ge(proj, t + 1)
                    dve.wait_ge(xr_in[t % 2], 16 * (t // 2 + 1))
                    if t >= 2:
                        dve.wait_ge(y_out[t % 2], 16 * (t // 2))
                        dve.wait_ge(f_sq, t - 1)
                    dve.tensor_tensor(x1[:, t % 2, :], flat(psum[:, 3:5, :]), xres[:, t % 2, :], ALU.add).then_inc(x1_ok, 1)
                    if s == EARLY - 1:
                        out_norms(1, EARLY, TILES)
                        mix_rows(EARLY)
                    dve.wait_ge(f_sq, t + 1)
                    dve.tensor_scalar(stat[:, t, 1:2], stat[:, t, 0:1], 1.0 / D, EPS, ALU.mult, ALU.add).then_inc(f_var, 1)
                    dve.wait_ge(f_std, t + 1)
                    dve.reciprocal(stat[:, t, 3:4], stat[:, t, 2:3]).then_inc(f_rstd, 1)
                    dve.wait_ge(f_rstd, t + 1)
                    dve.scalar_tensor_tensor(out=h2[:, t % 2, :], in0=x1[:, t % 2, :], scalar=stat[:, t, 3:4],
                                             in1=ffn_gain, op0=ALU.mult, op1=ALU.mult).then_inc(h2_ok, 1)
                if 0 <= s - 3 < TILES:
                    t = s - 3
                    dve.wait_ge(logit, t + 1)
                    dve.tensor_copy(logit_T[:, t * P:(t + 1) * P], psum[0:NE, 7, 0:P]).then_inc(logit_ok, 1)

            def by_tile(x):
                return lst[:, x, :].unsqueeze(2).broadcast_to([P, TILES, NE])

            logits = psum[:, 0, 0:TILES * NE].rearrange("p (t e) -> p t e", e=NE)
            dve.wait_ge(l_T, 1)
            dve.tensor_reduce(lst[:, 0, :], logits, AX_X, ALU.max, negate=True).then_inc(l_max, 1)
            dve.wait_ge(l_max, 1)
            dve.tensor_tensor(e16[:, :, :], logits, by_tile(0), ALU.add).then_inc(l_sub, 1)
            dve.wait_ge(l_exp, 1)
            dve.tensor_reduce(lst[:, 1, :], e16[:, :, :], AX_X, ALU.add).then_inc(l_sum, 1)
            dve.wait_ge(l_sum, 1)
            dve.reciprocal(lst[:, 2, :], lst[:, 1, :]).then_inc(l_rec, 1)
            dve.wait_ge(l_rec, 1)
            dve.tensor_tensor(aff_tok[:, :, :].rearrange("p i (g e) -> p g i e", g=3),
                              e16[:, :, :].rearrange("p (g i) e -> p g i e", g=3),
                              by_tile(2).rearrange("p (g i) e -> p g i e", g=3), ALU.mult).then_inc(a_ok, 1)
            dve.wait_ge(a_T, 1)
            dve.tensor_copy(aff[:, :], psum[0:SEL_ROWS, 1, :]).then_inc(a_sel, 1)

            dve.wait_ge(a_sel, 1)
            for r in range(CAP_P // 8):
                v, vi = top[:, 8 * r:8 * r + 8], topi[:, 8 * r:8 * r + 8]
                if r:
                    dve.wait_ge(pick, 3 * r)
                dve.max(v, aff[:, :]).then_inc(pick, 1)
                dve.wait_ge(pick, 3 * r + 1)
                dve.max_index(vi, v, aff[:, :]).then_inc(pick, 1)
                dve.match_replace(aff[:, :], v, aff[:, :], -2.0).then_inc(pick, 1)
            dve.wait_ge(pick, 3 * CAP_P // 8)
            dve.tensor_copy(topf[:, :], topi[:, :]).then_inc(picked, 1)
            dve.wait_ge(selT, 1)
            dve.tensor_copy(sel[:, :, :], psum[:, 0, 0:2 * SEL_ROWS].rearrange("p (x r) -> p x r", x=2)).then_inc(merge, 1)
            a, a_row = sel[:, 0, 0:NE], sel[:, 1, 0:NE]
            b, b_place = psum[:, 1, 0:NE], psum[:, 1, NE:2 * NE]
            dve.wait_ge(reversed_b, 1)
            dve.wait_ge(merge, 1)
            dve.tensor_tensor(gates[:, 0:NE], b, a, ALU.max).then_inc(sel_ok, 1)
            dve.tensor_tensor(from_first[:, :], b, a, ALU.is_le).then_inc(merge, 1)
            dve.tensor_scalar(second[:, :], b_place, float(HALF), None, ALU.add).then_inc(merge, 1)
            dve.tensor_copy(gates[:, SAMPLE_ROW:SEL_ROWS], sel[:, 0, SAMPLE_ROW:SEL_ROWS]).then_inc(sel_ok, 1)
            dve.tensor_copy(rows_s[:, :], sel[0:CAP_S, 1, SAMPLE_ROW:SEL_ROWS]).then_inc(sel_ok, 1)
            dve.tensor_scalar(rows_sg[:, :], sel[0:CAP_S, 1, SAMPLE_ROW:SEL_ROWS], float(N_PROMPT), None,
                              ALU.add).then_inc(sel_ok, 1)
            dve.wait_ge(merge, 3)
            dve.tensor_tensor(row_f[:, :], a_row, second[:, :], ALU.subtract).then_inc(merge, 1)
            dve.wait_ge(merge, 4)
            dve.tensor_tensor(row_f[:, :], row_f[:, :], from_first[:, :], ALU.mult).then_inc(merge, 1)
            dve.wait_ge(merge, 5)
            dve.tensor_tensor(rows_p[:, :], row_f[:, :], second[:, :], ALU.add).then_inc(sel_ok, 1)

            def lo_chunk(e, j):
                dve.wait_ge(e_hi, e * EC + (j + 1))
                dve.tensor_tensor(w_lo[:, j % SPLIT_SLOTS, :], raw[:, j % RAW_SLOTS, :],
                                  w_hi[:, j % SPLIT_SLOTS, :].bitcast(F32), ALU.subtract).then_inc(e_lo, 1)

            def gate_sum(e, m):
                dve.wait_ge(g_low, e * PAIRS + (m + 1))
                dve.wait_ge(h_mul, e * PAIRS + m)
                dve.tensor_tensor(gsum[:, :, :], psum[:, 0:2, 0:CAP], low_g[:, :, :], ALU.add).then_inc(g_sum, 1)

            def up_sum(e, m):
                dve.wait_ge(u_low, e * PAIRS + (m + 1))
                dve.wait_ge(h_mul, e * PAIRS + m)
                dve.tensor_tensor(usum[:, :, :], psum[:, 2:4, 0:CAP], low_u[:, :, :], ALU.add).then_inc(u_sum, 1)
                dve.wait_ge(g_act, e * PAIRS + (m + 1))
                dve.wait_ge(u_sum, e * PAIRS + (m + 1))
                dve.wait_ge(h_lo, 2 * (e * PAIRS + m))
                dve.tensor_tensor(hid[:, :, :], usum[:, :, :], gsum[:, :, :], ALU.mult).then_inc(h_mul, 1)

            def hid_low(e, m):
                dve.wait_ge(h_hi, e * PAIRS + (m + 1))
                st = hid_st[:, 2 * m:2 * m + 2, :]
                dve.tensor_tensor(st[:, :, CAP:CAP + CAP_S], hid[:, :, CAP_P:CAP], st[:, :, CAP_P:CAP].bitcast(F32),
                                  ALU.subtract).then_inc(h_lo, 1)
                dve.tensor_tensor(st[:, :, CAP + CAP_S:2 * CAP], hid[:, :, 0:CAP_P], st[:, :, 0:CAP_P].bitcast(F32),
                                  ALU.subtract).then_inc(h_lo, 1)

            def gathered_low(e):
                dve.wait_ge(xg_h, e + 1)
                halves = xgT[:, :, :].rearrange("p (a b) c -> p a b c", a=4)
                dve.tensor_tensor(halves[:, :, :, CAP:2 * CAP], psum[:, 0:4, 0:2 * CAP].rearrange("p a (b c) -> p a b c", b=2),
                                  halves[:, :, :, 0:CAP].bitcast(F32), ALU.subtract).then_inc(xg_l, 1)

            def out_add(e):
                dve.wait_ge(o_low, e + 1)
                dve.wait_ge(put_free, e + 1)
                dve.tensor_tensor(o_s[:, :], flat(psum[0:CAP_S, 6:8, :]), out_lo[:, :], ALU.add).then_inc(o_add, 1)

            def gates_of(e):
                dve.wait_ge(o_ok, 2 * e + 1)
                dve.tensor_copy(cur_g[:, 0:1], gates[:, bass.ds(e, 1)]).then_inc(g_cur, 1)
                dve.tensor_copy(cur_g[0:CAP_S, 1:2], gates[0:CAP_S, bass.ds(e + SAMPLE_ROW, 1)]).then_inc(g_cur, 1)

            def step(e, j):
                c = j - 3
                if 0 <= c < 2 * PAIRS:
                    (gate_sum, up_sum)[c % 2](e, c // 2)
                lo_chunk(e, j)
                if 0 <= c < 2 * PAIRS and c % 2 == 1:
                    hid_low(e, c // 2)

            def late(e, last):
                for j in range(TURN, EC):
                    step(e, j)
                    if j == 20 and not last:
                        gathered_low(e + 1)

            dve.sem_inc(o_add, 1)
            for j in range(SPLIT_SLOTS):
                step(0, j)
            gathered_low(0)
            for j in range(SPLIT_SLOTS, TURN):
                step(0, j)
            with dve.Fori(0, NE - 1) as e:
                late(e, False)
                gates_of(e)
                for j in range(TURN):
                    step(e + 1, j)
                    if j == 4:
                        out_add(e)
            late(NE - 1, True)
            gates_of(NE - 1)
            out_add(NE - 1)

        @block.tensor
        def _(pe):
            def product3(out, a_hi, a_lo, b_hi, b_lo, start, stop):
                pe.matmul(out, a_hi, b_hi, start=start, stop=False)
                pe.matmul(out, a_hi, b_lo, start=False, stop=False)
                return pe.matmul(out, a_lo, b_hi, start=False, stop=stop)

            pe.wait_ge(consts_in, 32)

            def x_transposes(t):
                pe.wait_ge(x_norm, t + 1)
                if t >= 2:
                    pe.wait_ge(hT_l, t - 1)
                for k in range(KD):
                    last = pe.transpose(x_transposed(t)[:, k, :], xin[:, t % 2, k * P:(k + 1) * P], ident[:, :])
                last.then_inc(xT, 1)

            for g in range(2):
                t0, nt, T, base = GROUPS[g]
                if g == 0:
                    for t in range(4):
                        x_transposes(t)
                for c in range(NC_CONV):
                    ch = CHUNKS * g + c
                    ws = ch % 2
                    pe.wait_ge(wi_l, 2 * ch + 2)
                    for b in range(T // 512):
                        n = glu_no[g, c, b]
                        if c == 0:
                            pe.wait_ge(hT_l, t0 + 4 * b + 4)
                        if n - glu_by[g] < 2 and g == 1:
                            pe.wait_ge(t_norm, tok_by[1])
                            pe.wait_ge(v_ok, GROUPS[0][1])
                        if n >= 2:
                            pe.wait_ge(glu_u, n - 1)
                        for half in range(2):
                            for k in range(KD):
                                ws_k = (wi_hi[:, ws, k, half * P:(half + 1) * P], wi_lo[:, ws, k, half * P:(half + 1) * P])
                                last = product3(psum[:, glu_bank(n) + half, :], *ws_k,
                                                hT_hi[:, k, b * 512:(b + 1) * 512], hT_lo[:, k, b * 512:(b + 1) * 512],
                                                k == 0, k == KD - 1)
                                if n == 0 and k % 4 == 3:
                                    x_transposes(4 + 2 * half + k // 4)
                        last.then_inc(pr_glu, 1)
                for c in range(3):
                    ch = CHUNKS * g + NC_CONV + c
                    ws = ch % 2
                    pe.wait_ge(wi_l, 2 * ch + 2)
                    for t in range(t0, t0 + nt):
                        n, i = tok_no[g, c, t], t - t0
                        if n - tok_by[g] < 4:
                            pe.wait_ge(glu_u, glu_by[g + 1])
                        else:
                            pe.wait_ge(t_norm, n - 3)
                            if c == 2 and i >= 4:
                                pe.wait_ge(v_ok, t - 3)
                        for k in range(KD):
                            last = product3(psum[:, tok_bank(n), 0:CCOLS],
                                            hT_hi[:, k, i * P:(i + 1) * P], hT_lo[:, k, i * P:(i + 1) * P],
                                            wi_hi[:, ws, k, :], wi_lo[:, ws, k, :], k == 0, k == KD - 1)
                        last.then_inc(pr_tok, 1)
                        now = sample_tiles_at(g, c, t)[1]
                        if now is not None:
                            x_transposes(now)

            for t in range(TILES):
                b0 = 4 * (t % 2)
                if t == 1:
                    pe.wait_ge(t_norm, len(TOK_STEPS))
                    pe.wait_ge(v_ok, TILES)
                pe.wait_ge(qk_lo, 2 * t + 2)
                if t >= 2:
                    pe.wait_ge(q_st_ok, t - 1)
                    pe.wait_ge(k_st_ok, t - 1)
                for h in range(NH):
                    pe.transpose(psum[:, b0 + h // 4, h % 4 * P:(h % 4 + 1) * P], q_split[:, t % 2, h, :], ident[:, :])
                for h in range(NKV):
                    for x in range(2):
                        last = pe.transpose(psum[:, b0 + 2, (2 * h + x) * P:(2 * h + x + 1) * P], k_split[:, t % 2, h, x, :],
                                            ident[:, :])
                last.then_inc(qk_T, 1)
            pe.wait_ge(q_st_ok, TILES)
            pe.wait_ge(k_st_ok, TILES)

            def scores(u):
                g, h, t = UNITS[u]
                key0 = GROUPS[g][0] * P
                if u >= 2:
                    pe.wait_ge(s_exp, u - 1)
                for hf in range(HALVES[u]):
                    for x in range(2):
                        last = pe.matmul(psum[:, 2 * (u % 2) + hf, :], q_st[:, h, t * P:(t + 1) * P],
                                         k_st[:, h // (NH // NKV), x, key0 + hf * 512:key0 + (hf + 1) * 512],
                                         start=(x == 0), stop=(x == 1))
                last.then_inc(scored, 1)

            def transposes(u):
                pe.wait_ge(s_exp, u + 1)
                for hf in range(HALVES[u]):
                    m = half_no[u] + hf
                    if m >= 3:
                        pe.wait_ge(pT_ok, m - 2)
                    for i in range(4):
                        last = pe.transpose(psum[:, 4 + m % 3, i * P:(i + 1) * P],
                                            probs[:, u % 2, (4 * hf + i) * P:(4 * hf + i + 1) * P], ident[:, :])
                    last.then_inc(pT, 1)

            def weighted(u):
                g, h, t = UNITS[u]
                pe.wait_ge(pT_ok, half_no[u + 1])
                if u:
                    pe.wait_ge(attn_ok, u)
                nk = 4 * HALVES[u]
                for i in range(nk):
                    last = pe.matmul(psum[:, 7, 0:NKV * HD], probs_T[:, u % 2, i * P:(i + 1) * P],
                                     val[:, GROUPS[g][0] + i, :], start=(i == 0), stop=(i == nk - 1))
                last.then_inc(pv, 1)

            def conv_transposes(t):
                g = 0 if t < ROT_TILES else 1
                col = GROUPS[g][3] + PAD + (t - GROUPS[g][0]) * P
                pe.wait_ge(conv_tap, len(TAPS))
                pe.wait_ge(pool_tap, len(POOL_TAPS))
                pe.wait_ge(s_exp, PROMPT_UNITS)
                if t >= 2:
                    pe.wait_ge(c_cen, t - 1)
                for c in range(NC_CONV):
                    last = pe.transpose(psum[:, 1 + 2 * (t % 2), c * P:(c + 1) * P], conv[:, c, col:col + P], ident[:, :])
                last.then_inc(cT, 1)

            scores(0)
            for u in range(NU):
                if u + 1 < NU:
                    scores(u + 1)
                if conv_tile_at(u) is not None:
                    conv_transposes(conv_tile_at(u))
                transposes(u)
                if u:
                    weighted(u - 1)
            weighted(NU - 1)

            pe.wait_ge(s_exp, NU)
            pe.wait_ge(attn_ok, NU)
            pe.wait_ge(c_cen, TILES)
            pe.wait_ge(rows_in, 32)
            def mixed_transposes(t):
                pe.wait_ge(m_ok, 2 * t + 2)
                if t:
                    pe.wait_ge(mT_l, t)
                for k in range(KD):
                    last = pe.transpose(psum[:, 1 + k // 4, k % 4 * P:(k % 4 + 1) * P], mix[:, k * P:(k + 1) * P], ident[:, :])
                last.then_inc(mT, 1)

            def out_product(t):
                pe.wait_ge(mT_l, t + 1)
                if t:
                    pe.wait_ge(x1_ok, t)
                for half in range(2):
                    for k in range(KD):
                        if t == 0 and half == 0:
                            pe.wait_ge(wo_l, k + 1)
                        last = product3(psum[:, 3 + half, :],
                                        mT_hi[:, t % 2, k * P:(k + 1) * P], mT_lo[:, t % 2, k * P:(k + 1) * P],
                                        wo_hi[:, k, half * 512:(half + 1) * 512], wo_lo[:, k, half * 512:(half + 1) * 512],
                                        k == 0, k == KD - 1)
                last.then_inc(proj, 1)

            for s in range(TILES + 3):
                if s == EARLY:
                    out_product(s - 1)
                if s < TILES:
                    mixed_transposes(s)
                if 0 <= s - 1 < TILES and s != EARLY:
                    out_product(s - 1)
                if 0 <= s - 2 < TILES:
                    t = s - 2
                    pe.wait_ge(h2_ok, t + 1)
                    if t:
                        pe.wait_ge(h2T_ok, t)
                    for k in range(KD):
                        last = pe.transpose(psum[:, 5 + k // 4, k % 4 * P:(k % 4 + 1) * P], h2[:, t % 2, k * P:(k + 1) * P], ident[:, :])
                    last.then_inc(h2_T, 1)
                if 0 <= s - 3 < TILES:
                    t = s - 3
                    pe.wait_ge(h2T_ok, t + 1)
                    if t:
                        pe.wait_ge(logit_ok, t)
                    for k in range(KD):
                        last = pe.matmul(psum[0:NE, 7, 0:P], wr_sb[:, k, :], h2T[:, k * P:(k + 1) * P],
                                         start=(k == 0), stop=(k == KD - 1))
                    last.then_inc(logit, 1)

            pe.wait_ge(logit_ok, TILES)
            for t in range(TILES):
                last = pe.transpose(psum[:, 0, t * NE:(t + 1) * NE], logit_T[:, t * P:(t + 1) * P], ident[0:NE, 0:NE])
            last.then_inc(l_T, 1)
            pe.wait_ge(a_ok, 1)
            for i in range(HALF // P):
                last = pe.transpose(psum[0:SEL_ROWS, 1, i * P:(i + 1) * P], aff_tok[:, i, :], ident[:, :])
            last.then_inc(a_T, 1)

            pe.wait_ge(picked, 1)
            pe.transpose(psum[:, 0, 0:SEL_ROWS], top[:, :], ident[0:SEL_ROWS, 0:SEL_ROWS])
            pe.transpose(psum[:, 0, SEL_ROWS:2 * SEL_ROWS], topf[:, :], ident[0:SEL_ROWS, 0:SEL_ROWS]).then_inc(selT, 1)
            pe.wait_ge(merge, 1)
            pe.matmul(psum[:, 1, 0:2 * NE], reversal, sel[:, :, NE:2 * NE], start=True, stop=True).then_inc(reversed_b, 1)

            def gathered_T(e):
                pe.wait_ge(gathered, 32 * e + 32)
                pe.wait_ge(g_sum, e * PAIRS)
                pe.wait_ge(u_sum, e * PAIRS)
                for k in range(KD):
                    c0 = k % 2 * CAP
                    pe.transpose(psum[:, k // 2, c0:c0 + CAP_P], xg_p[:, k * P:(k + 1) * P], ident[:, :])
                    last = pe.transpose(psum[:, k // 2, c0 + CAP_P:c0 + CAP], xg_s[:, k * P:(k + 1) * P],
                                        ident[0:CAP_S, 0:CAP_S])
                last.then_inc(xg_T, 1)

            def chunk(e, j):
                slot = j % SPLIT_SLOTS
                pe.wait_ge(e_lo, e * EC + (j + 1))
                if j < 2 * PAIRS:
                    m, up = j // 2, j % 2
                    if j == 0:
                        pe.wait_ge(xg_l, e + 1)
                    pe.wait_ge((g_sum, u_sum)[up], e * PAIRS + m)
                    for i in range(2):
                        for k in range(KD):
                            w0 = k * CCOLS + i * P
                            bank = psum[:, 2 * up + i, :]
                            pe.matmul(bank[:, 0:2 * CAP], w_hi[:, slot, w0:w0 + P], xgT[:, k, :],
                                      start=(k == 0), stop=False, skip_group_check=True)
                            last = pe.matmul(bank[:, 0:CAP], w_lo[:, slot, w0:w0 + P], xgT[:, k, 0:CAP],
                                             start=False, stop=(k == KD - 1), skip_group_check=True)
                else:
                    jj = j - 2 * PAIRS
                    if jj == 0:
                        pe.wait_ge(o_ok, 2 * e + 1)
                    pe.wait_ge(h_lo, 2 * (e * PAIRS + (jj + 1)))
                    for i in range(2):
                        st = hid_st[:, 2 * jj + i, :]
                        first, end = jj == 0 and i == 0, j == EC - 1 and i == 1
                        for half in range(2):
                            w0 = i * D + half * 512
                            hi, lo = w_hi[:, slot, w0:w0 + 512], w_lo[:, slot, w0:w0 + 512]
                            product3(psum[:, 4 + half, :], st[:, 0:CAP_P], st[:, CAP + CAP_S:2 * CAP], hi, lo, first, end)
                            both = st[:, CAP_P:CAP + CAP_S]
                            pe.matmul(psum[:, 6 + half, :], both, hi, start=first, stop=False)
                            last = pe.matmul(psum[:, 6 + half, :], both, lo, start=False, stop=end)
                last.then_inc(e_used, 1)

            def late(e, last):
                for j in range(TURN, EC):
                    chunk(e, j)
                    if j == 17 and not last:
                        gathered_T(e + 1)

            gathered_T(0)
            for j in range(TURN):
                chunk(0, j)
            with pe.Fori(0, NE - 1) as e:
                late(e, False)
                for j in range(TURN):
                    chunk(e + 1, j)
            late(NE - 1, True)


def rotary_tables():
    grid_w, axis = 64, HD // 2
    pos = np.arange(N_PROMPT)
    inv_freq = 10000.0 ** (-np.arange(0, axis, 2, dtype=np.float32) / np.float32(axis))
    ang = np.concatenate([(pos // grid_w).astype(np.float32)[:, None] * inv_freq.astype(np.float32),
                          (pos % grid_w).astype(np.float32)[:, None] * inv_freq.astype(np.float32)], axis=-1)
    cos = np.repeat(np.cos(ang), 2, axis=-1)
    sin = np.stack([-np.sin(ang), np.sin(ang)], axis=-1).reshape(N_PROMPT, HD)
    both = np.stack([cos, sin]).reshape(2, ROT_TILES, P, HD).transpose(2, 0, 1, 3)
    return np.ascontiguousarray(both.astype(np.float32))


def kernel(**inputs):
    import concourse.bacc as _bacc
    from concourse.bass_utils import run_bass_kernel_spmd as _run

    a = {k: np.asarray(v) for k, v in inputs.items()}

    def other_of_pair(g):
        return g.reshape(HD // 2, 2)[:, ::-1].reshape(HD)

    cols = np.concatenate([
        a["attn_norm_g"].reshape(KD, P).T,
        a["conv_dw_w"].reshape(CONV_K, NC_CONV, P).transpose(2, 1, 0).reshape(P, NC_CONV * CONV_K),
        a["conv_dw_b"].reshape(NC_CONV, P).T,
    ], axis=1)
    q_g, k_g = a["q_norm_g"][0], a["k_norm_g"][0]
    rows = np.concatenate([q_g, other_of_pair(q_g), k_g, other_of_pair(k_g), a["conv_ln_g"][0], a["conv_ln_b"][0],
                           a["attn_out_g"][0], a["conv_out_g"][0], a["ffn_norm_g"][0]])[None]
    ins = {
        "x_prompt": a["x_prompt"], "x_sample": a["x_sample"], "w_in": a["w_in"], "w_out": a["w_out"],
        "w_router": a["w_router"], "w_gate": a["w_gate"], "w_up": a["w_up"], "w_down": a["w_down"],
        "cols": cols, "rows": rows, "rotary": rotary_tables(), "ident": np.concatenate([np.eye(P, dtype=np.float32), np.eye(P, dtype=np.float32)[::-1]], axis=1),
    }
    nc = _bacc.Bacc("TRN2", target_bir_lowering=False, num_devices=1)
    arrays, args = {}, []
    for name, v in ins.items():
        v = np.ascontiguousarray(v)
        arrays[f"in_{name}_dram"] = v
        args.append(nc.dram_tensor(f"in_{name}_dram", v.shape, mybir.dt.from_np(v.dtype), kind="ExternalInput").ap())
    outs = [(1, N_PROMPT, D), (1, N_SAMPLE, D)]
    for i, shape in enumerate(outs):
        args.append(nc.dram_tensor(f"out_{i}_dram", shape, F32, kind="ExternalOutput").ap())
    encoder_layer_kernel(nc, *args)
    r = _run(nc, [arrays], core_ids=[0])
    return tuple(r.results[0][f"out_{i}_dram"] for i in range(len(outs)))
```
